# Optimizing a Trainium2 kernel written in Bass

```python
import math
import jax, jax.numpy as jnp
from jax import lax
import numpy as np

D_MODEL = 1024
BATCH = 1
SEQ = 2048
DEPTH = 1

N_HEADS = 8
N_KV_HEADS = 2
HEAD_DIM = 64
GROUP = N_HEADS // N_KV_HEADS
ATTN_WIDTH = N_HEADS * HEAD_DIM
KV_WIDTH = N_KV_HEADS * HEAD_DIM
WINDOW = 128
BLOCK = 128
SSM_WIDTH = D_MODEL // 2
SSM_CH = 16
SSM_GROUPS = SSM_WIDTH // SSM_CH
SSM_STATE = 64
DT_MIN = 1e-3
DT_MAX = 1e-1
D_FF = 2816
CONV_WIDTH = 3
N_BRANCH = 2
IN_WIDTH = ATTN_WIDTH + 2 * KV_WIDTH + SSM_WIDTH + N_BRANCH * D_MODEL
EPS = 1e-6
NEG_INF = -1e30

kernel_name = "hybrid_gqa_s5_convffn_encoder"

def rmsnorm(x, g):
    xf = x.astype(jnp.float32)
    xf = xf * lax.rsqrt(jnp.mean(xf * xf, axis=-1, keepdims=True) + EPS)
    return (xf * g.astype(jnp.float32)).astype(x.dtype)

def alibi_slopes():
    h = jnp.arange(N_HEADS, dtype=jnp.float32) + 1.0
    return 2.0 ** (-8.0 * h / N_HEADS)

def windowed_gqa_sink(q, k, v, sink):
    bsz, seq = q.shape[0], q.shape[1]
    nb = seq // BLOCK
    qb = q.reshape(bsz, nb, BLOCK, N_KV_HEADS, GROUP, HEAD_DIM)
    pad = ((0, 0), (BLOCK, BLOCK), (0, 0), (0, 0))
    kp = jnp.pad(k, pad).reshape(bsz, nb + 2, BLOCK, N_KV_HEADS, HEAD_DIM)
    vp = jnp.pad(v, pad).reshape(bsz, nb + 2, BLOCK, N_KV_HEADS, HEAD_DIM)
    kb = jnp.concatenate([kp[:, :-2], kp[:, 1:-1], kp[:, 2:]], axis=2)
    vb = jnp.concatenate([vp[:, :-2], vp[:, 1:-1], vp[:, 2:]], axis=2)
    scores = jnp.einsum('bnqkgd,bnskd->bnkgqs', qb, kb).astype(jnp.float32) * (HEAD_DIM ** -0.5)
    rel = jnp.arange(BLOCK)[:, None] - (jnp.arange(3 * BLOCK)[None, :] - BLOCK)
    dist = jnp.abs(rel).astype(jnp.float32)
    key_pos = (jnp.arange(nb)[:, None] - 1) * BLOCK + jnp.arange(3 * BLOCK)[None, :]
    valid = (jnp.abs(rel) <= WINDOW)[None] & ((key_pos >= 0) & (key_pos < seq))[:, None, :]
    slopes = alibi_slopes().reshape(N_KV_HEADS, GROUP)
    scores = scores - slopes[:, :, None, None] * dist
    scores = jnp.where(valid[None, :, None, None], scores, NEG_INF)
    sink_logit = jnp.broadcast_to(
        sink.astype(jnp.float32).reshape(N_KV_HEADS, GROUP)[None, None, :, :, None, None],
        scores.shape[:-1] + (1,))
    probs = jax.nn.softmax(jnp.concatenate([scores, sink_logit], axis=-1), axis=-1)[..., :-1]
    out = jnp.einsum('bnkgqs,bnskd->bnqkgd', probs.astype(v.dtype), vb)
    return out.reshape(bsz, seq, ATTN_WIDTH)

def _scan_op(e1, e2):
    a1, b1 = e1
    a2, b2 = e2
    return a1 * a2, a2 * b1 + b2

def s5_scan(u, lam_re, lam_im, log_dt, b_re, b_im, c_re, c_im):
    dt = jnp.exp(log_dt.astype(jnp.float32))[:, None]
    lam = lax.complex(lam_re.astype(jnp.float32), lam_im.astype(jnp.float32))
    lam_bar = jnp.exp(lam * dt)
    b = lax.complex(b_re.astype(jnp.float32), b_im.astype(jnp.float32))
    b_bar = ((lam_bar - 1.0) / lam)[..., None] * b
    bu = jnp.einsum('blgc,gnc->blgn', u.astype(jnp.complex64), b_bar)
    a = jnp.broadcast_to(lam_bar, bu.shape)
    _, xs = lax.associative_scan(_scan_op, (a, bu), axis=1)
    c = lax.complex(c_re.astype(jnp.float32), c_im.astype(jnp.float32))
    return jnp.einsum('blgn,gcn->blgc', xs, c).real

def s5_bidirectional(u, lam_re_f, lam_im_f, log_dt_f, b_re_f, b_im_f, c_re_f, c_im_f,
                     lam_re_b, lam_im_b, log_dt_b, b_re_b, b_im_b, c_re_b, c_im_b,
                     ssm_d, w_glu, b_glu):
    bsz, seq, _ = u.shape
    uf = u.astype(jnp.float32)
    ug = uf.reshape(bsz, seq, SSM_GROUPS, SSM_CH)
    y_f = s5_scan(ug, lam_re_f, lam_im_f, log_dt_f, b_re_f, b_im_f, c_re_f, c_im_f)
    y_b = s5_scan(ug[:, ::-1], lam_re_b, lam_im_b, log_dt_b, b_re_b, b_im_b, c_re_b, c_im_b)[:, ::-1]
    y = (y_f + y_b).reshape(bsz, seq, SSM_WIDTH) + ssm_d.astype(jnp.float32) * uf
    y = jax.nn.gelu(y).astype(u.dtype)
    return y * jax.nn.sigmoid(y @ w_glu + b_glu)

def hybrid_layer(x, norm_mix_pre, w_in, attn_sink,
                 lam_re_f, lam_im_f, log_dt_f, b_re_f, b_im_f, c_re_f, c_im_f,
                 lam_re_b, lam_im_b, log_dt_b, b_re_b, b_im_b, c_re_b, c_im_b,
                 ssm_d, w_glu, b_glu, w_branch_attn, w_branch_ssm, w_out, norm_mix_post,
                 norm_ffn_pre, w_ffn_gate, w_ffn_up, conv_w, conv_b, w_ffn_down, norm_ffn_post):
    bsz, seq, _ = x.shape
    h = rmsnorm(x, norm_mix_pre)
    z = h @ w_in
    splits = np.cumsum([ATTN_WIDTH, KV_WIDTH, KV_WIDTH, SSM_WIDTH]).tolist()
    q, k, v, u, gates = jnp.split(z, splits, axis=-1)
    k = k.reshape(bsz, seq, N_KV_HEADS, HEAD_DIM)
    v = v.reshape(bsz, seq, N_KV_HEADS, HEAD_DIM)
    y_attn = windowed_gqa_sink(q, k, v, attn_sink) @ w_branch_attn
    y_ssm = s5_bidirectional(u, lam_re_f, lam_im_f, log_dt_f, b_re_f, b_im_f, c_re_f, c_im_f,
                             lam_re_b, lam_im_b, log_dt_b, b_re_b, b_im_b, c_re_b, c_im_b,
                             ssm_d, w_glu, b_glu) @ w_branch_ssm
    g = jax.nn.sigmoid(gates.reshape(bsz, seq, N_BRANCH, D_MODEL))
    merged = g[:, :, 0] * y_attn + g[:, :, 1] * y_ssm
    x = x + rmsnorm(merged @ w_out, norm_mix_post)
    h2 = rmsnorm(x, norm_ffn_pre)
    gate = h2 @ w_ffn_gate
    up = h2 @ w_ffn_up
    gp = jnp.pad(gate, ((0, 0), (1, 1), (0, 0)))
    gate = gp[:, :-2] * conv_w[0] + gp[:, 1:-1] * conv_w[1] + gp[:, 2:] * conv_w[2] + conv_b
    f = jax.nn.gelu(gate) * up
    return x + rmsnorm(f @ w_ffn_down, norm_ffn_post)

def setup_inputs(seed: int = 0) -> dict:
    key = jax.random.key(seed)
    ks = iter(jax.random.split(key, 48))

    def nrm(shape, scale):
        return scale * jax.random.normal(next(ks), shape, jnp.float32)

    L = DEPTH
    n = jnp.arange(SSM_STATE, dtype=jnp.float32)

    def gain(dim):
        return 1.0 + nrm((L, dim), 0.05)

    def lam_re():
        return -0.5 + nrm((L, SSM_GROUPS, SSM_STATE), 0.01)

    def lam_im():
        return math.pi * n + nrm((L, SSM_GROUPS, SSM_STATE), 0.01)

    def log_dt():
        return jax.random.uniform(next(ks), (L, SSM_GROUPS), jnp.float32,
                                  math.log(DT_MIN), math.log(DT_MAX))

    b_scale = (2.0 * SSM_CH) ** -0.5
    c_scale = (2.0 * SSM_STATE) ** -0.5
    return {
        "x": nrm((BATCH, SEQ, D_MODEL), 1.0),
        "norm_mix_pre": gain(D_MODEL),
        "w_in": nrm((L, D_MODEL, IN_WIDTH), D_MODEL ** -0.5),
        "attn_sink": nrm((L, N_HEADS), 0.5),
        "lam_re_f": lam_re(),
        "lam_im_f": lam_im(),
        "log_dt_f": log_dt(),
        "b_re_f": nrm((L, SSM_GROUPS, SSM_STATE, SSM_CH), b_scale),
        "b_im_f": nrm((L, SSM_GROUPS, SSM_STATE, SSM_CH), b_scale),
        "c_re_f": nrm((L, SSM_GROUPS, SSM_CH, SSM_STATE), c_scale),
        "c_im_f": nrm((L, SSM_GROUPS, SSM_CH, SSM_STATE), c_scale),
        "lam_re_b": lam_re(),
        "lam_im_b": lam_im(),
        "log_dt_b": log_dt(),
        "b_re_b": nrm((L, SSM_GROUPS, SSM_STATE, SSM_CH), b_scale),
        "b_im_b": nrm((L, SSM_GROUPS, SSM_STATE, SSM_CH), b_scale),
        "c_re_b": nrm((L, SSM_GROUPS, SSM_CH, SSM_STATE), c_scale),
        "c_im_b": nrm((L, SSM_GROUPS, SSM_CH, SSM_STATE), c_scale),
        "ssm_d": nrm((L, SSM_WIDTH), 1.0),
        "w_glu": nrm((L, SSM_WIDTH, SSM_WIDTH), SSM_WIDTH ** -0.5),
        "b_glu": nrm((L, SSM_WIDTH), 0.02),
        "w_branch_attn": nrm((L, ATTN_WIDTH, D_MODEL), ATTN_WIDTH ** -0.5),
        "w_branch_ssm": nrm((L, SSM_WIDTH, D_MODEL), SSM_WIDTH ** -0.5),
        "w_out": nrm((L, D_MODEL, D_MODEL), D_MODEL ** -0.5),
        "norm_mix_post": gain(D_MODEL),
        "norm_ffn_pre": gain(D_MODEL),
        "w_ffn_gate": nrm((L, D_MODEL, D_FF), D_MODEL ** -0.5),
        "w_ffn_up": nrm((L, D_MODEL, D_FF), D_MODEL ** -0.5),
        "conv_w": nrm((L, CONV_WIDTH, D_FF), CONV_WIDTH ** -0.5),
        "conv_b": nrm((L, D_FF), 0.02),
        "w_ffn_down": nrm((L, D_FF, D_MODEL), D_FF ** -0.5),
        "norm_ffn_post": gain(D_MODEL),
    }

def reference(x, norm_mix_pre, w_in, attn_sink,
              lam_re_f, lam_im_f, log_dt_f, b_re_f, b_im_f, c_re_f, c_im_f,
              lam_re_b, lam_im_b, log_dt_b, b_re_b, b_im_b, c_re_b, c_im_b,
              ssm_d, w_glu, b_glu, w_branch_attn, w_branch_ssm, w_out, norm_mix_post,
              norm_ffn_pre, w_ffn_gate, w_ffn_up, conv_w, conv_b, w_ffn_down, norm_ffn_post):
    for l in range(DEPTH):
        x = hybrid_layer(
            x, norm_mix_pre[l], w_in[l], attn_sink[l],
            lam_re_f[l], lam_im_f[l], log_dt_f[l], b_re_f[l], b_im_f[l], c_re_f[l], c_im_f[l],
            lam_re_b[l], lam_im_b[l], log_dt_b[l], b_re_b[l], b_im_b[l], c_re_b[l], c_im_b[l],
            ssm_d[l], w_glu[l], b_glu[l], w_branch_attn[l], w_branch_ssm[l], w_out[l], norm_mix_post[l],
            norm_ffn_pre[l], w_ffn_gate[l], w_ffn_up[l], conv_w[l], conv_b[l], w_ffn_down[l], norm_ffn_post[l])
    return x


_drawn_inputs = setup_inputs


def setup_inputs(seed=0):
    import zlib

    import numpy as np

    out = dict(_drawn_inputs(seed))
    spreads = {}
    factors = {'lam_re_f': 200.0,
     'lam_re_b': 200.0,
     'b_glu': 8.0,
     'conv_b': 5.037,
     'lam_im_f': 27.776,
     'log_dt_f': 29.608,
     'b_re_f': 38.392,
     'b_im_f': 38.712,
     'c_re_f': 38.344,
     'c_im_f': 38.368,
     'lam_im_b': 26.96,
     'log_dt_b': 30.224,
     'b_re_b': 37.576,
     'b_im_b': 37.216,
     'c_re_b': 36.992,
     'c_im_b': 36.84}
    for name, (base, spread) in spreads.items():
        noise = np.random.default_rng([zlib.crc32(name.encode()), seed]).standard_normal(out[name].shape)
        drawn = base * np.exp(spread * noise) if base else spread * noise
        out[name] = __import__('jax').numpy.asarray(drawn.astype(out[name].dtype))
    for name, factor in factors.items():
        out[name] = (out[name] * factor).astype(out[name].dtype)
    return out
```

```python
from contextlib import ExitStack

import concourse.bass as bass
import concourse.mybir as mybir

F32 = mybir.dt.float32
F32R = mybir.dt.float32r
BF16 = mybir.dt.bfloat16
I32 = mybir.dt.int32
ALU = mybir.AluOpType
ACT = mybir.ActivationFunctionType
AX_X = mybir.AxisListType.X

P = 128
TOK = 2048
D = 1024
KD = D // P
N_HEADS, N_KV, HEAD = 8, 2, 64
ATTN = N_HEADS * HEAD
KV = N_KV * HEAD
WINDOW = 128
SSM, SSM_CH, SSM_N = 512, 16, 64
GROUPS = SSM // SSM_CH
FF = 2816
KF = FF // P
EPS = 1e-6
NEG_INF = -1e30
BANK = 512
TILES = TOK // P
CHUNKS = TOK // BANK

SSM_L = 8
SSM_J = TOK // SSM_L


class Pool:

    def __init__(self, nc, ctx, tag):
        self.nc, self.ctx, self.tag = nc, ctx, tag
        self.handles = []
        self.lowest = min(nc.free_semaphores)
        ctx.callback(self.zero)

    def zero(self):
        if self.handles:
            self.nc.all_engine_barrier(sems_to_clear=range(self.lowest, self.lowest + len(self.handles)))
            for handle in self.handles:
                self.nc.release_semaphore(handle)

    def sb(self, name, shape, dt=F32):
        return self.ctx.enter_context(self.nc.sbuf_tensor(f"{self.tag}_{name}", shape, dt))

    def psum(self, name, shape, dt=F32):
        return self.ctx.enter_context(self.nc.psum_tensor(f"{self.tag}_{name}", shape, dt))

    def sem(self, name):
        self.handles.append(self.nc.alloc_semaphore(f"{self.tag}_{name}", self.lowest + len(self.handles)))
        return self.handles[-1]

    def pool_dma_sem(self, name):
        return self.nc.alloc_semaphore(f"{self.tag}_{name}", max(self.nc.free_semaphores))


def row_broadcast(vector, n=P):
    return vector.rearrange("(a d) -> a d", a=1).broadcast_to([n, vector.shape[0]])


RING = 4


def over_tiles(engine, step, ahead=None):
    last = TILES // RING - 1
    if ahead:
        ahead(0, 0)
    with engine.Fori(0, last) as i:
        for s in range(RING):
            if ahead:
                ahead(i + (s + 1) // RING, (s + 1) % RING)
            step(i, s)
    for s in range(RING):
        if ahead and s + 1 < RING:
            ahead(last, s + 1)
        step(last, s)


def rms_constants(pool, consts, ready):
    for n, value in enumerate((1.0 / D, EPS, -0.5)):
        pool.memset(consts[:, n:n + 1], value).then_inc(ready, 1)


class NormTranspose:

    def __init__(self, m, src, gain):
        self.src, self.gain = src, gain
        self.feat_hi = m.sb("feat_hi", [P, KD, TOK], F32R)
        self.feat_lo = m.sb("feat_lo", [P, KD, TOK], F32R)
        self.rows = m.sb("rows", [P, RING, D])
        self.normed = m.sb("normed", [P, 2, D])
        self.squares = m.sb("squares", [P, D], BF16)
        self.gain_rows = m.sb("gain_rows", [P, D])
        self.ident = m.sb("ident", [P, P])
        self.consts = m.sb("consts", [P, 3])
        self.stat = m.sb("stat", [P, RING, 4])
        self.rows_in = [m.sem(f"rows_in{s}") for s in range(RING)]
        self.gain_in = m.sem("gain_in")
        self.const_ready = m.sem("const_ready")
        self.square_sum = m.sem("square_sum")
        self.mean_square = m.sem("mean_square")
        self.rstd = m.sem("rstd")
        self.normed_ready = m.sem("normed_ready")
        self.turned = m.sem("turned")
        self.hi_ready = m.sem("hi_ready")
        self.lo_ready = m.sem("lo_ready")

    def load(self, sync):
        def load_tile(i, s):
            t = i * RING + s
            sync.wait_ge(self.normed_ready, t + 1)
            sync.dma_start(self.rows[:, s, :], self.src[bass.ds(t * P, P), :]).then_inc(self.rows_in[s], 16)
            if isinstance(i, int) and t == 0:
                sync.dma_start(self.gain_rows[:], row_broadcast(self.gain)).then_inc(self.gain_in, 16)

        load_tile(0, 0)
        for s in range(1, RING):
            load_tile(0, s)
        with sync.Fori(1, TILES // RING) as i:
            for s in range(RING):
                load_tile(i, s)

    def gpsimd(self, pool):
        pool.memset(self.ident[:], 0.0).then_inc(self.const_ready, 1)
        rms_constants(pool, self.consts, self.const_ready)
        pool.wait_ge(self.const_ready, 4)
        pool.affine_select(out=self.ident[:], in_=self.ident[:], compare_op=ALU.not_equal, fill=1.0,
                           base=0, pattern=[[-1, P]], channel_multiplier=1).then_inc(self.const_ready, 1)

        def inverse_root(i, s):
            t = i * RING + s
            stat = self.stat
            pool.wait_ge(self.square_sum, t + 2)
            pool.tensor_tensor(stat[:, s, 1:2], stat[:, s, 0:1], self.consts[:, 0:1], ALU.mult)\
                .then_inc(self.mean_square, 1)
            pool.wait_ge(self.mean_square, t * 2 + 1)
            pool.tensor_tensor(stat[:, s, 2:3], stat[:, s, 1:2], self.consts[:, 1:2], ALU.add)\
                .then_inc(self.mean_square, 1)
            pool.wait_ge(self.mean_square, t * 2 + 2)
            pool.tensor_tensor(stat[:, s, 3:4], stat[:, s, 2:3], self.consts[:, 2:3], ALU.pow)\
                .then_inc(self.rstd, 1)

        over_tiles(pool, inverse_root)

    def scalar(self, act, psum):
        def square(i, s):
            t = i * RING + s
            act.wait_ge(self.square_sum, t + 1)
            act.wait_ge(self.rows_in[s], i * 16 + 16)
            act.wait_ge(self.normed_ready, t + 1)
            act.activation(self.squares[:], self.rows[:, s, :], ACT.Square,
                           accum_out=self.stat[:, s, 0:1]).then_inc(self.square_sum, 1)

        def keep_hi(i, s):
            t = i * RING + s
            act.wait_ge(self.turned, t + 3)
            act.activation(self.feat_hi[:, :, bass.ds(t * P, P)], psum[:, s % 2, :, :], ACT.Copy)\
                .then_inc(self.hi_ready, 1)

        act.sem_inc(self.square_sum, 1)
        over_tiles(act, keep_hi, square)

    def vector(self, dve, psum):
        def norm(i, s):
            t = i * RING + s
            dve.wait_ge(self.rstd, t + 1)
            dve.wait_ge(self.turned, t + 1)
            dve.scalar_tensor_tensor(out=self.normed[:, s % 2, :], in0=self.rows[:, s, :],
                                     scalar=self.stat[:, s, 3:4], in1=self.gain_rows[:],
                                     op0=ALU.mult, op1=ALU.mult).then_inc(self.normed_ready, 1)

        def keep_lo(i, s):
            t = i * RING + s
            dve.wait_ge(self.hi_ready, t + 1)
            cols = bass.ds(t * P, P)
            dve.tensor_tensor(self.feat_lo[:, :, cols], psum[:, s % 2, :, :],
                              self.feat_hi[:, :, cols].bitcast(F32), ALU.subtract).then_inc(self.lo_ready, 1)

        dve.sem_inc(self.normed_ready, RING)
        dve.sem_inc(self.lo_ready, 2)
        dve.wait_ge(self.gain_in, 16)
        over_tiles(dve, keep_lo, norm)

    def tensor(self, pe, psum):
        def turn_tile(i, s):
            t = i * RING + s
            pe.wait_ge(self.normed_ready, t + (RING + 1))
            pe.wait_ge(self.lo_ready, t + 1)
            for k in range(KD):
                turn = pe.transpose(psum[:, s % 2, k, :], self.normed[:, s % 2, k * P:(k + 1) * P], self.ident[:])
            turn.then_inc(self.turned, 1)

        pe.sem_inc(self.turned, 2)
        pe.wait_ge(self.const_ready, 5)
        over_tiles(pe, turn_tile)

    def tensor_done(self, pe):
        pe.wait_ge(self.lo_ready, TILES + 2)


class WeightStream:

    def __init__(self, m, k):
        self.k = k
        self.raw = m.sb("w_raw", [P, 2, k, P])
        self.hi = m.sb("w_hi", [P, 2, k, P], F32R)
        self.lo = m.sb("w_lo", [P, 2, k, P], F32R)
        self.raw_in = [m.sem("w_raw_in0"), m.sem("w_raw_in1")]
        self.raw_free = m.sem("w_raw_free")
        self.hi_ready = m.sem("w_hi_ready")
        self.lo_ready = m.sem("w_lo_ready")
        self.split_free = m.sem("w_split_free")

    def load(self, sync, weights, s, uses, n, columns):
        sync.wait_ge(self.raw_free, n + 1)
        sync.dma_start(self.raw[:, s], weights.rearrange("(k p) n -> p k n", p=P)[:, :, columns])\
            .then_inc(self.raw_in[s], 16)

    def vector(self, dve, s, uses, n):
        dve.wait_ge(self.raw_in[s], uses * 16 + 16)
        dve.wait_ge(self.split_free, n + 1)
        dve.tensor_copy(self.hi[:, s], self.raw[:, s]).then_inc(self.hi_ready, 1)
        dve.wait_ge(self.hi_ready, n + 1)
        dve.tensor_tensor(self.lo[:, s], self.raw[:, s], self.hi[:, s].bitcast(F32), ALU.subtract)\
            .then_inc(self.lo_ready, 1)
        dve.wait_ge(self.lo_ready, n + 1)
        dve.sem_inc(self.raw_free, 1)


def split_products(pe, out, w_hi, w_lo, x_hi, x_lo, first, last):
    pe.matmul(out, w_hi, x_hi, start=first, stop=False)
    pe.matmul(out, w_lo, x_hi, start=False, stop=False)
    return pe.matmul(out, w_hi, x_lo, start=False, stop=last)


def stage_project_in(nc, x, gain, w_in, qkv, u_scratch, gate_scratch):
    with ExitStack() as ctx:
        m = Pool(nc, ctx, "pi")
        nt = NormTranspose(m, x, gain)
        ws = WeightStream(m, KD)
        rows_out = m.sb("rows_out", [P, 2, TOK])
        banks = m.psum("banks", [P, 8, BANK])
        turn_psum = banks[:, 0:4, :].rearrange("p (s b) (k t) -> p s (b k) t", s=2, t=P)
        chunk_done = m.sem("chunk_done")
        chunk_free = m.sem("chunk_free")
        out_ready = m.sem("out_ready")
        stored = [m.sem("stored0"), m.sem("stored1")]
        n_qkv, n_u, n_gate = qkv.shape[0] // P, SSM // P, 2 * D // P
        parts = [(0, n_qkv, qkv, "plain"), (n_qkv, n_u, u_scratch, "by chunk"),
                 (n_qkv + n_u, n_gate, gate_scratch, "sigmoid")]
        n_blocks = n_qkv + n_u + n_gate
        block = ctx.enter_context(nc.Block())

        @block.gpsimd
        def _(pool):
            nt.gpsimd(pool)

        @block.sync
        def _(sync):
            nt.load(sync)
            with sync.Fori(0, n_blocks // 2) as i:
                for s in range(2):
                    ws.load(sync, w_in, s, i, i * 2 + s, bass.ds((i * 2 + s) * P, P))

        @block.vector
        def _(dve):
            nt.vector(dve, turn_psum)
            dve.sem_inc(ws.raw_free, 2)
            with dve.Fori(0, n_blocks // 2) as i:
                for s in range(2):
                    ws.vector(dve, s, i, i * 2 + s)

        @block.tensor
        def _(pe):
            nt.tensor(pe, turn_psum)
            nt.tensor_done(pe)
            pe.sem_inc(ws.split_free, 2)
            with pe.Fori(0, n_blocks // 2) as i:
                for s in range(2):
                    b = i * 2 + s
                    pe.wait_ge(ws.lo_ready, b + 1)
                    for c in range(CHUNKS):
                        pe.wait_ge(chunk_free, b * CHUNKS + c + 1)
                        for k in range(KD):
                            cols = slice(c * BANK, (c + 1) * BANK)
                            last = split_products(pe, banks[:, s * CHUNKS + c, :],
                                                  ws.hi[:, s, k], ws.lo[:, s, k],
                                                  nt.feat_hi[:, k, cols], nt.feat_lo[:, k, cols],
                                                  k == 0, k == KD - 1)
                        last.then_inc(chunk_done, 1)
                    pe.wait_ge(chunk_done, (b + 1) * CHUNKS)
                    pe.sem_inc(ws.split_free, 1)

        @block.scalar
        def _(act):
            nt.scalar(act, turn_psum)
            act.sem_inc(chunk_free, 2 * CHUNKS)
            for s in range(2):
                act.sem_inc(stored[s], 16)
            for first, count, dest, kind in parts:
                dest_rows = dest.rearrange("(b p) t -> b p t", p=P)
                with act.Fori(0, count // 2) as i:
                    for s in range(2):
                        b = i * 2 + s
                        uses = i + first // 2
                        act.wait_ge(stored[s], uses * 16 + 16)
                        for c in range(CHUNKS):
                            act.wait_ge(chunk_done, (b + first) * CHUNKS + c + 1)
                            if kind == "by chunk":
                                out = rows_out[:, s, :].rearrange("p (l j) -> p j l", l=SSM_L)
                                n = BANK // SSM_L
                                out = out[:, c * n:(c + 1) * n, :]
                                src = banks[:, s * CHUNKS + c, :].rearrange("p (j l) -> p j l", l=SSM_L)
                            else:
                                out = rows_out[:, s, c * BANK:(c + 1) * BANK]
                                src = banks[:, s * CHUNKS + c, :]
                            func = ACT.Sigmoid if kind == "sigmoid" else ACT.Copy
                            act.activation(out, src, func).then_inc(chunk_free, 1)
                        act.wait_ge(chunk_free, (b + first) * CHUNKS + 3 * CHUNKS)
                        act.dma_start(dest_rows[b], rows_out[:, s, :]).then_inc(stored[s], 16)
            for s in range(2):
                act.wait_ge(stored[s], (n_blocks // 2) * 16 + 16)


def stage_gate_up(nc, x_mid, gain, w_gate, w_up, conv_w, conv_b, f_scratch):
    with ExitStack() as ctx:
        m = Pool(nc, ctx, "gu")
        nt = NormTranspose(m, x_mid, gain)
        ws = WeightStream(m, KD)
        gate = m.sb("gate", [P, TOK + 2])
        conv = m.sb("conv", [P, TOK])
        taps = m.sb("taps", [P, 4, KF])
        banks = m.psum("banks", [P, 8, BANK])
        turn_psum = banks[:, 0:4, :].rearrange("p (s b) (k t) -> p s (b k) t", s=2, t=P)
        taps_in = m.sem("taps_in")
        edges_zero = m.sem("edges_zero")
        chunk_done = m.sem("chunk_done")
        gate_read = m.sem("gate_read")
        up_read = m.sem("up_read")
        gate_free = m.sem("gate_free")
        tap = m.sem("tap")
        gelu_done = m.sem("gelu_done")
        stored = m.pool_dma_sem("stored")
        conv_free = m.sem("conv_free")
        f_rows = f_scratch.rearrange("(b p) t -> b p t", p=P)
        block = ctx.enter_context(nc.Block())

        @block.gpsimd
        def _(pool):
            pool.memset(gate[:, 0:1], 0.0).then_inc(edges_zero, 1)
            pool.memset(gate[:, TOK + 1:TOK + 2], 0.0).then_inc(edges_zero, 1)
            nt.gpsimd(pool)

        @block.sync
        def _(sync):
            nt.load(sync)
            with sync.Fori(0, KF) as i:
                ws.load(sync, w_gate, 0, i, i * 2, bass.ds(i * P, P))
                ws.load(sync, w_up, 1, i, i * 2 + 1, bass.ds(i * P, P))

        @block.tensor
        def _(pe):
            nt.tensor(pe, turn_psum)
            nt.tensor_done(pe)
            pe.sem_inc(ws.split_free, 2)
            with pe.Fori(0, KF) as i:
                for s in range(2):
                    b = i * 2 + s
                    pe.wait_ge(ws.lo_ready, b + 1)
                    for c in range(CHUNKS):
                        pe.wait_ge(up_read if s else gate_read, i * CHUNKS + c + 1)
                        for k in range(KD):
                            cols = slice(c * BANK, (c + 1) * BANK)
                            last = split_products(pe, banks[:, s * CHUNKS + c, :],
                                                  ws.hi[:, s, k], ws.lo[:, s, k],
                                                  nt.feat_hi[:, k, cols], nt.feat_lo[:, k, cols],
                                                  k == 0, k == KD - 1)
                        last.then_inc(chunk_done, 1)
                    pe.wait_ge(chunk_done, (b + 1) * CHUNKS)
                    pe.sem_inc(ws.split_free, 1)

        @block.scalar
        def _(act):
            with nc.allow_non_contiguous_dma(reason="small"):
                for j in range(3):
                    act.dma_start(taps[:, j, :], conv_w[j].rearrange("(b p) -> p b", p=P)).then_inc(taps_in, 16)
                act.dma_start(taps[:, 3, :], conv_b.rearrange("(b p) -> p b", p=P)).then_inc(taps_in, 16)
            nt.scalar(act, turn_psum)
            act.sem_inc(gate_read, CHUNKS)
            act.sem_inc(gelu_done, 1)
            act.wait_ge(taps_in, 64)
            with act.Fori(0, KF) as i:
                act.wait_ge(gate_free, i + 1)
                for c in range(CHUNKS):
                    act.wait_ge(chunk_done, i * 2 * CHUNKS + c + 1)
                    act.activation(gate[:, 1 + c * BANK:1 + (c + 1) * BANK], banks[:, c, :], ACT.Copy)\
                        .then_inc(gate_read, 1)
                act.wait_ge(tap, i * 3 + 3)
                act.activation(conv[:], conv[:], ACT.Gelu_apprx_tanh, bias=taps[:, 3, bass.ds(i, 1)]).then_inc(gelu_done, 1)

        @block.vector
        def _(dve):
            nt.vector(dve, turn_psum)
            dve.sem_inc(ws.raw_free, 2)
            dve.sem_inc(gate_free, 1)
            dve.sem_inc(up_read, CHUNKS)
            ws.vector(dve, 0, 0, 0)
            ws.vector(dve, 1, 0, 1)
            dve.wait_ge(taps_in, 64)
            dve.wait_ge(edges_zero, 2)
            dve.sem_inc(conv_free, 1)

            def finish(i):
                dve.wait_ge(gate_read, i * CHUNKS + 2 * CHUNKS)
                dve.wait_ge(conv_free, i + 1)
                dve.tensor_scalar(conv[:], gate[:, 0:TOK], taps[:, 0, bass.ds(i, 1)], None,
                                  ALU.mult).then_inc(tap, 1)
                dve.wait_ge(tap, i * 3 + 1)
                dve.scalar_tensor_tensor(out=conv[:], in0=gate[:, 1:TOK + 1], scalar=taps[:, 1, bass.ds(i, 1)],
                                         in1=conv[:], op0=ALU.mult, op1=ALU.add).then_inc(tap, 1)
                dve.wait_ge(tap, i * 3 + 2)
                dve.scalar_tensor_tensor(out=conv[:], in0=gate[:, 2:TOK + 2], scalar=taps[:, 2, bass.ds(i, 1)],
                                         in1=conv[:], op0=ALU.mult, op1=ALU.add).then_inc(tap, 1)

            def times_up(i):
                dve.wait_ge(gelu_done, i + 2)
                for c in range(CHUNKS):
                    cols = slice(c * BANK, (c + 1) * BANK)
                    dve.wait_ge(chunk_done, (i * 2 + 1) * CHUNKS + c + 1)
                    dve.tensor_tensor(conv[:, cols], conv[:, cols], banks[:, CHUNKS + c, :], ALU.mult)\
                        .then_inc(up_read, 1)

            with dve.Fori(0, KF - 1) as i:
                ws.vector(dve, 0, i + 1, i * 2 + 2)
                finish(i)
                dve.wait_ge(tap, i * 3 + 3)
                dve.sem_inc(gate_free, 1)
                ws.vector(dve, 1, i + 1, i * 2 + 3)
                times_up(i)
            finish(KF - 1)
            times_up(KF - 1)

        @block.gpsimd
        def _(pool):
            with pool.Fori(0, KF) as i:
                pool.wait_ge(up_read, i * CHUNKS + 2 * CHUNKS)
                pool.dma_start(f_rows[i], conv[:]).then_inc(stored, 16)
                pool.wait_ge(stored, i * 16 + 16)
                pool.sem_inc(conv_free, 1)


class PostNorm:

    def __init__(self, m, residual, gain, out):
        self.residual = residual.rearrange("(t p) d -> t p d", p=P)
        self.out = out.rearrange("(t p) d -> t p d", p=P)
        self.gain = gain
        self.gain_rows = m.sb("gain_rows", [P, 2, BANK])
        self.rows = m.sb("rows", [P, 2, 2, BANK])
        self.scaled = m.sb("scaled", [P, 2, BANK])
        self.stat = m.sb("stat", [P, 2, 6])
        self.consts = m.sb("consts", [P, 3])
        self.gain_in = m.sem("gain_in")
        self.rows_in = [m.sem("rows_in0"), m.sem("rows_in1")]
        self.square_sum = m.sem("square_sum")
        self.mean_square = m.sem("mean_square")
        self.const_ready = m.sem("const_ready")
        self.rstd = m.sem("rstd")
        self.scaled_ready = m.sem("scaled_ready")
        self.sum_ready = m.sem("sum_ready")
        self.stored = m.pool_dma_sem("stored")
        self.rows_free = m.sem("rows_free")

    def load_gain(self, sync):
        sync.dma_start(self.gain_rows[:].rearrange("p a b -> p (a b)"), row_broadcast(self.gain))\
            .then_inc(self.gain_in, 16)
        sync.sem_inc(self.rows_free, 2)

    def load(self, sync, t, s, uses):
        sync.wait_ge(self.rows_free, t + 1)
        sync.dma_start(self.rows[:, s].rearrange("p a b -> p (a b)"), self.residual[t]).then_inc(self.rows_in[s], 16)

    def scalar(self, act, t, s, halves):
        act.wait_ge(self.sum_ready, t + 1)
        for h in range(2):
            act.activation(self.scaled[:, h, :], halves[h], ACT.Square,
                           accum_out=self.stat[:, s, h:h + 1]).then_inc(self.square_sum, 1)

    def inverse_root(self, pool, t, s):
        stat = self.stat
        pool.wait_ge(self.square_sum, t * 2 + 2)
        pool.tensor_tensor(stat[:, s, 2:3], stat[:, s, 0:1], stat[:, s, 1:2], ALU.add).then_inc(self.mean_square, 1)
        pool.wait_ge(self.mean_square, t * 3 + 1)
        pool.tensor_tensor(stat[:, s, 3:4], stat[:, s, 2:3], self.consts[:, 0:1], ALU.mult)\
            .then_inc(self.mean_square, 1)
        pool.wait_ge(self.mean_square, t * 3 + 2)
        pool.tensor_tensor(stat[:, s, 4:5], stat[:, s, 3:4], self.consts[:, 1:2], ALU.add)\
            .then_inc(self.mean_square, 1)
        pool.wait_ge(self.mean_square, t * 3 + 3)
        pool.tensor_tensor(stat[:, s, 5:6], stat[:, s, 4:5], self.consts[:, 2:3], ALU.pow).then_inc(self.rstd, 1)

    def gpsimd_start(self, pool):
        rms_constants(pool, self.consts, self.const_ready)
        pool.wait_ge(self.const_ready, 3)

    def vector(self, dve, t, s, uses, halves):
        dve.wait_ge(self.rstd, t + 1)
        for h in range(2):
            dve.scalar_tensor_tensor(out=self.scaled[:, h, :], in0=halves[h], scalar=self.stat[:, s, 5:6],
                                     in1=self.gain_rows[:, h, :], op0=ALU.mult, op1=ALU.mult)\
                .then_inc(self.scaled_ready, 1)
        dve.wait_ge(self.scaled_ready, t * 2 + 2)
        dve.wait_ge(self.rows_in[s], uses * 16 + 16)
        dve.tensor_tensor(self.rows[:, s], self.rows[:, s], self.scaled[:], ALU.add).then_inc(self.sum_ready, 1)

    def vector_start(self, dve):
        dve.wait_ge(self.gain_in, 16)
        dve.sem_inc(self.sum_ready, 1)

    def store(self, pool, t, s):
        pool.wait_ge(self.sum_ready, t + 2)
        pool.dma_start(self.out[t], self.rows[:, s].rearrange("p a b -> p (a b)")).then_inc(self.stored, 16)
        pool.wait_ge(self.stored, t * 16 + 16)
        pool.sem_inc(self.rows_free, 1)


def stage_down(nc, f_scratch, w_down, gain, x_mid, out):
    with ExitStack() as ctx:
        m = Pool(nc, ctx, "dn")
        pn = PostNorm(m, x_mid, gain, out)
        KH = KF // 2
        w_raw = m.sb("w_raw", [P, 2, BANK])
        w_hi = m.sb("w_hi", [P, KF, BANK], F32R)
        w_lo = m.sb("w_lo", [P, KF, BANK], F32R)
        f_raw = m.sb("f_raw", [P, 2, 2, KH, P])
        f_hi = m.sb("f_hi", [P, 2, KF, P], F32R)
        f_lo = m.sb("f_lo", [P, 2, KF, P], F32R)
        y_first = m.sb("y_first", [P, TILES, BANK])
        y = m.psum("y", [P, 2, BANK])
        w_in = [m.pool_dma_sem("w_in0"), m.pool_dma_sem("w_in1")]
        w_hi_ready = m.sem("w_hi_ready")
        w_lo_ready = m.sem("w_lo_ready")
        f_in = [[m.sem(f"f_in{s}{h}") for h in range(2)] for s in range(2)]
        f_hi_ready = m.sem("f_hi_ready")
        f_lo_ready = m.sem("f_lo_ready")
        f_free = m.sem("f_free")
        y_done = m.sem("y_done")
        y_copied = m.sem("y_copied")
        y_free = m.sem("y_free")
        w_used = m.sem("w_used")
        f_tiles = f_scratch.rearrange("(h k p) (t c) -> t h p k c", p=P, h=2, c=P)
        w_rows = w_down.rearrange("(k p) (h n) -> h k p n", p=P, h=2)
        block = ctx.enter_context(nc.Block())


        @block.sync
        def _(sync):
            pn.load_gain(sync)
            for half in range(2):
                with sync.Fori(0, TILES // 2) as i:
                    for s in range(2):
                        t = i * 2 + s
                        if half:
                            pn.load(sync, t, s, i)
                        for h in range(2):
                            sync.wait_ge(f_lo_ready, t * 2 + (half * TILES * 2 + h + 1))
                            sync.dma_start(f_raw[:, s, h], f_tiles[t, h]).then_inc(f_in[s][h], 16)

        @block.gpsimd
        def _(pool):
            pn.gpsimd_start(pool)
            for half in range(2):
                with pool.Fori(0, KF // 2) as i:
                    for s in range(2):
                        k = i * 2 + s
                        pool.wait_ge(w_lo_ready, k + (half * KF + 1))
                        pool.dma_start(w_raw[:, s], w_rows[half, k]).then_inc(w_in[s], 16)
            with pool.Fori(0, TILES // 2) as i:
                for s in range(2):
                    pn.inverse_root(pool, i * 2 + s, s)
                    pn.store(pool, i * 2 + s, s)

        @block.tensor
        def _(pe):
            def tile(i, s, half, first=False, last=False):
                n = i * 2 + (half * TILES + s)
                pe.wait_ge(f_lo_ready, n * 2 + 6)
                pe.wait_ge(y_free, n + 1)
                for k in range(KF):
                    if first:
                        pe.wait_ge(w_lo_ready, half * KF + k + 3)
                    done = split_products(pe, y[:, s], f_hi[:, s, k], f_lo[:, s, k],
                                          w_hi[:, k], w_lo[:, k], k == 0, k == KF - 1)
                    if last and k < KF - 1:
                        done.then_inc(w_used, 1)
                done.then_inc(y_done, 1)
                pe.wait_ge(y_done, n + 1)
                pe.sem_inc(f_free, 1)
                if last:
                    pe.sem_inc(w_used, 1)

            pe.sem_inc(f_free, 2)
            for half in range(2):
                tile(0, 0, half, first=True)
                tile(0, 1, half)
                with pe.Fori(1, TILES // 2 - 1) as i:
                    for s in range(2):
                        tile(i, s, half)
                tile(TILES // 2 - 1, 0, half)
                tile(TILES // 2 - 1, 1, half, last=half == 0)

        @block.scalar
        def _(act):
            def split_hi(i, s):
                n = i * 2 + s
                act.wait_ge(f_free, n + 1)
                for h in range(2):
                    act.wait_ge(f_in[s][h], i * 16 + 16)
                    act.activation(f_hi[:, s, h * KH:(h + 1) * KH], f_raw[:, s, h], ACT.Copy)\
                        .then_inc(f_hi_ready, 1)

            def norm(i, s):
                t = i * 2 + s
                act.wait_ge(y_done, t + (TILES + 1))
                pn.scalar(act, t, s, [y_first[:, bass.ds(t, 1), :], y[:, s]])

            with act.Fori(0, TILES // 2 + 1) as i:
                for s in range(2):
                    split_hi(i, s)
            with act.Fori(0, TILES // 2 - 1) as i:
                for s in range(2):
                    norm(i, s)
                    split_hi(i + (TILES // 2 + 1), s)
            for s in range(2):
                norm(TILES // 2 - 1, s)

        @block.vector
        def _(dve):
            def split_lo(i, s):
                n = i * 2 + s
                for h in range(2):
                    dve.wait_ge(f_hi_ready, n * 2 + h + 1)
                    part = slice(h * KH, (h + 1) * KH)
                    dve.tensor_tensor(f_lo[:, s, part], f_raw[:, s, h], f_hi[:, s, part].bitcast(F32),
                                      ALU.subtract).then_inc(f_lo_ready, 1)

            def split_weights(half):
                with dve.Fori(0, KF // 2) as i:
                    for s in range(2):
                        k = i * 2 + s
                        dve.wait_ge(w_in[s], i * 16 + (half * KF * 8 + 16))
                        if half:
                            dve.wait_ge(w_used, k + 1)
                        dve.tensor_copy(w_hi[:, bass.ds(k, 1)], w_raw[:, s:s + 1]).then_inc(w_hi_ready, 1)
                        dve.wait_ge(w_hi_ready, k + (half * KF + 1))
                        dve.tensor_tensor(w_lo[:, bass.ds(k, 1)], w_raw[:, s:s + 1],
                                          w_hi[:, bass.ds(k, 1)].bitcast(F32), ALU.subtract)\
                            .then_inc(w_lo_ready, 1)

            def keep(i, s):
                t = i * 2 + s
                dve.wait_ge(y_done, t + 1)
                dve.tensor_copy(y_first[:, bass.ds(t, 1), :], y[:, s:s + 1]).then_inc(y_copied, 1)
                dve.wait_ge(y_copied, t + 1)
                dve.sem_inc(y_free, 1)

            def finish(i, s):
                t = i * 2 + s
                pn.vector(dve, t, s, i, [y_first[:, bass.ds(t, 1), :], y[:, s]])
                dve.sem_inc(y_free, 1)

            dve.sem_inc(f_lo_ready, 4)
            dve.sem_inc(w_lo_ready, 2)
            dve.sem_inc(y_free, 2)
            pn.vector_start(dve)
            for s in range(2):
                split_lo(0, s)
            split_weights(0)
            with dve.Fori(0, TILES // 2 - 1) as i:
                for s in range(2):
                    keep(i, s)
                    split_lo(i + 1, s)
            keep(TILES // 2 - 1, 0)
            split_lo(TILES // 2, 0)
            split_weights(1)
            keep(TILES // 2 - 1, 1)
            split_lo(TILES // 2, 1)
            with dve.Fori(0, TILES // 2 - 1) as i:
                for s in range(2):
                    finish(i, s)
                    split_lo(i + (TILES // 2 + 1), s)
            for s in range(2):
                finish(TILES // 2 - 1, s)


def stage_branches(nc, attn_scratch, y_scratch, gate_scratch, w_glu, b_glu, w_attn, w_ssm, merged_scratch):
    with ExitStack() as ctx:
        m = Pool(nc, ctx, "br")
        K = SSM // P
        ws = WeightStream(m, K)
        attn_hi = m.sb("attn_hi", [P, K, TOK], F32R)
        attn_lo = m.sb("attn_lo", [P, K, TOK], F32R)
        y = m.sb("y", [P, K, TOK])
        y_hi = m.sb("y_hi", [P, K, TOK], F32R)
        y_lo = m.sb("y_lo", [P, K, TOK], F32R)
        rows = m.sb("rows", [P, 4, TOK])
        bias = m.sb("bias", [P, K])
        banks = m.psum("banks", [P, 8, BANK])
        bias_in = m.sem("bias_in")
        y_in = [m.sem(f"y_in{k}") for k in range(K)]
        rows_in = [m.sem(f"rows_in{k}") for k in range(4)]
        hi_ready = m.sem("hi_ready")
        lo_ready = m.sem("lo_ready")
        chunk_done = m.sem("chunk_done")
        sigmoid_ready = m.sem("sigmoid_ready")
        glu_done = m.sem("glu_done")
        chunk_free = m.sem("chunk_free")
        gated = m.sem("gated")
        merged_ready = m.sem("merged_ready")
        stored = m.sem("stored")
        rows_free = m.sem("rows_free")
        gates_in = [[m.pool_dma_sem(f"gates_in{s}{h}") for h in range(2)] for s in range(2)]
        gates = gate_scratch.rearrange("(h b p) t -> h b p t", h=2, p=P)
        merged_rows = merged_scratch.rearrange("(b p) t -> b p t", p=P)
        n_out = D // P
        by_token = "p (j l) -> p l j"
        by_chunk = "p (l j) -> p l j"
        block = ctx.enter_context(nc.Block())

        @block.sync
        def _(sync):
            with nc.allow_non_contiguous_dma(reason="512 bias values"):
                sync.dma_start(bias[:], b_glu.rearrange("(k p) -> p k", p=P)).then_inc(bias_in, 16)
            for k in range(K):
                sync.dma_start(y[:, k], y_scratch[k * P:(k + 1) * P, :]).then_inc(y_in[k], 16)
            for k in range(K):
                sync.dma_start(rows[:, k], attn_scratch[k * P:(k + 1) * P, :]).then_inc(rows_in[k], 16)
            with sync.Fori(0, K // 2) as i:
                for s in range(2):
                    ws.load(sync, w_glu, s, i, i * 2 + s, bass.ds((i * 2 + s) * P, P))
            with sync.Fori(0, n_out) as i:
                ws.load(sync, w_attn, 0, i + K // 2, i * 2 + K, bass.ds(i * P, P))
                ws.load(sync, w_ssm, 1, i + K // 2, i * 2 + K + 1, bass.ds(i * P, P))

        @block.gpsimd
        def _(pool):
            pool.wait_ge(lo_ready, 2 * K)
            with pool.Fori(0, n_out // 2) as i:
                for s in range(2):
                    pool.wait_ge(rows_free, i * 2 + s + 1)
                    for h in range(2):
                        pool.dma_start(rows[:, 2 * s + h], gates[h, i * 2 + s]).then_inc(gates_in[s][h], 16)

        @block.tensor
        def _(pe):
            pe.sem_inc(ws.split_free, 2)

            def product(b, s, x_hi, x_lo):
                pe.wait_ge(ws.lo_ready, b + 1)
                for c in range(CHUNKS):
                    pe.wait_ge(chunk_free, b * CHUNKS + c + 1)
                    for k in range(K):
                        cols = slice(c * BANK, (c + 1) * BANK)
                        last = split_products(pe, banks[:, s * CHUNKS + c, :], ws.hi[:, s, k], ws.lo[:, s, k],
                                              x_hi[:, k, cols], x_lo[:, k, cols], k == 0, k == K - 1)
                    last.then_inc(chunk_done, 1)
                pe.wait_ge(chunk_done, b * CHUNKS + CHUNKS)
                pe.sem_inc(ws.split_free, 1)

            pe.wait_ge(lo_ready, K)
            with pe.Fori(0, K // 2) as i:
                for s in range(2):
                    product(i * 2 + s, s, y_hi, y_lo)
            pe.wait_ge(lo_ready, 2 * K)
            product(K, 0, attn_hi, attn_lo)
            pe.wait_ge(lo_ready, 3 * K)
            product(K + 1, 1, y_hi, y_lo)
            with pe.Fori(1, n_out) as i:
                product(i * 2 + K, 0, attn_hi, attn_lo)
                product(i * 2 + K + 1, 1, y_hi, y_lo)

        @block.scalar
        def _(act):
            act.wait_ge(bias_in, 16)
            for k in range(K):
                act.wait_ge(y_in[k], 16)
                act.activation(y_hi[:, k], y[:, k], ACT.Copy).then_inc(hi_ready, 1)
            for k in range(K):
                act.wait_ge(rows_in[k], 16)
                act.activation(attn_hi[:, k], rows[:, k], ACT.Copy).then_inc(hi_ready, 1)
            for b in range(K):
                for c in range(CHUNKS):
                    act.wait_ge(chunk_done, b * CHUNKS + c + 1)
                    bank = banks[:, b % 2 * CHUNKS + c, :]
                    act.activation(bank, bank, ACT.Sigmoid, bias=bias[:, b:b + 1]).then_inc(sigmoid_ready, 1)
            for k in range(K):
                act.wait_ge(glu_done, K * CHUNKS)
                act.activation(y_hi[:, k].rearrange(by_token, l=SSM_L), y[:, k].rearrange(by_chunk, l=SSM_L),
                               ACT.Copy).then_inc(hi_ready, 1)
            with act.Fori(0, n_out // 2) as i:
                for s in range(2):
                    n = i * 2 + s
                    act.wait_ge(merged_ready, n + 1)
                    act.dma_start(merged_rows[n], rows[:, 2 * s]).then_inc(stored, 16)
                    act.wait_ge(stored, n * 16 + 16)
                    act.sem_inc(rows_free, 1)

        @block.vector
        def _(dve):
            dve.sem_inc(ws.raw_free, 2)
            dve.sem_inc(chunk_free, 2 * CHUNKS)
            dve.sem_inc(rows_free, 2)
            for k in range(K):
                dve.wait_ge(hi_ready, k + 1)
                dve.tensor_tensor(y_lo[:, k], y[:, k], y_hi[:, k].bitcast(F32), ALU.subtract).then_inc(lo_ready, 1)
            for s in range(2):
                ws.vector(dve, s, 0, s)
            for k in range(K):
                dve.wait_ge(hi_ready, K + k + 1)
                dve.tensor_tensor(attn_lo[:, k], rows[:, k], attn_hi[:, k].bitcast(F32), ALU.subtract)\
                    .then_inc(lo_ready, 1)
            for b in range(K):
                for c in range(CHUNKS):
                    dve.wait_ge(sigmoid_ready, b * CHUNKS + c + 1)
                    cols = slice(c * BANK, (c + 1) * BANK)
                    dve.tensor_tensor(y[:, b, cols], y[:, b, cols], banks[:, b % 2 * CHUNKS + c, :], ALU.mult)\
                        .then_inc(glu_done, 1)
                    dve.wait_ge(glu_done, b * CHUNKS + c + 1)
                    dve.sem_inc(chunk_free, 1)
                ws.vector(dve, b % 2, b // 2 + 1, b + 2)
            for k in range(K):
                dve.wait_ge(hi_ready, 2 * K + k + 1)
                dve.tensor_tensor(y_lo[:, k].rearrange(by_token, l=SSM_L), y[:, k].rearrange(by_chunk, l=SSM_L),
                                  y_hi[:, k].bitcast(F32).rearrange(by_token, l=SSM_L), ALU.subtract)\
                    .then_inc(lo_ready, 1)

            def merge(i, s, last=False):
                n = i * 2 + s
                for h in range(2):
                    dve.wait_ge(gates_in[s][h], i * 16 + 16)
                    for c in range(CHUNKS):
                        dve.wait_ge(chunk_done, n * (2 * CHUNKS) + ((K + h) * CHUNKS + c + 1))
                        cols = slice(c * BANK, (c + 1) * BANK)
                        dve.tensor_tensor(rows[:, 2 * s + h, cols], rows[:, 2 * s + h, cols],
                                          banks[:, h * CHUNKS + c, :], ALU.mult).then_inc(gated, 1)
                        dve.wait_ge(gated, n * (2 * CHUNKS) + (h * CHUNKS + c + 1))
                        dve.sem_inc(chunk_free, 1)
                    if not last:
                        ws.vector(dve, h, n + (K // 2 + 1), n * 2 + (K + 2 + h))
                dve.tensor_tensor(rows[:, 2 * s], rows[:, 2 * s], rows[:, 2 * s + 1], ALU.add)\
                    .then_inc(merged_ready, 1)

            with dve.Fori(0, n_out // 2 - 1) as i:
                for s in range(2):
                    merge(i, s)
            merge(n_out // 2 - 1, 0)
            merge(n_out // 2 - 1, 1, last=True)


def stage_out(nc, merged_scratch, w_out, gain, x, x_mid):
    with ExitStack() as ctx:
        m = Pool(nc, ctx, "ou")
        pn = PostNorm(m, x, gain, x_mid)
        w_raw = m.sb("w_raw", [P, 2, D])
        w_hi = m.sb("w_hi", [P, KD, D], F32R)
        w_lo = m.sb("w_lo", [P, KD, D], F32R)
        g_raw = m.sb("g_raw", [P, 2, KD, P])
        g_hi = m.sb("g_hi", [P, 2, KD, P], F32R)
        g_lo = m.sb("g_lo", [P, 2, KD, P], F32R)
        y = m.psum("y", [P, 2, 2, BANK])
        w_in = [m.pool_dma_sem("w_in0"), m.pool_dma_sem("w_in1")]
        w_hi_ready = m.sem("w_hi_ready")
        w_lo_ready = m.sem("w_lo_ready")
        g_in = [m.sem("g_in0"), m.sem("g_in1")]
        g_hi_ready = m.sem("g_hi_ready")
        g_lo_ready = m.sem("g_lo_ready")
        g_free = m.sem("g_free")
        y_done = m.sem("y_done")
        y_free = m.sem("y_free")
        g_tiles = merged_scratch.rearrange("(k p) (t c) -> t p k c", p=P, c=P)
        w_rows = w_out.rearrange("(k p) n -> k p n", p=P)
        block = ctx.enter_context(nc.Block())

        @block.sync
        def _(sync):
            pn.load_gain(sync)
            with sync.Fori(0, TILES // 2) as i:
                for s in range(2):
                    t = i * 2 + s
                    sync.wait_ge(g_lo_ready, t + 1)
                    sync.dma_start(g_raw[:, s], g_tiles[t]).then_inc(g_in[s], 16)
                    pn.load(sync, t, s, i)

        @block.gpsimd
        def _(pool):
            pn.gpsimd_start(pool)
            with pool.Fori(0, KD // 2) as i:
                for s in range(2):
                    pool.wait_ge(w_lo_ready, i * 2 + s + 1)
                    pool.dma_start(w_raw[:, s], w_rows[i * 2 + s]).then_inc(w_in[s], 16)
            with pool.Fori(0, TILES // 2) as i:
                for s in range(2):
                    pn.inverse_root(pool, i * 2 + s, s)
                    pn.store(pool, i * 2 + s, s)

        @block.tensor
        def _(pe):
            def tile(i, s, first=False):
                t = i * 2 + s
                pe.wait_ge(g_lo_ready, t + 3)
                pe.wait_ge(y_free, t + 1)
                for k in range(KD):
                    if first:
                        pe.wait_ge(w_lo_ready, k + 3)
                    for h in range(2):
                        cols = slice(h * BANK, (h + 1) * BANK)
                        done = split_products(pe, y[:, s, h], g_hi[:, s, k], g_lo[:, s, k],
                                              w_hi[:, k, cols], w_lo[:, k, cols], k == 0, k == KD - 1)
                done.then_inc(y_done, 1)
                pe.wait_ge(y_done, t + 1)
                pe.sem_inc(g_free, 1)

            pe.sem_inc(g_free, 2)
            tile(0, 0, first=True)
            tile(0, 1)
            with pe.Fori(1, TILES // 2) as i:
                for s in range(2):
                    tile(i, s)

        @block.scalar
        def _(act):
            def split_hi(i, s):
                act.wait_ge(g_free, i * 2 + s + 1)
                act.wait_ge(g_in[s], i * 16 + 16)
                act.activation(g_hi[:, s], g_raw[:, s], ACT.Copy).then_inc(g_hi_ready, 1)

            def norm(i, s):
                t = i * 2 + s
                act.wait_ge(y_done, t + 1)
                pn.scalar(act, t, s, [y[:, s, 0], y[:, s, 1]])

            for s in range(2):
                split_hi(0, s)
            with act.Fori(0, TILES // 2 - 1) as i:
                for s in range(2):
                    norm(i, s)
                    split_hi(i + 1, s)
            for s in range(2):
                norm(TILES // 2 - 1, s)

        @block.vector
        def _(dve):
            def split_lo(i, s):
                dve.wait_ge(g_hi_ready, i * 2 + s + 1)
                dve.tensor_tensor(g_lo[:, s], g_raw[:, s], g_hi[:, s].bitcast(F32), ALU.subtract)\
                    .then_inc(g_lo_ready, 1)

            def finish(i, s):
                pn.vector(dve, i * 2 + s, s, i, [y[:, s, 0], y[:, s, 1]])
                dve.sem_inc(y_free, 1)

            dve.sem_inc(g_lo_ready, 2)
            dve.sem_inc(w_lo_ready, 2)
            dve.sem_inc(y_free, 2)
            for s in range(2):
                split_lo(0, s)
            with dve.Fori(0, KD // 2) as i:
                for s in range(2):
                    k = i * 2 + s
                    dve.wait_ge(w_in[s], i * 16 + 16)
                    dve.tensor_copy(w_hi[:, bass.ds(k, 1)], w_raw[:, s:s + 1]).then_inc(w_hi_ready, 1)
                    dve.wait_ge(w_hi_ready, k + 1)
                    dve.tensor_tensor(w_lo[:, bass.ds(k, 1)], w_raw[:, s:s + 1],
                                      w_hi[:, bass.ds(k, 1)].bitcast(F32), ALU.subtract)\
                        .then_inc(w_lo_ready, 1)
            pn.vector_start(dve)
            with dve.Fori(0, TILES // 2 - 1) as i:
                for s in range(2):
                    finish(i, s)
                    split_lo(i + 1, s)
            for s in range(2):
                finish(TILES // 2 - 1, s)


def stage_attention(nc, qkv, sink, attn_scratch):
    with ExitStack() as ctx:
        m = Pool(nc, ctx, "at")
        KEYS = 3 * P
        group = N_HEADS // N_KV
        ident = m.sb("ident", [P, P])
        distance = m.sb("distance", [P, KEYS], I32)
        distance_f = m.sb("distance_f", [P, KEYS])
        bias = m.sb("bias", [P, N_HEADS, KEYS])
        sinks = m.sb("sinks", [P, N_HEADS])
        neg_sinks = m.sb("neg_sinks", [P, N_HEADS])
        q = m.sb("q", [HEAD, 2, N_HEADS, P])
        k = m.sb("k", [HEAD, 2, N_KV, KEYS])
        v_rows = m.sb("v_rows", [P, 2, KEYS])
        v = m.sb("v", [P, 2, 3, KV])
        neg_scores = m.sb("neg_scores", [P, 2, KEYS])
        probs = m.sb("probs", [P, 2, KEYS])
        probs_t = m.sb("probs_t", [P, 2, KEYS])
        neg_top = m.sb("neg_top", [P, 2, N_HEADS])
        sums = m.sb("sums", [P, 2, N_HEADS])
        sink_gap = m.sb("sink_gap", [P, N_HEADS])
        sink_exp = m.sb("sink_exp", [P, N_HEADS])
        total = m.sb("total", [P, N_HEADS])
        share = m.sb("share", [P, N_HEADS])
        attn = m.sb("attn", [P, N_HEADS, HEAD])
        attn_t = m.sb("attn_t", [P, 2, ATTN])
        s_psum = m.psum("s_psum", [P, 2, BANK])
        p_psum = m.psum("p_psum", [P, 2, BANK])
        o_psum = m.psum("o_psum", [P, 2, BANK])
        v_psum = m.psum("v_psum", [P, BANK])
        a_psum = m.psum("a_psum", [P, BANK])
        sinks_in = m.sem("sinks_in")
        ident_ready = m.sem("ident_ready")
        iota_ready = m.sem("iota_ready")
        bias_step = m.sem("bias_step")
        bias_ready = m.sem("bias_ready")
        q_in = [m.sem("q_in0"), m.sem("q_in1")]
        k_in = [m.sem("k_in0"), m.sem("k_in1")]
        v_in = [m.sem("v_in0"), m.sem("v_in1")]
        loaded_free = m.sem("loaded_free")
        scores_done = m.sem("scores_done")
        mask_started = m.sem("mask_started")
        masked = m.sem("masked")
        exp_done = m.sem("exp_done")
        turned = m.sem("turned")
        probs_t_ready = m.sem("probs_t_ready")
        pv_done = m.sem("pv_done")
        v_turned = m.sem("v_turned")
        v_ready = m.sem("v_ready")
        gap_ready = m.sem("gap_ready")
        sink_ready = m.sem("sink_ready")
        share_step = m.sem("share_step")
        attn_ready = m.sem("attn_ready")
        attn_turned = m.sem("attn_turned")
        out_ready = m.sem("out_ready")
        out_free = m.sem("out_free")
        stored = m.pool_dma_sem("stored")
        q_rows = qkv[0:ATTN, :].rearrange("(h d) t -> d h t", d=HEAD)
        k_rows = qkv[ATTN:ATTN + KV, :].rearrange("(h d) t -> d h t", d=HEAD)
        v_src = qkv[ATTN + KV:ATTN + 2 * KV, :]
        out_rows = attn_scratch.rearrange("(b p) t -> p b t", p=P)

        def keys_of(kind):
            lo, hi = {"first": (1, 3), "middle": (0, 3), "last": (0, 2)}[kind]
            return lo, hi, slice(lo * P, hi * P)

        def over_blocks(engine, body):
            body(0, 0, "first", "middle")
            body(0, 1, "middle", "middle")
            with engine.Fori(1, TILES // 2 - 1) as i:
                for s in range(2):
                    body(i, s, "middle", "middle")
            body(TILES // 2 - 1, 0, "middle", "last")
            body(TILES // 2 - 1, 1, "last", None)

        block = ctx.enter_context(nc.Block())

        @block.sync
        def _(sync):
            sync.dma_start(sinks[:], row_broadcast(sink)).then_inc(sinks_in, 16)

            def load(i, s, kind, following):
                lo, hi, part = keys_of(kind)
                b = i * 2 + s
                sync.wait_ge(loaded_free, b + 1)
                sync.dma_start(q[:, s], q_rows[:, :, bass.ds(b * P, P)]).then_inc(q_in[s], 16)
                keys = bass.ds(b * P + (lo - 1) * P, (hi - lo) * P)
                sync.dma_start(k[:, s, :, part], k_rows[:, :, keys]).then_inc(k_in[s], 16)
                sync.dma_start(v_rows[:, s, part], v_src[:, keys]).then_inc(v_in[s], 16)

            over_blocks(sync, load)

        @block.gpsimd
        def _(pool):
            pool.memset(ident[:], 0.0).then_inc(ident_ready, 1)
            pool.iota(distance[:], pattern=[[-1, KEYS]], base=P, channel_multiplier=1).then_inc(iota_ready, 1)
            pool.wait_ge(ident_ready, 1)
            pool.affine_select(out=ident[:], in_=ident[:], compare_op=ALU.not_equal, fill=1.0,
                               base=0, pattern=[[-1, P]], channel_multiplier=1).then_inc(ident_ready, 1)
            pool.wait_ge(bias_step, 2 + N_HEADS)
            pool.affine_select(out=bias[:], in_=bias[:], compare_op=ALU.is_ge, fill=NEG_INF * HEAD ** 0.5,
                               base=WINDOW + P, pattern=[[0, N_HEADS], [-1, KEYS]], channel_multiplier=1)\
                .then_inc(bias_ready, 1)
            pool.wait_ge(bias_ready, 1)
            pool.affine_select(out=bias[:], in_=bias[:], compare_op=ALU.is_ge, fill=NEG_INF * HEAD ** 0.5,
                               base=WINDOW - P, pattern=[[0, N_HEADS], [1, KEYS]], channel_multiplier=-1)\
                .then_inc(bias_ready, 1)
            with pool.Fori(0, TILES) as b:
                pool.wait_ge(out_ready, b + 1)
                pool.dma_start(out_rows[:, :, bass.ds(b * P, P)],
                               attn_t[:, bass.ds(b % 2, 1), :].rearrange("p a (b t) -> p (a b) t", t=P))\
                    .then_inc(stored, 16)
                pool.wait_ge(stored, b * 16 + 16)
                pool.sem_inc(out_free, 1)

        @block.tensor
        def _(pe):
            def turn_values(i, s, kind):
                lo, hi, part = keys_of(kind)
                pe.wait_ge(v_in[s], i * 16 + 16)
                pe.wait_ge(v_ready, i * 2 + s + 1)
                for j in range(lo, hi):
                    turn = pe.transpose(v_psum[:, j * P:(j + 1) * P], v_rows[:, s, j * P:(j + 1) * P], ident[:])
                turn.then_inc(v_turned, 1)

            def score(i, s, kind, h):
                lo, hi, part = keys_of(kind)
                if h == 0:
                    pe.wait_ge(q_in[s], i * 16 + 16)
                    pe.wait_ge(k_in[s], i * 16 + 16)
                pe.wait_ge(masked, i * (2 * N_HEADS) + (s * N_HEADS + h + 1))
                pe.matmul(s_psum[:, h % 2, part], q[:, s, h, :], k[:, s, h // group, part],
                          start=True, stop=True).then_inc(scores_done, 1)

            def turn_probs(i, s, kind, h):
                lo, hi, part = keys_of(kind)
                n = i * (2 * N_HEADS) + (s * N_HEADS + h)
                pe.wait_ge(exp_done, n + 3)
                pe.wait_ge(probs_t_ready, n + 1)
                for j in range(lo, hi):
                    turn = pe.transpose(p_psum[:, h % 2, j * P:(j + 1) * P], probs[:, h % 2, j * P:(j + 1) * P],
                                        ident[:])
                turn.then_inc(turned, 1)

            def weigh(i, s, kind, h):
                lo, hi, part = keys_of(kind)
                pe.wait_ge(probs_t_ready, i * (2 * N_HEADS) + (s * N_HEADS + h + 3))
                if h == 0:
                    pe.wait_ge(v_ready, i * 2 + s + 2)
                    pe.wait_ge(attn_ready, i * 2 + s + 1)
                g = h // group
                for j in range(lo, hi):
                    pv = pe.matmul(o_psum[:, s, h * HEAD:(h + 1) * HEAD], probs_t[:, h % 2, j * P:(j + 1) * P],
                                   v[:, s, j, g * HEAD:(g + 1) * HEAD], start=j == lo, stop=j == hi - 1)
                pv.then_inc(pv_done, 1)

            def turn_attn(i, s):
                b = i * 2 + s
                pe.wait_ge(attn_ready, b + 3)
                if not isinstance(b, int) or b:
                    pe.wait_ge(out_ready, b)
                for j in range(ATTN // P):
                    turn = pe.transpose(a_psum[:, j * P:(j + 1) * P],
                                        attn[:, 2 * j:2 * j + 2, :].rearrange("p h d -> p (h d)"), ident[:])
                turn.then_inc(attn_turned, 1)

            def attend(i, s, kind, following):
                later, before = (i + s, 1 - s), (i + (s - 1), 1 - s)
                for h in range(N_HEADS):
                    if h + 2 < N_HEADS:
                        score(i, s, kind, h + 2)
                    elif following:
                        score(*later, following, h + 2 - N_HEADS)
                    turn_probs(i, s, kind, h)
                    if h:
                        weigh(i, s, kind, h - 1)
                    elif kind != "first":
                        weigh(*before, "first" if isinstance(i, int) and i * 2 + s == 1 else "middle", N_HEADS - 1)
                    if h == 4 and kind != "first":
                        turn_attn(*before)
                    if h == N_HEADS - 2:
                        pe.wait_ge(scores_done, (i * 2 + s) * N_HEADS + N_HEADS)
                        pe.wait_ge(v_turned, i * 2 + s + 1)
                        pe.sem_inc(loaded_free, 1)
                        if following:
                            turn_values(*later, following)

            pe.sem_inc(loaded_free, 2)
            pe.sem_inc(turned, 2)
            pe.sem_inc(pv_done, 2)
            pe.wait_ge(ident_ready, 2)
            turn_values(0, 0, "first")
            score(0, 0, "first", 0)
            score(0, 0, "first", 1)
            over_blocks(pe, attend)
            weigh(TILES // 2 - 1, 1, "last", N_HEADS - 1)
            turn_attn(TILES // 2 - 1, 1)

        @block.vector
        def _(dve):
            def mask(i, s, kind, h):
                part = keys_of(kind)[2]
                n = i * (2 * N_HEADS) + (s * N_HEADS + h)
                dve.wait_ge(exp_done, n + 1)
                dve.wait_ge(scores_done, n + 1)
                dve.sem_inc(mask_started, 1)
                dve.tensor_tensor_reduce(neg_scores[:, h % 2, part], s_psum[:, h % 2, part], bias[:, h, part],
                                         -HEAD ** -0.5, neg_sinks[:, h:h + 1], ALU.add, ALU.min,
                                         neg_top[:, s, h:h + 1]).then_inc(masked, 1)

            def copy_turned(i, s, kind, h):
                part = keys_of(kind)[2]
                n = i * (2 * N_HEADS) + (s * N_HEADS + h)
                dve.wait_ge(turned, n + 3)
                dve.wait_ge(pv_done, n + 1)
                dve.tensor_copy(probs_t[:, h % 2, part], p_psum[:, h % 2, part]).then_inc(probs_t_ready, 1)

            def copy_values(i, s, kind):
                lo, hi, part = keys_of(kind)
                dve.wait_ge(v_turned, i * 2 + s + 1)
                dve.tensor_copy(v[:, s, lo:hi].rearrange("p a b -> p (a b)"), v_psum[:, part]).then_inc(v_ready, 1)

            def open_norm(i, s):
                dve.wait_ge(masked, (i * 2 + s) * N_HEADS + (N_HEADS + 2))
                dve.tensor_tensor(sink_gap[:], sinks[:], neg_top[:, s], ALU.add).then_inc(gap_ready, 1)

            def norm(i, s):
                b = i * 2 + s
                dve.wait_ge(sink_ready, b + 1)
                dve.tensor_tensor(total[:], sums[:, s], sink_exp[:], ALU.add).then_inc(share_step, 1)
                dve.wait_ge(share_step, b * 2 + 1)
                dve.reciprocal(share[:], total[:]).then_inc(share_step, 1)
                dve.wait_ge(share_step, b * 2 + 2)
                dve.wait_ge(pv_done, b * N_HEADS + (N_HEADS + 2))
                if not isinstance(b, int) or b:
                    dve.wait_ge(attn_turned, b)
                dve.tensor_tensor(attn[:], o_psum[:, s].rearrange("p (h d) -> p h d", d=HEAD),
                                  share[:].rearrange("p (h a) -> p h a", a=1).broadcast_to([P, N_HEADS, HEAD]),
                                  ALU.mult).then_inc(attn_ready, 1)

            def attend(i, s, kind, following):
                later, before = (i + s, 1 - s), (i + (s - 1), 1 - s)
                for h in range(N_HEADS):
                    if h + 1 < N_HEADS:
                        mask(i, s, kind, h + 1)
                    elif following:
                        mask(*later, following, 0)
                    copy_turned(i, s, kind, h)
                    if kind != "first":
                        if h == 0:
                            open_norm(*before)
                        if h == 2:
                            norm(*before)
                    if h == N_HEADS - 1 and following:
                        copy_values(*later, following)

            dve.wait_ge(iota_ready, 1)
            dve.tensor_copy(distance_f[:], distance[:]).then_inc(bias_step, 1)
            dve.wait_ge(bias_step, 1)
            dve.scalar_tensor_tensor(out=distance_f[:], in0=distance_f[:], scalar=-1.0, in1=distance_f[:],
                                     op0=ALU.mult, op1=ALU.max).then_inc(bias_step, 1)
            dve.wait_ge(bias_step, 2)
            for h in range(N_HEADS):
                slope = 2.0 ** (-8.0 * (h + 1) / N_HEADS)
                dve.tensor_scalar(bias[:, h, :], distance_f[:], -slope * HEAD ** 0.5, None, ALU.mult)\
                    .then_inc(bias_step, 1)
            dve.wait_ge(sinks_in, 16)
            dve.tensor_scalar(neg_sinks[:], sinks[:], -1.0, None, ALU.mult).then_inc(bias_step, 1)
            dve.wait_ge(bias_step, 3 + N_HEADS)
            dve.wait_ge(bias_ready, 2)
            dve.sem_inc(masked, 2)
            dve.sem_inc(probs_t_ready, 2)
            dve.sem_inc(v_ready, 1)
            dve.sem_inc(attn_ready, 2)
            copy_values(0, 0, "first")
            mask(0, 0, "first", 0)
            over_blocks(dve, attend)
            open_norm(TILES // 2 - 1, 1)
            norm(TILES // 2 - 1, 1)

        @block.scalar
        def _(act):
            def exponentials(i, s, kind, h):
                part = keys_of(kind)[2]
                n = i * (2 * N_HEADS) + (s * N_HEADS + h)
                act.wait_ge(masked, n + 3)
                act.wait_ge(turned, n + 1)
                act.activation(probs[:, h % 2, part], neg_scores[:, h % 2, part], ACT.Exp, scale=-1.0,
                               bias=neg_top[:, s, h:h + 1], accum_out=sums[:, s, h:h + 1]).then_inc(exp_done, 1)

            def sink_part(i, s):
                act.wait_ge(gap_ready, i * 2 + s + 1)
                act.activation(sink_exp[:], sink_gap[:], ACT.Exp).then_inc(sink_ready, 1)

            def copy_out(i, s):
                b = i * 2 + s
                act.wait_ge(attn_turned, b + 1)
                act.wait_ge(out_free, b + 1)
                act.activation(attn_t[:, s], a_psum[:], ACT.Copy).then_inc(out_ready, 1)

            def attend(i, s, kind, following):
                before = (i + (s - 1), 1 - s)
                for h in range(N_HEADS):
                    exponentials(i, s, kind, h)
                    if kind != "first":
                        if h == 1:
                            sink_part(*before)
                        if h == 5:
                            copy_out(*before)

            act.sem_inc(exp_done, 2)
            act.sem_inc(out_free, 2)
            over_blocks(act, attend)
            sink_part(TILES // 2 - 1, 1)
            copy_out(TILES // 2 - 1, 1)


class Steps:

    def __init__(self, engine, done):
        self.engine, self.done, self.count = engine, done, 0

    def __call__(self, instruction):
        instruction.then_inc(self.done, 1)
        self.count += 1
        self.engine.wait_ge(self.done, self.count)


def complex_product(step, engine, out, x, y, temp, negate_im=False):
    (out_re, out_im), (x_re, x_im), (y_re, y_im) = out, x, y
    step(engine.tensor_tensor(out_re, x_re, y_re, ALU.mult))
    step(engine.tensor_tensor(temp, x_im, y_im, ALU.mult))
    step(engine.tensor_tensor(out_re, out_re, temp, ALU.subtract))
    step(engine.tensor_tensor(out_im, x_re, y_im, ALU.mult))
    step(engine.tensor_tensor(temp, x_im, y_re, ALU.mult))
    step(engine.tensor_tensor(out_im, out_im, temp, ALU.add))


TWO_PI = 6.283185307179586
ROUND = 1.5 * 2.0 ** 23
LN2 = 0.6931471805599453


def head_bits(x, bits):
    import math
    mantissa, exponent = math.frexp(x)
    return math.ldexp(math.floor(mantissa * 2 ** bits), exponent - bits)


def reduce_argument(step, dve, out, x, turns, period):
    a = head_bits(period, 8)
    b = head_bits(period - a, 11)
    c = period - a - b
    step(dve.tensor_scalar(turns, x, 1.0 / period, None, ALU.mult))
    step(dve.tensor_scalar(turns, turns, ROUND, None, ALU.add))
    step(dve.tensor_scalar(turns, turns, -ROUND, None, ALU.add))
    step(dve.scalar_tensor_tensor(out=out, in0=turns, scalar=-a, in1=x, op0=ALU.mult, op1=ALU.add))
    step(dve.scalar_tensor_tensor(out=out, in0=turns, scalar=-b, in1=out, op0=ALU.mult, op1=ALU.add))
    step(dve.scalar_tensor_tensor(out=out, in0=turns, scalar=-c, in1=out, op0=ALU.mult, op1=ALU.add))


def horner(step, dve, out, x, coefficients):
    *rest, last = coefficients
    step(dve.tensor_scalar(out, x, last, rest[-1], ALU.mult, ALU.add))
    for c in reversed(rest[:-1]):
        step(dve.tensor_tensor(out, out, x, ALU.mult))
        step(dve.tensor_scalar(out, out, c, None, ALU.add))


QS = GROUPS // 2
LC = SSM_L * SSM_CH
SPAN = 2 * SSM_L - 1
POWERS = SSM_L + 1
SCAN_I = 16
SCAN_J = SSM_J // SCAN_I


def stage_ssm(nc, u_scratch, params, ssm_d, y_scratch):
    with ExitStack() as ctx:
        m = Pool(nc, ctx, "sm")
        outof = [[m.sb(f"outof{d}{r}", [P, QS, POWERS, SSM_CH]) for r in range(2)] for d in range(2)]
        into = m.sb("into", [P, 2, 2, QS, P])
        local = m.sb("local", [P, GROUPS, LC])
        leaps = [m.sb(f"leaps{d}", [P, 2, SCAN_I, QS]) for d in range(2)]
        with ExitStack() as first:
            ssm_tables(nc, Pool(nc, first, "st"), params, ssm_d, outof, into, local, leaps)
        with ExitStack() as second:
            ssm_run(nc, Pool(nc, second, "sr"), u_scratch, y_scratch, outof, into, local, leaps)


def ssm_tables(nc, m, params, ssm_d, outof, into, local, leaps):
    ident = m.sb("ident", [P, P])
    both = [P, 2, QS]
    lam_re, lam_im, log_dt = m.sb("lam_re", both), m.sb("lam_im", both), m.sb("log_dt", both)
    b_raw = m.sb("b_raw", [P, 2, 2, QS, SSM_CH])
    c_rows = m.sb("c_rows", [P, 2, 2, 4, 2 * SSM_N])
    c_t = m.sb("c_t", [P, 2, 2, QS, SSM_CH])
    d_rows = m.sb("d_rows", [SSM_CH, GROUPS, SSM_CH])
    d_diag = m.sb("d_diag", [SSM_CH, GROUPS, SSM_CH])
    names = "dt x em1 turns r scale half s c s2 c2 cosm1 a_re a_im am1_re den inv co_re co_im t0 t1".split()
    v = {n: m.sb(n, both) for n in names}
    scale_int = m.sb("scale_int", both, I32)
    bbar = m.sb("bbar", [P, 2, 2, QS, SSM_CH])
    bbar_temp = m.sb("bbar_temp", [P, QS, SSM_CH])
    rising = m.sb("rising", [P, 2, 2, POWERS, QS])
    falling = m.sb("falling", [P, 2, 2, POWERS, QS])
    power_temp = m.sb("power_temp", [P, SSM_L, QS])
    b_table = [[m.sb(f"b_table{d}{r}", [P, QS, SSM_L, SSM_CH]) for r in range(2)] for d in range(2)]
    temps = [m.sb(f"table_temp{d}", [P, QS, POWERS, SSM_CH]) for d in range(2)]
    kernels = m.sb("kernels", [SSM_CH, GROUPS, SPAN, SSM_CH])
    banks = m.psum("banks", [P, 8, BANK])
    lam_loaded = m.sem("lam_loaded")
    b_loaded = m.sem("b_loaded")
    c_loaded = m.sem("c_loaded")
    d_loaded = m.sem("d_loaded")
    ident_ready = m.sem("ident_ready")
    dt_ready = m.sem("dt_ready")
    c_turned = m.sem("c_turned")
    c_copied = m.sem("c_copied")
    dve_step = m.sem("dve_step")
    pool_step = m.sem("pool_step")
    bases_ready = m.sem("bases_ready")
    tables_ready = [m.sem("tables_ready0"), m.sem("tables_ready1")]
    kernels_done = m.sem("kernels_done")
    kernels_copied = m.sem("kernels_copied")
    kernels_ready = m.sem("kernels_ready")
    into_turned = m.sem("into_turned")
    into_copied = m.sem("into_copied")
    local_placed = m.sem("local_placed")
    PER_BANK = BANK // LC

    block = m.ctx.enter_context(nc.Block())

    @block.sync
    def _(sync):
        with nc.allow_non_contiguous_dma(reason="2048 values each, once"):
            for d in range(2):
                p_lam_re, p_lam_im, p_log_dt = params[d][:3]
                sync.dma_start(lam_re[:, d], p_lam_re.rearrange("(q e) n -> (e n) q", e=2)).then_inc(lam_loaded, 16)
                sync.dma_start(lam_im[:, d], p_lam_im.rearrange("(q e) n -> (e n) q", e=2)).then_inc(lam_loaded, 16)
                for e in range(2):
                    steps = p_log_dt.rearrange("(a q e) -> e a q", a=1, e=2)[e]
                    sync.dma_start(log_dt[e * SSM_N:(e + 1) * SSM_N, d], steps.broadcast_to([SSM_N, QS]))\
                        .then_inc(lam_loaded, 16)
            for d in range(2):
                for r in range(2):
                    sync.dma_start(b_raw[:, d, r], params[d][3 + r].rearrange("(q e) n c -> (e n) q c", e=2))\
                        .then_inc(b_loaded, 16)

    @block.scalar
    def _(act):
        for d in range(2):
            for r in range(2):
                rows = params[d][5 + r].rearrange("(w g) c n -> (g c) w n", w=4)
                for twice in range(2):
                    act.dma_start(c_rows[:, d, r, :, twice * SSM_N:(twice + 1) * SSM_N], rows).then_inc(c_loaded, 16)
        act.dma_start(d_rows[:].rearrange("p g c -> p (g c)"), row_broadcast(ssm_d, SSM_CH)).then_inc(d_loaded, 16)
        for d in range(2):
            for r in range(2):
                act.wait_ge(c_turned, d * 2 + r + 1)
                turned = banks[:, d * 2 + r, :].rearrange("p (q e c) -> p q e c", e=2, c=SSM_CH)
                for e in range(2):
                    half = slice(e * SSM_N, (e + 1) * SSM_N)
                    act.activation(c_t[half, d, r], turned[half, :, e], ACT.Copy).then_inc(c_copied, 1)
        for n in range(4):
            for b in range(4):
                act.wait_ge(into_turned, n * 4 + b + 1)
                d, r = n // 2, n % 2
                act.activation(into[:, d, r, b * 4:(b + 1) * 4].rearrange("p a b -> p (a b)"),
                               banks[:, 4 + b, :], ACT.Copy).then_inc(into_copied, 1)
        for l in range(SSM_L):
            if l == 0:
                act.wait_ge(kernels_ready, 1)
            act.dma_start(local[l * SSM_CH:(l + 1) * SSM_CH, :, :],
                          kernels[:, :, SSM_L - 1 - l:2 * SSM_L - 1 - l, :].rearrange("c g k o -> c g (k o)"))\
                .then_inc(local_placed, 16)
        act.wait_ge(local_placed, SSM_L * 16)

    def tables(engine, step, d):
        powers = (falling, 1) if d == 0 else (rising, 0)
        source, k0 = powers

        def power(table, k0, n, r):
            return table[:, d, r, k0:k0 + n, :].rearrange("p k (q a) -> p q k a", a=1)\
                .broadcast_to([P, QS, n, SSM_CH])

        def per_group(values, n):
            return values.rearrange("p q (a c) -> p q a c", a=1).broadcast_to([P, QS, n, SSM_CH])

        complex_product(step, engine, [b_table[d][0][:], b_table[d][1][:]],
                        [power(source, k0, SSM_L, r) for r in range(2)],
                        [per_group(bbar[:, d, r], SSM_L) for r in range(2)], temps[d][:, :, 0:SSM_L])
        engine.wait_ge(c_copied, 4 * (d + 1))
        source = rising if d == 0 else falling
        complex_product(step, engine, [outof[d][0][:], outof[d][1][:]],
                        [power(source, 0, POWERS, r) for r in range(2)],
                        [per_group(c_t[:, d, r], POWERS) for r in range(2)], temps[d][:])
        step(engine.tensor_scalar(outof[d][1][:], outof[d][1][:], -1.0, None, ALU.mult))
        engine.sem_inc(tables_ready[d], 1)

    @block.gpsimd
    def _(pool):
        step = Steps(pool, pool_step)
        step(pool.memset(ident[:], 0.0))
        step(pool.affine_select(out=ident[:], in_=ident[:], compare_op=ALU.not_equal, fill=1.0,
                                base=0, pattern=[[-1, P]], channel_multiplier=1))
        pool.sem_inc(ident_ready, 1)
        for r in range(2):
            step(pool.memset(rising[:, :, r, 0, :], 1.0 - r))
            step(pool.memset(falling[:, :, r, SSM_L, :], 1.0 - r))
        pool.sem_inc(ident_ready, 1)
        pool.wait_ge(d_loaded, 16)
        step(pool.tensor_tensor(d_diag[:], d_rows[:],
                                ident[0:SSM_CH, 0:SSM_CH].rearrange("p (a c) -> p a c", a=1)
                                .broadcast_to([SSM_CH, GROUPS, SSM_CH]), ALU.mult))
        pool.sem_inc(ident_ready, 1)
        pool.wait_ge(bases_ready, 1)
        tables(pool, step, 1)

    @block.vector
    def _(dve):
        step = Steps(dve, dve_step)
        op = {n: t[:] for n, t in v.items()}

        def tt(out, a, b, kind):
            step(dve.tensor_tensor(out, a, b, kind))

        def ts(out, a, x, kind, y=None, kind2=None):
            if y is None:
                step(dve.tensor_scalar(out, a, x, None, kind))
            else:
                step(dve.tensor_scalar(out, a, x, y, kind, kind2))

        def exp_minus_1(out, x):
            ts(op["x"], x, -87.0, ALU.max, 88.0, ALU.min)
            reduce_argument(step, dve, op["r"], op["x"], op["turns"], LN2)
            horner(step, dve, op["t0"], op["r"], [1 / 1, 1 / 2, 1 / 6, 1 / 24, 1 / 120, 1 / 720, 1 / 5040, 1 / 40320])
            tt(op["t0"], op["t0"], op["r"], ALU.mult)
            ts(op["t1"], op["turns"], 127.0, ALU.add)
            step(dve.tensor_copy(scale_int[:], op["t1"]))
            step(dve.tensor_scalar(scale_int[:], scale_int[:], 23, None, ALU.logical_shift_left))
            step(dve.tensor_copy(op["scale"], scale_int[:].bitcast(F32)))
            tt(op["t0"], op["t0"], op["scale"], ALU.mult)
            ts(op["scale"], op["scale"], -1.0, ALU.add)
            tt(out, op["t0"], op["scale"], ALU.add)

        dve.wait_ge(lam_loaded, 16 * 8)
        exp_minus_1(op["dt"], log_dt[:])
        step(dve.tensor_copy(op["scale"], scale_int[:].bitcast(F32)))
        tt(op["dt"], op["t0"], op["scale"], ALU.add)
        tt(op["half"], lam_re[:], op["dt"], ALU.mult)
        exp_minus_1(op["em1"], op["half"])
        tt(op["x"], lam_im[:], op["dt"], ALU.mult)
        reduce_argument(step, dve, op["r"], op["x"], op["turns"], TWO_PI)
        ts(op["r"], op["r"], 0.25, ALU.mult)
        tt(op["t0"], op["r"], op["r"], ALU.mult)
        horner(step, dve, op["s"], op["t0"], [1.0, -1 / 6, 1 / 120, -1 / 5040, 1 / 362880])
        tt(op["s"], op["s"], op["r"], ALU.mult)
        horner(step, dve, op["c"], op["t0"], [1.0, -1 / 2, 1 / 24, -1 / 720, 1 / 40320, -1 / 3628800])
        step(dve.scalar_tensor_tensor(out=op["s2"], in0=op["s"], scalar=2.0, in1=op["c"], op0=ALU.mult, op1=ALU.mult))
        step(dve.scalar_tensor_tensor(out=op["c2"], in0=op["s"], scalar=-2.0, in1=op["s"], op0=ALU.mult, op1=ALU.mult))
        ts(op["c2"], op["c2"], 1.0, ALU.add)
        step(dve.scalar_tensor_tensor(out=op["s"], in0=op["s2"], scalar=2.0, in1=op["c2"], op0=ALU.mult, op1=ALU.mult))
        step(dve.scalar_tensor_tensor(out=op["cosm1"], in0=op["s2"], scalar=-2.0, in1=op["s2"],
                                      op0=ALU.mult, op1=ALU.mult))
        ts(op["c"], op["cosm1"], 1.0, ALU.add)
        ts(op["t1"], op["em1"], 1.0, ALU.add)
        tt(op["a_re"], op["t1"], op["c"], ALU.mult)
        tt(op["a_im"], op["t1"], op["s"], ALU.mult)
        tt(op["am1_re"], op["em1"], op["c"], ALU.mult)
        tt(op["am1_re"], op["am1_re"], op["cosm1"], ALU.add)
        tt(op["den"], lam_re[:], lam_re[:], ALU.mult)
        tt(op["t0"], lam_im[:], lam_im[:], ALU.mult)
        tt(op["den"], op["den"], op["t0"], ALU.add)
        step(dve.reciprocal(op["inv"], op["den"]))
        tt(op["co_re"], op["am1_re"], lam_re[:], ALU.mult)
        tt(op["t0"], op["a_im"], lam_im[:], ALU.mult)
        tt(op["co_re"], op["co_re"], op["t0"], ALU.add)
        tt(op["co_re"], op["co_re"], op["inv"], ALU.mult)
        tt(op["co_im"], op["a_im"], lam_re[:], ALU.mult)
        tt(op["t0"], op["am1_re"], lam_im[:], ALU.mult)
        tt(op["co_im"], op["co_im"], op["t0"], ALU.subtract)
        tt(op["co_im"], op["co_im"], op["inv"], ALU.mult)
        dve.wait_ge(b_loaded, 16 * 4)
        for d in range(2):
            def over_channels(value):
                return value[:, d].rearrange("p (q a) -> p q a", a=1).broadcast_to([P, QS, SSM_CH])
            complex_product(step, dve, [bbar[:, d, r] for r in range(2)],
                            [over_channels(op["co_re"]), over_channels(op["co_im"])],
                            [b_raw[:, d, r] for r in range(2)], bbar_temp[:])
        dve.wait_ge(ident_ready, 2)
        for r, part in enumerate(("a_re", "a_im")):
            step(dve.tensor_copy(rising[:, :, r, 1, :], op[part]))
        for n in (1, 2, 4):
            for d in range(2):
                last = [rising[:, d, r, n:n + 1, :].broadcast_to([P, n, QS]) for r in range(2)]
                complex_product(step, dve, [rising[:, d, r, n + 1:2 * n + 1, :] for r in range(2)], last,
                                [rising[:, d, r, 1:n + 1, :] for r in range(2)], power_temp[:, 0:n])
        for k in range(SSM_L):
            step(dve.tensor_copy(falling[:, :, :, k, :], rising[:, :, :, SSM_L - k, :]))
        dve.sem_inc(bases_ready, 1)
        tables(dve, step, 0)
        for d in range(2):
            for r in range(2):
                step(dve.tensor_copy(leaps[d][:, r, 0, :], rising[:, d, r, SSM_L, :]))
            for n in (1, 2, 4, 8):
                last = [leaps[d][:, r, n - 1:n, :].broadcast_to([P, n, QS]) for r in range(2)]
                complex_product(step, dve, [leaps[d][:, r, n:2 * n, :] for r in range(2)], last,
                                [leaps[d][:, r, 0:n, :] for r in range(2)], power_temp[:, 0:n])
        copied = Steps(dve, kernels_copied)
        for d in range(2):
            for b in range(GROUPS // PER_BANK):
                dve.wait_ge(kernels_done, d * (GROUPS // PER_BANK) + b + 1)
                qs = slice(b // 2 * PER_BANK, (b // 2 + 1) * PER_BANK)
                mine = kernels[:].rearrange("c (q e) k o -> c e q k o", e=2)[:, b % 2, qs]
                found = banks[0:SSM_CH, b % 4, :].rearrange("c (g k o) -> c g k o", g=PER_BANK, o=SSM_CH)
                if d == 0:
                    copied(dve.tensor_copy(mine[:, :, SSM_L - 1:SPAN], found))
                else:
                    step(dve.tensor_tensor(mine[:, :, SSM_L - 1], mine[:, :, SSM_L - 1],
                                           found[:, :, SSM_L - 1], ALU.add))
                    copied(dve.tensor_copy(mine[:, :, 0:SSM_L - 1], found[:, :, 0:SSM_L - 1]))
        dve.wait_ge(ident_ready, 3)
        step(dve.tensor_tensor(kernels[:, :, SSM_L - 1], kernels[:, :, SSM_L - 1], d_diag[:], ALU.add))
        dve.sem_inc(kernels_ready, 1)

    @block.tensor
    def _(pe):
        pe.wait_ge(ident_ready, 1)
        pe.wait_ge(c_loaded, 16 * 8)
        for d in range(2):
            for r in range(2):
                for w in range(4):
                    turn = pe.transpose(banks[:, d * 2 + r, w * P:(w + 1) * P], c_rows[:, d, r, w], ident[:])
                turn.then_inc(c_turned, 1)
        for d in range(2):
            pe.wait_ge(tables_ready[d], 1)
            for r in range(2):
                for b in range(4):
                    n = (d * 2 + r) * 4 + b
                    if n >= 4:
                        pe.wait_ge(into_copied, n - 3)
                    for a in range(4):
                        turn = pe.transpose(banks[:, 4 + b, a * P:(a + 1) * P],
                                            b_table[d][r][:, b * 4 + a].rearrange("p l c -> p (l c)"), ident[:])
                    turn.then_inc(into_turned, 1)
            pe.wait_ge(c_copied, 8)
            k0 = 0 if d == 0 else 1
            bare = SSM_L - 1 if d == 0 else 0
            for b in range(GROUPS // PER_BANK):
                n = d * (GROUPS // PER_BANK) + b
                if n >= 4:
                    pe.wait_ge(kernels_copied, n - 3)
                for j in range(PER_BANK):
                    q, part = b // 2 * PER_BANK + j, slice(b % 2 * SSM_N, (b % 2 + 1) * SSM_N)
                    for r in range(2):
                        done = pe.matmul(banks[0:SSM_CH, b % 4, j * LC:(j + 1) * LC], b_table[d][r][part, q, bare],
                                         outof[d][r][part, q, k0:k0 + SSM_L].rearrange("p k c -> p (k c)"),
                                         start=r == 0, stop=r == 1)
                done.then_inc(kernels_done, 1)


def ssm_run(nc, m, u_scratch, y_scratch, outof, into, local, leaps):
    u = m.sb("u", [P, GROUPS, SSM_J])
    states = [m.sb(f"states{d}", [P, 2, QS, SSM_J + 1]) for d in range(2)]
    y = m.sb("y", [P, 2, 2, SSM_J])
    part_a = [m.sb(f"part_a{d}", [P, 2, QS, SCAN_J]) for d in range(2)]
    part_b = [m.sb(f"part_b{d}", [P, 2, QS, SCAN_J]) for d in range(2)]
    banks = m.psum("banks", [P, 8, BANK])
    u_in = m.sem("u_in")
    edge_zero = m.sem("edge_zero")
    into_done = m.sem("into_done")
    into_copied = m.sem("into_copied")
    scan_step = [m.sem("scan_step0"), m.sem("scan_step1")]
    scan_start = m.sem("scan_start")
    scanned = m.sem("scanned")
    y_done = m.sem("y_done")
    y_ready = m.sem("y_ready")
    y_free = m.sem("y_free")
    stored = m.sem("stored")
    u_chunks = u_scratch.rearrange("(g c) (l j) -> l c g j", c=SSM_CH, l=SSM_L)
    y_chunks = y_scratch.rearrange("(g c) (l j) -> l c g j", c=SSM_CH, l=SSM_L)
    block = m.ctx.enter_context(nc.Block())

    def scan(engine, d, on_pool):
        done = scan_step[d]
        PER_STEP = 5
        grid = states[d][:, :, :, 1 - d:1 - d + SSM_J].rearrange("p r q (j i) -> p r q j i", i=SCAN_I)

        def add_product(target, source, power, blocks, before):
            a, b = part_a[d][:, :, :, 0:blocks], part_b[d][:, :, :, 0:blocks]

            def factor(r):
                one = leaps[d][:, r, power, :].rearrange("p k (q b) -> p k q b", b=1)
                return one.broadcast_to([P, 2, QS, blocks])

            def ready(n):
                engine.wait_ge(done, before + n)
                if on_pool:
                    engine.sem_inc(scan_start, 1)

            ready(0)
            engine.tensor_tensor(a, source, factor(0), ALU.mult).then_inc(done, 1)
            engine.tensor_tensor(b, source, factor(1), ALU.mult).then_inc(done, 1)
            ready(2)
            engine.tensor_tensor(target, target, a, ALU.add).then_inc(done, 1)
            ready(3)
            engine.tensor_tensor(target[:, 0:1], target[:, 0:1], b[:, 1:2], ALU.subtract).then_inc(done, 1)
            engine.tensor_tensor(target[:, 1:2], target[:, 1:2], b[:, 0:1], ALU.add).then_inc(done, 1)

        with engine.Fori(0, SCAN_I - 1) as i:
            now, last = (i + 1, i) if d == 0 else (SCAN_I - 2 - i, SCAN_I - 1 - i)
            add_product(grid[:, :, :, :, bass.ds(now, 1)].rearrange("p r q j i -> p r q (j i)"),
                        grid[:, :, :, :, bass.ds(last, 1)].rearrange("p r q j i -> p r q (j i)"),
                        slice(0, 1), SCAN_J, i * PER_STEP + 1)
        end = SCAN_I - 1 if d == 0 else 0
        with engine.Fori(0, SCAN_J - 1) as i:
            now, last = (i + 1, i) if d == 0 else (SCAN_J - 2 - i, SCAN_J - 1 - i)
            add_product(grid[:, :, :, bass.ds(now, 1), end], grid[:, :, :, bass.ds(last, 1), end],
                        slice(SCAN_I - 1, SCAN_I), 1, i * PER_STEP + (PER_STEP * (SCAN_I - 1) + 1))
        targets, sources = (slice(1, SCAN_J), slice(0, SCAN_J - 1)) if d == 0 else (slice(0, SCAN_J - 1), slice(1, SCAN_J))
        with engine.Fori(0, SCAN_I - 1) as i:
            now = i if d == 0 else SCAN_I - 1 - i
            add_product(grid[:, :, :, targets, bass.ds(now, 1)].rearrange("p r q j i -> p r q (j i)"),
                        grid[:, :, :, sources, end],
                        bass.ds(i, 1), SCAN_J - 1, i * PER_STEP + (PER_STEP * (SCAN_I + SCAN_J - 2) + 1))
        engine.wait_ge(done, PER_STEP * (2 * SCAN_I + SCAN_J - 3) + 1)
        engine.sem_inc(scanned, 1)

    @block.sync
    def _(sync):
        for l in range(SSM_L):
            sync.dma_start(u[l * SSM_CH:(l + 1) * SSM_CH], u_chunks[l]).then_inc(u_in, 16)
        with sync.Fori(0, GROUPS // 4) as i:
            for s in range(2):
                sync.wait_ge(y_ready, i * 2 + s + 1)
                for l in range(SSM_L):
                    sync.dma_start(y_chunks[l, :, bass.ds((i * 2 + s) * 2, 2), :], y[l * SSM_CH:(l + 1) * SSM_CH, s])\
                        .then_inc(stored, 16)
                sync.wait_ge(stored, (i * 2 + s + 1) * (16 * SSM_L))
                sync.sem_inc(y_free, 1)

    @block.tensor
    def _(pe):
        pe.wait_ge(u_in, 16 * SSM_L)
        for q in range(QS):
            for d in range(2):
                n = q * 2 + d
                if n >= 8:
                    pe.wait_ge(into_copied, n - 7)
                for r in range(2):
                    for e in range(2):
                        half = slice(e * SSM_N, (e + 1) * SSM_N)
                        done = pe.matmul(banks[half, n % 8, r * SSM_J:(r + 1) * SSM_J], into[:, d, r, q, half],
                                         u[:, 2 * q + e, :], start=True, stop=True)
                done.then_inc(into_done, 1)
        pe.wait_ge(into_copied, 2 * QS)
        pe.wait_ge(scanned, 2)
        for q in range(QS):
            if q >= 4:
                pe.wait_ge(y_ready, q - 3)
            for e in range(2):
                half = slice(e * SSM_N, (e + 1) * SSM_N)
                bank = banks[:, q % 4 * 2 + e, 0:SSM_J]
                pe.matmul(bank, local[:, 2 * q + e, :], u[:, 2 * q + e, :], start=True, stop=False)
                for d in range(2):
                    for r in range(2):
                        done = pe.matmul(bank, outof[d][r][half, q, 1 - d:1 - d + SSM_L].rearrange("p k c -> p (k c)"),
                                         states[d][half, r, q, d:d + SSM_J],
                                         start=False, stop=d == 1 and r == 1)
            done.then_inc(y_done, 1)

    @block.scalar
    def _(act):
        act.wait_ge(edge_zero, 2)
        for n in range(2 * QS):
            q, d = n // 2, n % 2
            act.wait_ge(into_done, n + 1)
            act.activation(states[d][:, :, q, 1 - d:1 - d + SSM_J],
                           banks[:, n % 8, :].rearrange("p (r j) -> p r j", r=2), ACT.Copy).then_inc(into_copied, 1)
        for q in range(QS):
            act.wait_ge(y_done, q + 1)
            act.wait_ge(y_free, q + 1)
            act.activation(y[:, q % 2], banks[:, q % 4 * 2:q % 4 * 2 + 2, 0:SSM_J], ACT.Gelu_apprx_tanh)\
                .then_inc(y_ready, 1)

    @block.vector
    def _(dve):
        dve.memset(states[0][:, :, :, 0:1], 0.0).then_inc(edge_zero, 1)
        dve.sem_inc(scan_step[0], 1)
        dve.wait_ge(into_copied, 2 * QS)
        scan(dve, 0, False)

    @block.gpsimd
    def _(pool):
        pool.memset(states[1][:, :, :, SSM_J:SSM_J + 1], 0.0).then_inc(edge_zero, 1)
        pool.sem_inc(scan_step[1], 1)
        pool.sem_inc(y_free, 2)
        pool.wait_ge(into_copied, 2 * QS)
        scan(pool, 1, True)


LAM_NAMES = ("lam_re", "lam_im", "log_dt", "b_re", "b_im", "c_re", "c_im")


def hybrid_layer(nc, t):
    def scratch(name, shape):
        return nc.dram_tensor(name, shape, F32, kind="Internal").ap()

    qkv = scratch("qkv", (ATTN + 2 * KV, TOK))
    u = scratch("u", (SSM, TOK))
    gates = scratch("gates", (2 * D, TOK))
    attn = scratch("attn", (ATTN, TOK))
    y = scratch("y_ssm", (SSM, TOK))
    merged = scratch("merged", (D, TOK))
    x_mid = scratch("x_mid", (TOK, D))
    f = scratch("f", (FF, TOK))
    params = [[t[f"{name}_{direction}"] for name in LAM_NAMES] for direction in "fb"]

    stage_project_in(nc, t["x"], t["norm_mix_pre"], t["w_in"], qkv, u, gates)
    stage_ssm(nc, u, params, t["ssm_d"], y)
    stage_attention(nc, qkv, t["attn_sink"], attn)
    stage_branches(nc, attn, y, gates, t["w_glu"], t["b_glu"], t["w_branch_attn"], t["w_branch_ssm"], merged)
    stage_out(nc, merged, t["w_out"], t["norm_mix_post"], t["x"], x_mid)
    stage_gate_up(nc, x_mid, t["norm_ffn_pre"], t["w_ffn_gate"], t["w_ffn_up"], t["conv_w"], t["conv_b"], f)
    stage_down(nc, f, t["w_ffn_down"], t["norm_ffn_post"], x_mid, t["out"])


def kernel(**inputs):
    import numpy as np
    from concourse import bacc
    from concourse.bass_utils import run_bass_kernel_spmd

    nc = bacc.Bacc("TRN2", target_bir_lowering=False, num_devices=1)
    arrays, tensors = {}, {}
    for name, value in inputs.items():
        array = np.ascontiguousarray(value)
        arrays[f"in_{name}"] = array
        handle = nc.dram_tensor(f"in_{name}", array.shape, mybir.dt.from_np(array.dtype), kind="ExternalInput").ap()
        tensors[name] = handle[0]
    out = nc.dram_tensor("out", (1, TOK, D), F32, kind="ExternalOutput").ap()
    tensors["out"] = out[0]
    hybrid_layer(nc, tensors)
    result = run_bass_kernel_spmd(nc, [arrays], core_ids=[0])
    return result.results[0]["out"]
```

```python
import math
from contextlib import ExitStack

import concourse.bass as bass
import concourse.mybir as mybir

F32 = mybir.dt.float32
F32R = mybir.dt.float32r
BF16 = mybir.dt.bfloat16
I32 = mybir.dt.int32
ALU = mybir.AluOpType
ACT = mybir.ActivationFunctionType
AX_X = mybir.AxisListType.X

P = 128
TOK = 2048
D = 1024
KD = D // P
N_HEADS, N_KV, HEAD = 8, 2, 64
ATTN = N_HEADS * HEAD
KV = N_KV * HEAD
WINDOW = 128
SSM, SSM_CH, SSM_N = 512, 16, 64
GROUPS = SSM // SSM_CH
FF = 2816
KF = FF // P
EPS = 1e-6
NEG_INF = -1e30
BANK = 512
TILES = TOK // P
CHUNKS = TOK // BANK
WARM_UP = 112

SSM_L = 8
SSM_J = TOK // SSM_L


class Pool:

    def __init__(self, nc, ctx, tag):
        self.nc, self.ctx, self.tag = nc, ctx, tag
        self.handles = []
        self.lowest = min(nc.free_semaphores)
        ctx.callback(self.zero)

    def zero(self):
        if self.handles:
            self.nc.all_engine_barrier(sems_to_clear=range(self.lowest, self.lowest + len(self.handles)))
            for handle in self.handles:
                self.nc.release_semaphore(handle)

    def sb(self, name, shape, dt=F32):
        return self.ctx.enter_context(self.nc.sbuf_tensor(f"{self.tag}_{name}", shape, dt))

    def psum(self, name, shape, dt=F32):
        return self.ctx.enter_context(self.nc.psum_tensor(f"{self.tag}_{name}", shape, dt))

    def sem(self, name):
        self.handles.append(self.nc.alloc_semaphore(f"{self.tag}_{name}", self.lowest + len(self.handles)))
        return self.handles[-1]

    def pool_dma_sem(self, name):
        return self.nc.alloc_semaphore(f"{self.tag}_{name}", max(self.nc.free_semaphores))


def carve(region, shapes):
    views, used = {}, 0
    for name, (partitions, sizes) in shapes.items():
        axes = "abcde"[:len(sizes)]
        views[name] = region[0:partitions, used:used + math.prod(sizes)].rearrange(
            f"p ({' '.join(axes)}) -> p {' '.join(axes)}", **dict(zip(axes, sizes)))
        used += math.prod(sizes)
    return views


def row_broadcast(vector, n=P):
    return vector.rearrange("(a d) -> a d", a=1).broadcast_to([n, vector.shape[0]])


RING = BANK // P


def over_tiles(engine, step, ahead=None, after_first=None):
    last = TILES // RING - 1
    if ahead:
        ahead(0, 0)
    if after_first:
        for s in range(RING):
            if ahead:
                ahead((s + 1) // RING, (s + 1) % RING)
            step(0, s)
        after_first()
    with engine.Fori(1 if after_first else 0, last) as i:
        for s in range(RING):
            if ahead:
                ahead(i + (s + 1) // RING, (s + 1) % RING)
            step(i, s)
    for s in range(RING):
        if ahead and s + 1 < RING:
            ahead(last, s + 1)
        step(last, s)


def rms_constants(pool, consts, ready):
    for n, value in enumerate((1.0 / D, EPS, -0.5)):
        pool.memset(consts[:, n:n + 1], value).then_inc(ready, 1)


class NormTranspose:

    def __init__(self, m, src, gain, rows=None):
        self.src, self.gain = src, gain
        self.feat_hi = m.sb("feat_hi", [P, KD, TOK], F32R)
        self.feat_lo = m.sb("feat_lo", [P, KD, TOK], F32R)
        self.rows = rows or m.sb("rows", [P, RING, D])
        self.normed = m.sb("normed", [P, 2, D])
        self.squares = m.sb("squares", [P, D], BF16)
        self.gain_rows = m.sb("gain_rows", [P, D])
        self.ident = m.sb("ident", [P, P])
        self.consts = m.sb("consts", [P, 3])
        self.stat = m.sb("stat", [P, RING, 4])
        self.rows_in = [m.sem(f"rows_in{s}") for s in range(RING)]
        self.gain_in = m.sem("gain_in")
        self.const_ready = m.sem("const_ready")
        self.square_sum = m.sem("square_sum")
        self.mean_square = m.sem("mean_square")
        self.rstd = m.sem("rstd")
        self.normed_ready = m.sem("normed_ready")
        self.turned = m.sem("turned")
        self.hi_ready = m.sem("hi_ready")
        self.lo_ready = m.sem("lo_ready")

    def load(self, sync, ws, first_weights):
        def load_tile(i, s):
            t = i * RING + s
            sync.wait_ge(self.normed_ready, t + 1)
            sync.dma_start(self.rows[:, s, :], self.src[bass.ds(t * P, P), :]).then_inc(self.rows_in[s], 16)
            if isinstance(i, int) and t == 0:
                sync.dma_start(self.gain_rows[:], row_broadcast(self.gain)).then_inc(self.gain_in, 16)

        load_tile(0, 0)
        for s in range(1, RING):
            load_tile(0, s)
        for s, weights, columns in first_weights:
            ws.load(sync, weights, s, 0, s, columns)
        with sync.Fori(1, TILES // RING) as i:
            for s in range(RING):
                load_tile(i, s)

    def gpsimd(self, pool):
        pool.memset(self.ident[:], 0.0).then_inc(self.const_ready, 1)
        rms_constants(pool, self.consts, self.const_ready)
        pool.wait_ge(self.const_ready, 4)
        pool.affine_select(out=self.ident[:], in_=self.ident[:], compare_op=ALU.not_equal, fill=1.0,
                           base=0, pattern=[[-1, P]], channel_multiplier=1).then_inc(self.const_ready, 1)

        def inverse_root(i, s):
            t = i * RING + s
            stat = self.stat
            pool.wait_ge(self.square_sum, t + 2)
            pool.tensor_tensor(stat[:, s, 1:2], stat[:, s, 0:1], self.consts[:, 0:1], ALU.mult)\
                .then_inc(self.mean_square, 1)
            pool.wait_ge(self.mean_square, t * 2 + 1)
            pool.tensor_tensor(stat[:, s, 2:3], stat[:, s, 1:2], self.consts[:, 1:2], ALU.add)\
                .then_inc(self.mean_square, 1)
            pool.wait_ge(self.mean_square, t * 2 + 2)
            pool.tensor_tensor(stat[:, s, 3:4], stat[:, s, 2:3], self.consts[:, 2:3], ALU.pow)\
                .then_inc(self.rstd, 1)

        over_tiles(pool, inverse_root)

    def scalar(self, act, psum):
        def square(i, s):
            t = i * RING + s
            act.wait_ge(self.square_sum, t + 1)
            act.wait_ge(self.rows_in[s], i * 16 + 16)
            act.wait_ge(self.normed_ready, t + 1)
            act.activation(self.squares[:], self.rows[:, s, :], ACT.Square,
                           accum_out=self.stat[:, s, 0:1]).then_inc(self.square_sum, 1)

        def keep_hi(i, s):
            t = i * RING + s
            act.wait_ge(self.turned, t + 3)
            act.activation(self.feat_hi[:, :, bass.ds(t * P, P)], psum[:, s % 2, :, :], ACT.Copy)\
                .then_inc(self.hi_ready, 1)

        act.sem_inc(self.square_sum, 1)
        over_tiles(act, keep_hi, square)

    def vector(self, dve, psum, ws):
        def norm(i, s):
            t = i * RING + s
            dve.wait_ge(self.rstd, t + 1)
            dve.wait_ge(self.turned, t + 1)
            dve.scalar_tensor_tensor(out=self.normed[:, s % 2, :], in0=self.rows[:, s, :],
                                     scalar=self.stat[:, s, 3:4], in1=self.gain_rows[:],
                                     op0=ALU.mult, op1=ALU.mult).then_inc(self.normed_ready, 1)

        def keep_lo(i, s):
            t = i * RING + s
            dve.wait_ge(self.hi_ready, t + 1)
            cols = bass.ds(t * P, P)
            dve.tensor_tensor(self.feat_lo[:, :, cols], psum[:, s % 2, :, :],
                              self.feat_hi[:, :, cols].bitcast(F32), ALU.subtract).then_inc(self.lo_ready, 1)

        dve.sem_inc(self.normed_ready, RING)
        dve.sem_inc(self.lo_ready, 2)
        dve.sem_inc(ws.raw_free, 2)
        dve.wait_ge(self.gain_in, 16)
        over_tiles(dve, keep_lo, norm, lambda: ws.vector(dve, 0, 0, 0))
        ws.vector(dve, 1, 0, 1)

    def tensor(self, pe, psum, banks, ws):
        def turn_tile(i, s):
            t = i * RING + s
            pe.wait_ge(self.normed_ready, t + (RING + 1))
            pe.wait_ge(self.lo_ready, t + 1)
            for k in range(KD):
                turn = pe.transpose(psum[:, s % 2, k, :], self.normed[:, s % 2, k * P:(k + 1) * P], self.ident[:])
            turn.then_inc(self.turned, 1)

        def quarter(i, s):
            cols = bass.ds(i * BANK, BANK)
            for k in range(s * KD // RING, (s + 1) * KD // RING):
                last = split_products(pe, banks[:, bass.ds(i, 1), :], ws.hi[:, 0, k], ws.lo[:, 0, k],
                                      self.feat_hi[:, k, cols], self.feat_lo[:, k, cols], k == 0, k == KD - 1)
            if s == RING - 1:
                last.then_inc(ws.chunk_done, 1)

        pe.sem_inc(self.turned, 2)
        ws.start(pe)
        pe.wait_ge(self.const_ready, 5)
        for s in range(RING):
            turn_tile(0, s)
        with pe.Fori(1, TILES // RING) as i:
            pe.wait_ge(ws.lo_ready, 1)
            pe.wait_ge(self.lo_ready, i * RING + 2)
            for s in range(RING):
                turn_tile(i, s)
                quarter(i - 1, s)
        pe.wait_ge(self.lo_ready, TILES + 2)
        for s in range(RING):
            quarter(TILES // RING - 1, s)


class WeightStream:

    def __init__(self, m, k):
        self.k = k
        self.raw = m.sb("w_raw", [P, 2, k, P])
        self.hi = m.sb("w_hi", [P, 2, k, P], F32R)
        self.lo = m.sb("w_lo", [P, 2, k, P], F32R)
        self.raw_in = [m.sem("w_raw_in0"), m.sem("w_raw_in1")]
        self.raw_free = m.sem("w_raw_free")
        self.hi_ready = m.sem("w_hi_ready")
        self.lo_ready = m.sem("w_lo_ready")
        self.chunk_done = m.sem("w_chunk_done")

    def load(self, sync, weights, s, uses, n, columns):
        sync.wait_ge(self.raw_free, n + 1)
        sync.dma_start(self.raw[:, s], weights.rearrange("(k p) n -> p k n", p=P)[:, :, columns])\
            .then_inc(self.raw_in[s], 16)

    def start(self, pe):
        pe.sem_inc(self.chunk_done, 2 * CHUNKS)

    def wait_chunk(self, engine, n, c):
        engine.wait_ge(self.chunk_done, n * CHUNKS + (2 * CHUNKS + c + 1))

    def vector(self, dve, s, uses, n):
        dve.wait_ge(self.raw_in[s], uses * 16 + 16)
        dve.wait_ge(self.chunk_done, n * CHUNKS + CHUNKS)
        dve.tensor_copy(self.hi[:, s], self.raw[:, s]).then_inc(self.hi_ready, 1)
        dve.wait_ge(self.hi_ready, n + 1)
        dve.tensor_tensor(self.lo[:, s], self.raw[:, s], self.hi[:, s].bitcast(F32), ALU.subtract)\
            .then_inc(self.lo_ready, 1)
        dve.wait_ge(self.lo_ready, n + 1)
        dve.sem_inc(self.raw_free, 1)


def split_products(pe, out, w_hi, w_lo, x_hi, x_lo, first, last):
    pe.matmul(out, w_hi, x_hi, start=first, stop=False)
    pe.matmul(out, w_lo, x_hi, start=False, stop=False)
    return pe.matmul(out, w_hi, x_lo, start=False, stop=last)


def stage_project_in(nc, x, gain, w_in, qkv, u_scratch, gate_scratch, bases):
    with ExitStack() as ctx:
        m = Pool(nc, ctx, "pi")
        nt = NormTranspose(m, x, gain, bases.memory[:].rearrange("p (s d) -> p s d", s=RING))
        bases.enter(m, nt.normed[:].rearrange("p s d -> p (s d)"))
        ws = WeightStream(m, KD)
        rows_out = m.sb("rows_out", [P, 2, TOK])
        banks = m.psum("banks", [P, 8, BANK])
        turn_psum = banks[:, 4:8, :].rearrange("p (s b) (k t) -> p s (b k) t", s=2, t=P)
        chunk_free = m.sem("chunk_free")
        out_ready = m.sem("out_ready")
        stored = [m.sem("stored0"), m.sem("stored1")]
        n_qkv, n_u, n_gate = qkv.shape[0] // P, SSM // P, 2 * D // P
        parts = [(0, n_qkv, qkv, "plain"), (n_qkv, n_u, u_scratch, "by chunk"),
                 (n_qkv + n_u, n_gate, gate_scratch, "sigmoid")]
        n_blocks = n_qkv + n_u + n_gate
        block = ctx.enter_context(nc.Block())

        @block.gpsimd
        def _(pool):
            nt.gpsimd(pool)
            pool.wait_ge(nt.normed_ready, TILES + RING)
            bases.compute(pool)

        @block.sync
        def _(sync):
            nt.load(sync, ws, [(s, w_in, slice(s * P, (s + 1) * P)) for s in range(2)])
            sync.wait_ge(nt.turned, TILES + 2)
            bases.load(nc, sync)
            with sync.Fori(1, n_blocks // 2) as i:
                for s in range(2):
                    ws.load(sync, w_in, s, i, i * 2 + s, bass.ds((i * 2 + s) * P, P))

        @block.vector
        def _(dve):
            nt.vector(dve, turn_psum, ws)
            bases.invert(dve)
            with dve.Fori(1, n_blocks // 2) as i:
                for s in range(2):
                    ws.vector(dve, s, i, i * 2 + s)

        @block.tensor
        def _(pe):
            def product(i, s):
                b = i * 2 + s
                pe.wait_ge(ws.lo_ready, b + 1)
                for c in range(CHUNKS):
                    pe.wait_ge(chunk_free, b * CHUNKS + c + 1)
                    for k in range(KD):
                        cols = slice(c * BANK, (c + 1) * BANK)
                        last = split_products(pe, banks[:, s * CHUNKS + c, :], ws.hi[:, s, k], ws.lo[:, s, k],
                                              nt.feat_hi[:, k, cols], nt.feat_lo[:, k, cols],
                                              k == 0, k == KD - 1)
                    last.then_inc(ws.chunk_done, 1)

            nt.tensor(pe, turn_psum, banks, ws)
            product(0, 1)
            with pe.Fori(1, n_blocks // 2) as i:
                for s in range(2):
                    product(i, s)

        @block.scalar
        def _(act):
            nt.scalar(act, turn_psum)
            act.sem_inc(chunk_free, 2 * CHUNKS)
            for s in range(2):
                act.sem_inc(stored[s], 16)
            for first, count, dest, kind in parts:
                dest_rows = dest.rearrange("(b p) t -> b p t", p=P)
                with act.Fori(0, count // 2) as i:
                    for s in range(2):
                        b = i * 2 + s
                        uses = i + first // 2
                        act.wait_ge(stored[s], uses * 16 + 16)
                        for c in range(CHUNKS):
                            ws.wait_chunk(act, b + first, c)
                            if kind == "by chunk":
                                out = rows_out[:, s, :].rearrange("p (l j) -> p j l", l=SSM_L)
                                n = BANK // SSM_L
                                out = out[:, c * n:(c + 1) * n, :]
                                src = banks[:, s * CHUNKS + c, :].rearrange("p (j l) -> p j l", l=SSM_L)
                            else:
                                out = rows_out[:, s, c * BANK:(c + 1) * BANK]
                                src = banks[:, s * CHUNKS + c, :]
                            func = ACT.Sigmoid if kind == "sigmoid" else ACT.Copy
                            act.activation(out, src, func).then_inc(chunk_free, 1)
                        act.wait_ge(chunk_free, (b + first) * CHUNKS + 3 * CHUNKS)
                        act.dma_start(dest_rows[b], rows_out[:, s, :]).then_inc(stored[s], 16)
            for s in range(2):
                act.wait_ge(stored[s], (n_blocks // 2) * 16 + 16)


def stage_gate_up(nc, x_mid, gain, w_gate, w_up, conv_w, conv_b, f_scratch):
    with ExitStack() as ctx:
        m = Pool(nc, ctx, "gu")
        nt = NormTranspose(m, x_mid, gain)
        ws = WeightStream(m, KD)
        gate = m.sb("gate", [P, TOK + 2])
        conv = m.sb("conv", [P, TOK])
        taps = m.sb("taps", [P, 4, KF])
        banks = m.psum("banks", [P, 8, BANK])
        turn_psum = banks[:, 4:8, :].rearrange("p (s b) (k t) -> p s (b k) t", s=2, t=P)
        taps_in = m.sem("taps_in")
        edges_zero = m.sem("edges_zero")
        gate_read = m.sem("gate_read")
        up_read = m.sem("up_read")
        gate_free = m.sem("gate_free")
        tap = m.sem("tap")
        gelu_done = m.sem("gelu_done")
        stored = m.pool_dma_sem("stored")
        conv_free = m.sem("conv_free")
        f_rows = f_scratch.rearrange("(b p) t -> b p t", p=P)
        block = ctx.enter_context(nc.Block())

        @block.gpsimd
        def _(pool):
            pool.memset(gate[:, 0:1], 0.0).then_inc(edges_zero, 1)
            pool.memset(gate[:, TOK + 1:TOK + 2], 0.0).then_inc(edges_zero, 1)
            nt.gpsimd(pool)

        @block.sync
        def _(sync):
            nt.load(sync, ws, [(s, weights, slice(0, P)) for s, weights in enumerate((w_gate, w_up))])
            with sync.Fori(1, KF) as i:
                ws.load(sync, w_gate, 0, i, i * 2, bass.ds(i * P, P))
                ws.load(sync, w_up, 1, i, i * 2 + 1, bass.ds(i * P, P))

        @block.tensor
        def _(pe):
            def product(i, s):
                pe.wait_ge(ws.lo_ready, i * 2 + s + 1)
                for c in range(CHUNKS):
                    pe.wait_ge(up_read if s else gate_read, i * CHUNKS + c + 1)
                    for k in range(KD):
                        cols = slice(c * BANK, (c + 1) * BANK)
                        last = split_products(pe, banks[:, s * CHUNKS + c, :], ws.hi[:, s, k], ws.lo[:, s, k],
                                              nt.feat_hi[:, k, cols], nt.feat_lo[:, k, cols],
                                              k == 0, k == KD - 1)
                    last.then_inc(ws.chunk_done, 1)

            nt.tensor(pe, turn_psum, banks, ws)
            product(0, 1)
            with pe.Fori(1, KF) as i:
                for s in range(2):
                    product(i, s)

        @block.scalar
        def _(act):
            with nc.allow_non_contiguous_dma(reason="small"):
                for j in range(3):
                    act.dma_start(taps[:, j, :], conv_w[j].rearrange("(b p) -> p b", p=P)).then_inc(taps_in, 16)
                act.dma_start(taps[:, 3, :], conv_b.rearrange("(b p) -> p b", p=P)).then_inc(taps_in, 16)
            nt.scalar(act, turn_psum)
            act.sem_inc(gate_read, CHUNKS)
            act.sem_inc(gelu_done, 1)
            act.wait_ge(taps_in, 64)
            with act.Fori(0, KF) as i:
                act.wait_ge(gate_free, i + 1)
                for c in range(CHUNKS):
                    ws.wait_chunk(act, i * 2, c)
                    act.activation(gate[:, 1 + c * BANK:1 + (c + 1) * BANK], banks[:, c, :], ACT.Copy)\
                        .then_inc(gate_read, 1)
                act.wait_ge(tap, i * 3 + 3)
                act.activation(conv[:], conv[:], ACT.Gelu_apprx_tanh, bias=taps[:, 3, bass.ds(i, 1)]).then_inc(gelu_done, 1)

        @block.vector
        def _(dve):
            nt.vector(dve, turn_psum, ws)
            dve.sem_inc(gate_free, 1)
            dve.sem_inc(up_read, CHUNKS)
            dve.wait_ge(taps_in, 64)
            dve.wait_ge(edges_zero, 2)
            dve.sem_inc(conv_free, 1)

            def finish(i):
                dve.wait_ge(gate_read, i * CHUNKS + 2 * CHUNKS)
                dve.wait_ge(conv_free, i + 1)
                dve.tensor_scalar(conv[:], gate[:, 0:TOK], taps[:, 0, bass.ds(i, 1)], None,
                                  ALU.mult).then_inc(tap, 1)
                dve.wait_ge(tap, i * 3 + 1)
                dve.scalar_tensor_tensor(out=conv[:], in0=gate[:, 1:TOK + 1], scalar=taps[:, 1, bass.ds(i, 1)],
                                         in1=conv[:], op0=ALU.mult, op1=ALU.add).then_inc(tap, 1)
                dve.wait_ge(tap, i * 3 + 2)
                dve.scalar_tensor_tensor(out=conv[:], in0=gate[:, 2:TOK + 2], scalar=taps[:, 2, bass.ds(i, 1)],
                                         in1=conv[:], op0=ALU.mult, op1=ALU.add).then_inc(tap, 1)

            def times_up(i):
                dve.wait_ge(gelu_done, i + 2)
                for c in range(CHUNKS):
                    cols = slice(c * BANK, (c + 1) * BANK)
                    ws.wait_chunk(dve, i * 2 + 1, c)
                    dve.tensor_tensor(conv[:, cols], conv[:, cols], banks[:, CHUNKS + c, :], ALU.mult)\
                        .then_inc(up_read, 1)

            with dve.Fori(0, KF - 1) as i:
                ws.vector(dve, 0, i + 1, i * 2 + 2)
                finish(i)
                dve.wait_ge(tap, i * 3 + 3)
                dve.sem_inc(gate_free, 1)
                ws.vector(dve, 1, i + 1, i * 2 + 3)
                times_up(i)
            finish(KF - 1)
            times_up(KF - 1)

        @block.gpsimd
        def _(pool):
            with pool.Fori(0, KF) as i:
                pool.wait_ge(up_read, i * CHUNKS + 2 * CHUNKS)
                pool.dma_start(f_rows[i], conv[:]).then_inc(stored, 16)
                pool.wait_ge(stored, i * 16 + 16)
                pool.sem_inc(conv_free, 1)


class PostNorm:

    def __init__(self, m, residual, gain, out):
        self.residual = residual.rearrange("(t p) d -> t p d", p=P)
        self.out = out.rearrange("(t p) d -> t p d", p=P)
        self.gain = gain
        self.gain_rows = m.sb("gain_rows", [P, 2, BANK])
        self.rows = m.sb("rows", [P, 2, 2, BANK])
        self.scaled = m.sb("scaled", [P, 2, BANK])
        self.stat = m.sb("stat", [P, 2, 6])
        self.consts = m.sb("consts", [P, 3])
        self.gain_in = m.sem("gain_in")
        self.rows_in = [m.sem("rows_in0"), m.sem("rows_in1")]
        self.square_sum = m.sem("square_sum")
        self.mean_square = m.sem("mean_square")
        self.const_ready = m.sem("const_ready")
        self.rstd = m.sem("rstd")
        self.scaled_ready = m.sem("scaled_ready")
        self.sum_ready = m.sem("sum_ready")
        self.stored = m.pool_dma_sem("stored")
        self.rows_free = m.sem("rows_free")

    def load_gain(self, sync):
        sync.dma_start(self.gain_rows[:].rearrange("p a b -> p (a b)"), row_broadcast(self.gain))\
            .then_inc(self.gain_in, 16)
        sync.sem_inc(self.rows_free, 2)

    def load(self, sync, t, s, uses):
        sync.wait_ge(self.rows_free, t + 1)
        sync.dma_start(self.rows[:, s].rearrange("p a b -> p (a b)"), self.residual[t]).then_inc(self.rows_in[s], 16)

    def scalar(self, act, t, s, halves):
        act.wait_ge(self.sum_ready, t + 1)
        for h in range(2):
            act.activation(self.scaled[:, h, :], halves[h], ACT.Square,
                           accum_out=self.stat[:, s, h:h + 1]).then_inc(self.square_sum, 1)

    def inverse_root(self, pool, t, s):
        stat = self.stat
        pool.wait_ge(self.square_sum, t * 2 + 2)
        pool.tensor_tensor(stat[:, s, 2:3], stat[:, s, 0:1], stat[:, s, 1:2], ALU.add).then_inc(self.mean_square, 1)
        pool.wait_ge(self.mean_square, t * 3 + 1)
        pool.tensor_tensor(stat[:, s, 3:4], stat[:, s, 2:3], self.consts[:, 0:1], ALU.mult)\
            .then_inc(self.mean_square, 1)
        pool.wait_ge(self.mean_square, t * 3 + 2)
        pool.tensor_tensor(stat[:, s, 4:5], stat[:, s, 3:4], self.consts[:, 1:2], ALU.add)\
            .then_inc(self.mean_square, 1)
        pool.wait_ge(self.mean_square, t * 3 + 3)
        pool.tensor_tensor(stat[:, s, 5:6], stat[:, s, 4:5], self.consts[:, 2:3], ALU.pow).then_inc(self.rstd, 1)

    def gpsimd_start(self, pool):
        rms_constants(pool, self.consts, self.const_ready)
        pool.wait_ge(self.const_ready, 3)

    def vector(self, dve, t, s, uses, halves):
        dve.wait_ge(self.rstd, t + 1)
        for h in range(2):
            dve.scalar_tensor_tensor(out=self.scaled[:, h, :], in0=halves[h], scalar=self.stat[:, s, 5:6],
                                     in1=self.gain_rows[:, h, :], op0=ALU.mult, op1=ALU.mult)\
                .then_inc(self.scaled_ready, 1)
        dve.wait_ge(self.scaled_ready, t * 2 + 2)
        dve.wait_ge(self.rows_in[s], uses * 16 + 16)
        dve.tensor_tensor(self.rows[:, s], self.rows[:, s], self.scaled[:], ALU.add).then_inc(self.sum_ready, 1)

    def vector_start(self, dve):
        dve.wait_ge(self.gain_in, 16)
        dve.sem_inc(self.sum_ready, 1)

    def store(self, pool, t, s):
        pool.wait_ge(self.sum_ready, t + 2)
        pool.dma_start(self.out[t], self.rows[:, s].rearrange("p a b -> p (a b)")).then_inc(self.stored, 16)
        pool.wait_ge(self.stored, t * 16 + 16)
        pool.sem_inc(self.rows_free, 1)


def stage_down(nc, f_scratch, w_down, gain, x_mid, out):
    with ExitStack() as ctx:
        m = Pool(nc, ctx, "dn")
        pn = PostNorm(m, x_mid, gain, out)
        KH = KF // 2
        PAIRS = KF // 2
        RAW = 4
        w_raw = m.sb("w_raw", [P, RAW, 2, BANK])
        w_hi = m.sb("w_hi", [P, KF, BANK], F32R)
        w_lo = m.sb("w_lo", [P, KF, BANK], F32R)
        f_raw = m.sb("f_raw", [P, 2, KH, P])
        f_hi = m.sb("f_hi", [P, 2, KF, P], F32R)
        f_lo = m.sb("f_lo", [P, 2, KF, P], F32R)
        y_first = m.sb("y_first", [P, TILES, BANK])
        y = m.psum("y", [P, 2, BANK])
        w_in = [m.pool_dma_sem(f"w_in{s}") for s in range(RAW)]
        w_hi_ready = m.sem("w_hi_ready")
        w_lo_ready = m.sem("w_lo_ready")
        f_in = [m.sem(f"f_in{h}") for h in range(2)]
        f_hi_ready = m.sem("f_hi_ready")
        f_lo_ready = m.sem("f_lo_ready")
        y_done = m.sem("y_done")
        y_copied = m.sem("y_copied")
        y_free = m.sem("y_free")
        w_used = m.sem("w_used")
        f_tiles = f_scratch.rearrange("(h k p) (t c) -> t h p k c", p=P, h=2, c=P)
        w_pairs = w_down.rearrange("(a k p) (h n) -> h a p k n", k=2, p=P, h=2)
        block = ctx.enter_context(nc.Block())


        @block.sync
        def _(sync):
            def load_tile(half, t):
                for h in range(2):
                    sync.wait_ge(f_lo_ready, t * 2 + (half * TILES * 2 + h + 1))
                    sync.dma_start(f_raw[:, h], f_tiles[t, h]).then_inc(f_in[h], 16)

            load_tile(0, 0)
            pn.load_gain(sync)
            with sync.Fori(1, TILES) as t:
                load_tile(0, t)
            load_tile(1, 0)
            load_tile(1, 1)
            with sync.Fori(1, TILES // 2) as i:
                for s in range(2):
                    load_tile(1, i * 2 + s)
                    pn.load(sync, i * 2 + (s - 2), s, i - 1)
            for s in range(2):
                pn.load(sync, TILES - 2 + s, s, TILES // 2 - 1)

        @block.gpsimd
        def _(pool):
            for g in range(2 * PAIRS):
                if g >= RAW:
                    pool.wait_ge(w_lo_ready, g - RAW + 1)
                pool.dma_start(w_raw[:, g % RAW], w_pairs[g // PAIRS, g % PAIRS]).then_inc(w_in[g % RAW], 16)
            pn.gpsimd_start(pool)
            with pool.Fori(0, TILES // 2) as i:
                for s in range(2):
                    pn.inverse_root(pool, i * 2 + s, s)
                    pn.store(pool, i * 2 + s, s)

        @block.tensor
        def _(pe):
            def tile(i, s, half, first=False, last=False):
                n = i * 2 + (half * TILES + s)
                pe.wait_ge(y_free, n + 1)
                for k in range(KF):
                    if k % KH == 0:
                        pe.wait_ge(f_lo_ready, n * 2 + (k // KH + 3))
                    if first and k % 2 == 0:
                        pe.wait_ge(w_lo_ready, half * PAIRS + k // 2 + 1)
                    done = split_products(pe, y[:, s], f_hi[:, s, k], f_lo[:, s, k],
                                          w_hi[:, k], w_lo[:, k], k == 0, k == KF - 1)
                    if last and k % 2 and k < KF - 1:
                        done.then_inc(w_used, 1)
                done.then_inc(y_done, 1)

            for half in range(2):
                tile(0, 0, half, first=True)
                tile(0, 1, half)
                with pe.Fori(1, TILES // 2 - 1) as i:
                    for s in range(2):
                        tile(i, s, half)
                tile(TILES // 2 - 1, 0, half)
                tile(TILES // 2 - 1, 1, half, last=half == 0)

        @block.scalar
        def _(act):
            def split_hi(i, s, halves=range(2)):
                n = i * 2 + s
                for h in halves:
                    act.wait_ge(y_done, n + 1)
                    act.wait_ge(f_in[h], n * 16 + 16)
                    act.activation(f_hi[:, s, h * KH:(h + 1) * KH], f_raw[:, h], ACT.Copy)\
                        .then_inc(f_hi_ready, 1)

            def split_weights_hi(half, pairs):
                for a in pairs:
                    g = half * PAIRS + a
                    act.wait_ge(w_in[g % RAW], g // RAW * 16 + 16)
                    if half and a < PAIRS - 1:
                        act.wait_ge(w_used, a + 1)
                    elif half:
                        act.wait_ge(y_done, TILES + 2)
                    act.activation(w_hi[:, 2 * a:2 * a + 2], w_raw[:, g % RAW], ACT.Copy).then_inc(w_hi_ready, 1)

            def norm(i, s):
                t = i * 2 + s
                act.wait_ge(y_done, t + (TILES + 3))
                pn.scalar(act, t, s, [y_first[:, bass.ds(t, 1), :], y[:, s]])

            act.sem_inc(y_done, 2)
            split_hi(0, 0, [0])
            split_weights_hi(0, range(0, 2))
            split_hi(0, 0, [1])
            split_weights_hi(0, range(2, PAIRS))
            split_hi(0, 1)
            with act.Fori(1, TILES // 2) as i:
                for s in range(2):
                    split_hi(i, s)
            split_hi(TILES // 2, 0)
            split_weights_hi(1, range(PAIRS))
            split_hi(TILES // 2, 1)
            with act.Fori(0, TILES // 2 - 1) as i:
                for s in range(2):
                    norm(i, s)
                    split_hi(i + (TILES // 2 + 1), s)
            for s in range(2):
                norm(TILES // 2 - 1, s)

        @block.vector
        def _(dve):
            def split_lo(i, s, halves=range(2)):
                n = i * 2 + s
                for h in halves:
                    dve.wait_ge(f_hi_ready, n * 2 + h + 1)
                    part = slice(h * KH, (h + 1) * KH)
                    dve.tensor_tensor(f_lo[:, s, part], f_raw[:, h], f_hi[:, s, part].bitcast(F32),
                                      ALU.subtract).then_inc(f_lo_ready, 1)

            def split_weights_lo(half, pairs):
                for a in pairs:
                    g = half * PAIRS + a
                    dve.wait_ge(w_hi_ready, g + 1)
                    dve.tensor_tensor(w_lo[:, 2 * a:2 * a + 2], w_raw[:, g % RAW],
                                      w_hi[:, 2 * a:2 * a + 2].bitcast(F32), ALU.subtract).then_inc(w_lo_ready, 1)

            def keep(i, s):
                t = i * 2 + s
                dve.wait_ge(y_done, t + 3)
                dve.tensor_copy(y_first[:, bass.ds(t, 1), :], y[:, s:s + 1]).then_inc(y_copied, 1)
                dve.wait_ge(y_copied, t + 1)
                dve.sem_inc(y_free, 1)

            def finish(i, s):
                t = i * 2 + s
                pn.vector(dve, t, s, i, [y_first[:, bass.ds(t, 1), :], y[:, s]])
                dve.sem_inc(y_free, 1)

            dve.sem_inc(f_lo_ready, 2)
            dve.sem_inc(y_free, 2)
            split_lo(0, 0, [0])
            split_weights_lo(0, range(0, 2))
            split_lo(0, 0, [1])
            split_weights_lo(0, range(2, PAIRS))
            split_lo(0, 1)
            pn.vector_start(dve)
            with dve.Fori(0, TILES // 2 - 1) as i:
                for s in range(2):
                    keep(i, s)
                    split_lo(i + 1, s)
            keep(TILES // 2 - 1, 0)
            split_lo(TILES // 2, 0)
            split_weights_lo(1, range(PAIRS))
            keep(TILES // 2 - 1, 1)
            split_lo(TILES // 2, 1)
            with dve.Fori(0, TILES // 2 - 1) as i:
                for s in range(2):
                    finish(i, s)
                    split_lo(i + (TILES // 2 + 1), s)
            for s in range(2):
                finish(TILES // 2 - 1, s)


def stage_branches(nc, attn_scratch, y_scratch, gate_scratch, w_glu, b_glu, w_attn, w_ssm, merged_scratch):
    with ExitStack() as ctx:
        m = Pool(nc, ctx, "br")
        K = SSM // P
        ws = WeightStream(m, K)
        attn_hi = m.sb("attn_hi", [P, K, TOK], F32R)
        attn_lo = m.sb("attn_lo", [P, K, TOK], F32R)
        y = m.sb("y", [P, K, TOK])
        y_hi = m.sb("y_hi", [P, K, TOK], F32R)
        y_lo = m.sb("y_lo", [P, K, TOK], F32R)
        rows = m.sb("rows", [P, 4, TOK])
        bias = m.sb("bias", [P, K])
        banks = m.psum("banks", [P, 8, BANK])
        bias_in = m.sem("bias_in")
        y_in = [m.sem(f"y_in{k}") for k in range(K)]
        rows_in = [m.sem(f"rows_in{k}") for k in range(4)]
        hi_ready = m.sem("hi_ready")
        lo_ready = m.sem("lo_ready")
        sigmoid_ready = m.sem("sigmoid_ready")
        glu_done = m.sem("glu_done")
        chunk_free = m.sem("chunk_free")
        gated = m.sem("gated")
        merged_ready = m.sem("merged_ready")
        stored = m.sem("stored")
        rows_free = m.sem("rows_free")
        gates_in = [[m.pool_dma_sem(f"gates_in{s}{h}") for h in range(2)] for s in range(2)]
        gates = gate_scratch.rearrange("(h b p) t -> h b p t", h=2, p=P)
        merged_rows = merged_scratch.rearrange("(b p) t -> b p t", p=P)
        n_out = D // P
        by_token = "p (j l) -> p l j"
        by_chunk = "p (l j) -> p l j"
        block = ctx.enter_context(nc.Block())

        @block.sync
        def _(sync):
            with nc.allow_non_contiguous_dma(reason="512 bias values"):
                sync.dma_start(bias[:], b_glu.rearrange("(k p) -> p k", p=P)).then_inc(bias_in, 16)
            for k in range(K):
                sync.dma_start(y[:, k], y_scratch[k * P:(k + 1) * P, :]).then_inc(y_in[k], 16)
            for k in range(K):
                sync.dma_start(rows[:, k], attn_scratch[k * P:(k + 1) * P, :]).then_inc(rows_in[k], 16)
            with sync.Fori(0, K // 2) as i:
                for s in range(2):
                    ws.load(sync, w_glu, s, i, i * 2 + s, bass.ds((i * 2 + s) * P, P))
            with sync.Fori(0, n_out) as i:
                ws.load(sync, w_attn, 0, i + K // 2, i * 2 + K, bass.ds(i * P, P))
                ws.load(sync, w_ssm, 1, i + K // 2, i * 2 + K + 1, bass.ds(i * P, P))

        @block.gpsimd
        def _(pool):
            pool.wait_ge(lo_ready, 2 * K)
            with pool.Fori(0, n_out // 2) as i:
                for s in range(2):
                    pool.wait_ge(rows_free, i * 2 + s + 1)
                    for h in range(2):
                        pool.dma_start(rows[:, 2 * s + h], gates[h, i * 2 + s]).then_inc(gates_in[s][h], 16)

        @block.tensor
        def _(pe):
            ws.start(pe)

            def product(b, s, x_hi, x_lo):
                pe.wait_ge(ws.lo_ready, b + 1)
                for c in range(CHUNKS):
                    pe.wait_ge(chunk_free, b * CHUNKS + c + 1)
                    for k in range(K):
                        cols = slice(c * BANK, (c + 1) * BANK)
                        last = split_products(pe, banks[:, s * CHUNKS + c, :], ws.hi[:, s, k], ws.lo[:, s, k],
                                              x_hi[:, k, cols], x_lo[:, k, cols], k == 0, k == K - 1)
                    last.then_inc(ws.chunk_done, 1)

            pe.wait_ge(lo_ready, K)
            with pe.Fori(0, K // 2) as i:
                for s in range(2):
                    product(i * 2 + s, s, y_hi, y_lo)
            pe.wait_ge(lo_ready, 2 * K)
            product(K, 0, attn_hi, attn_lo)
            pe.wait_ge(lo_ready, 3 * K)
            product(K + 1, 1, y_hi, y_lo)
            with pe.Fori(1, n_out) as i:
                product(i * 2 + K, 0, attn_hi, attn_lo)
                product(i * 2 + K + 1, 1, y_hi, y_lo)

        @block.scalar
        def _(act):
            act.wait_ge(bias_in, 16)
            for k in range(K):
                act.wait_ge(y_in[k], 16)
                act.activation(y_hi[:, k], y[:, k], ACT.Copy).then_inc(hi_ready, 1)
            for k in range(K):
                act.wait_ge(rows_in[k], 16)
                act.activation(attn_hi[:, k], rows[:, k], ACT.Copy).then_inc(hi_ready, 1)
            for b in range(K):
                for c in range(CHUNKS):
                    ws.wait_chunk(act, b, c)
                    bank = banks[:, b % 2 * CHUNKS + c, :]
                    act.activation(bank, bank, ACT.Sigmoid, bias=bias[:, b:b + 1]).then_inc(sigmoid_ready, 1)
            for k in range(K):
                act.wait_ge(glu_done, K * CHUNKS)
                act.activation(y_hi[:, k].rearrange(by_token, l=SSM_L), y[:, k].rearrange(by_chunk, l=SSM_L),
                               ACT.Copy).then_inc(hi_ready, 1)
            with act.Fori(0, n_out // 2) as i:
                for s in range(2):
                    n = i * 2 + s
                    act.wait_ge(merged_ready, n + 1)
                    act.dma_start(merged_rows[n], rows[:, 2 * s]).then_inc(stored, 16)
                    act.wait_ge(stored, n * 16 + 16)
                    act.sem_inc(rows_free, 1)

        @block.vector
        def _(dve):
            dve.sem_inc(ws.raw_free, 2)
            dve.sem_inc(chunk_free, 2 * CHUNKS)
            dve.sem_inc(rows_free, 2)
            for k in range(K):
                dve.wait_ge(hi_ready, k + 1)
                dve.tensor_tensor(y_lo[:, k], y[:, k], y_hi[:, k].bitcast(F32), ALU.subtract).then_inc(lo_ready, 1)
            for s in range(2):
                ws.vector(dve, s, 0, s)
            for k in range(K):
                dve.wait_ge(hi_ready, K + k + 1)
                dve.tensor_tensor(attn_lo[:, k], rows[:, k], attn_hi[:, k].bitcast(F32), ALU.subtract)\
                    .then_inc(lo_ready, 1)
            for b in range(K):
                for c in range(CHUNKS):
                    dve.wait_ge(sigmoid_ready, b * CHUNKS + c + 1)
                    cols = slice(c * BANK, (c + 1) * BANK)
                    dve.tensor_tensor(y[:, b, cols], y[:, b, cols], banks[:, b % 2 * CHUNKS + c, :], ALU.mult)\
                        .then_inc(glu_done, 1)
                    dve.wait_ge(glu_done, b * CHUNKS + c + 1)
                    dve.sem_inc(chunk_free, 1)
                ws.vector(dve, b % 2, b // 2 + 1, b + 2)
            for k in range(K):
                dve.wait_ge(hi_ready, 2 * K + k + 1)
                dve.tensor_tensor(y_lo[:, k].rearrange(by_token, l=SSM_L), y[:, k].rearrange(by_chunk, l=SSM_L),
                                  y_hi[:, k].bitcast(F32).rearrange(by_token, l=SSM_L), ALU.subtract)\
                    .then_inc(lo_ready, 1)

            def merge(i, s, last=False):
                n = i * 2 + s
                for h in range(2):
                    dve.wait_ge(gates_in[s][h], i * 16 + 16)
                    for c in range(CHUNKS):
                        ws.wait_chunk(dve, n * 2 + (K + h), c)
                        cols = slice(c * BANK, (c + 1) * BANK)
                        dve.tensor_tensor(rows[:, 2 * s + h, cols], rows[:, 2 * s + h, cols],
                                          banks[:, h * CHUNKS + c, :], ALU.mult).then_inc(gated, 1)
                        dve.wait_ge(gated, n * (2 * CHUNKS) + (h * CHUNKS + c + 1))
                        dve.sem_inc(chunk_free, 1)
                    if not last:
                        ws.vector(dve, h, n + (K // 2 + 1), n * 2 + (K + 2 + h))
                dve.tensor_tensor(rows[:, 2 * s], rows[:, 2 * s], rows[:, 2 * s + 1], ALU.add)\
                    .then_inc(merged_ready, 1)

            with dve.Fori(0, n_out // 2 - 1) as i:
                for s in range(2):
                    merge(i, s)
            merge(n_out // 2 - 1, 0)
            merge(n_out // 2 - 1, 1, last=True)


def stage_out(nc, merged_scratch, w_out, gain, x, x_mid):
    with ExitStack() as ctx:
        m = Pool(nc, ctx, "ou")
        pn = PostNorm(m, x, gain, x_mid)
        w_raw = m.sb("w_raw", [P, 2, D])
        w_hi = m.sb("w_hi", [P, KD, D], F32R)
        w_lo = m.sb("w_lo", [P, KD, D], F32R)
        g_raw = m.sb("g_raw", [P, 2, KD, P])
        g_hi = m.sb("g_hi", [P, 2, KD, P], F32R)
        g_lo = m.sb("g_lo", [P, 2, KD, P], F32R)
        y = m.psum("y", [P, 2, 2, BANK])
        w_in = [m.pool_dma_sem("w_in0"), m.pool_dma_sem("w_in1")]
        w_hi_ready = m.sem("w_hi_ready")
        w_lo_ready = m.sem("w_lo_ready")
        g_in = [m.sem("g_in0"), m.sem("g_in1")]
        g_hi_ready = m.sem("g_hi_ready")
        g_lo_ready = m.sem("g_lo_ready")
        y_done = m.sem("y_done")
        y_free = m.sem("y_free")
        g_tiles = merged_scratch.rearrange("(k p) (t c) -> t p k c", p=P, c=P)
        w_rows = w_out.rearrange("(k p) n -> k p n", p=P)
        block = ctx.enter_context(nc.Block())

        @block.sync
        def _(sync):
            def load_tile(t, s):
                sync.wait_ge(g_lo_ready, t + 1)
                sync.dma_start(g_raw[:, s], g_tiles[t]).then_inc(g_in[s], 16)

            for s in range(2):
                load_tile(s, s)
            pn.load_gain(sync)
            with sync.Fori(1, TILES // 2) as i:
                for s in range(2):
                    load_tile(i * 2 + s, s)
                    pn.load(sync, i * 2 + (s - 2), s, i - 1)
            for s in range(2):
                pn.load(sync, TILES - 2 + s, s, TILES // 2 - 1)

        @block.gpsimd
        def _(pool):
            pn.gpsimd_start(pool)
            with pool.Fori(0, KD // 2) as i:
                for s in range(2):
                    pool.wait_ge(w_lo_ready, i * 2 + s + 1)
                    pool.dma_start(w_raw[:, s], w_rows[i * 2 + s]).then_inc(w_in[s], 16)
            with pool.Fori(0, TILES // 2) as i:
                for s in range(2):
                    pn.inverse_root(pool, i * 2 + s, s)
                    pn.store(pool, i * 2 + s, s)

        @block.tensor
        def _(pe):
            def tile(i, s, first=False):
                t = i * 2 + s
                pe.wait_ge(g_lo_ready, t + 3)
                pe.wait_ge(y_free, t + 1)
                for k in range(KD):
                    if first:
                        pe.wait_ge(w_lo_ready, k + 3)
                    for h in range(2):
                        cols = slice(h * BANK, (h + 1) * BANK)
                        done = split_products(pe, y[:, s, h], g_hi[:, s, k], g_lo[:, s, k],
                                              w_hi[:, k, cols], w_lo[:, k, cols], k == 0, k == KD - 1)
                done.then_inc(y_done, 1)

            pe.sem_inc(y_done, 2)
            tile(0, 0, first=True)
            tile(0, 1)
            with pe.Fori(1, TILES // 2) as i:
                for s in range(2):
                    tile(i, s)

        @block.scalar
        def _(act):
            def split_hi(i, s):
                act.wait_ge(y_done, i * 2 + s + 1)
                act.wait_ge(g_in[s], i * 16 + 16)
                act.activation(g_hi[:, s], g_raw[:, s], ACT.Copy).then_inc(g_hi_ready, 1)

            def norm(i, s):
                t = i * 2 + s
                act.wait_ge(y_done, t + 3)
                pn.scalar(act, t, s, [y[:, s, 0], y[:, s, 1]])

            for s in range(2):
                split_hi(0, s)
            with act.Fori(0, TILES // 2 - 1) as i:
                for s in range(2):
                    norm(i, s)
                    split_hi(i + 1, s)
            for s in range(2):
                norm(TILES // 2 - 1, s)

        @block.vector
        def _(dve):
            def split_lo(i, s):
                dve.wait_ge(g_hi_ready, i * 2 + s + 1)
                dve.tensor_tensor(g_lo[:, s], g_raw[:, s], g_hi[:, s].bitcast(F32), ALU.subtract)\
                    .then_inc(g_lo_ready, 1)

            def finish(i, s):
                pn.vector(dve, i * 2 + s, s, i, [y[:, s, 0], y[:, s, 1]])
                dve.sem_inc(y_free, 1)

            dve.sem_inc(g_lo_ready, 2)
            dve.sem_inc(w_lo_ready, 2)
            dve.sem_inc(y_free, 2)
            for s in range(2):
                split_lo(0, s)
            with dve.Fori(0, KD // 2) as i:
                for s in range(2):
                    k = i * 2 + s
                    dve.wait_ge(w_in[s], i * 16 + 16)
                    dve.tensor_copy(w_hi[:, bass.ds(k, 1)], w_raw[:, s:s + 1]).then_inc(w_hi_ready, 1)
                    dve.wait_ge(w_hi_ready, k + 1)
                    dve.tensor_tensor(w_lo[:, bass.ds(k, 1)], w_raw[:, s:s + 1],
                                      w_hi[:, bass.ds(k, 1)].bitcast(F32), ALU.subtract)\
                        .then_inc(w_lo_ready, 1)
            pn.vector_start(dve)
            with dve.Fori(0, TILES // 2 - 1) as i:
                for s in range(2):
                    finish(i, s)
                    split_lo(i + 1, s)
            for s in range(2):
                finish(TILES // 2 - 1, s)


class Steps:

    def __init__(self, engine, done):
        self.engine, self.done, self.count = engine, done, 0

    def __call__(self, instruction):
        instruction.then_inc(self.done, 1)
        self.count += 1
        self.engine.wait_ge(self.done, self.count)


def complex_product(step, engine, out, x, y, temp, conjugate=False):
    (out_re, out_im), (x_re, x_im), (y_re, y_im) = out, x, y
    step(engine.tensor_tensor(out_re, x_re, y_re, ALU.mult))
    step(engine.tensor_tensor(temp, x_im, y_im, ALU.mult))
    step(engine.tensor_tensor(out_re, out_re, temp, ALU.add if conjugate else ALU.subtract))
    step(engine.tensor_tensor(out_im, x_re, y_im, ALU.mult))
    step(engine.tensor_tensor(temp, x_im, y_re, ALU.mult))
    step(engine.tensor_tensor(out_im, out_im, temp, ALU.subtract if conjugate else ALU.add))


TWO_PI = 6.283185307179586
ROUND = 1.5 * 2.0 ** 23
LN2 = 0.6931471805599453


def head_bits(x, bits):
    mantissa, exponent = math.frexp(x)
    return math.ldexp(math.floor(mantissa * 2 ** bits), exponent - bits)


def scaled_product(step, engine, out, x, scale, y, temp, kind=ALU.mult):
    step(engine.tensor_scalar(temp, x, scale, None, ALU.mult))
    step(engine.tensor_tensor(out, temp, y, kind))


def reduce_argument(step, engine, out, x, turns, period, temp):
    a = head_bits(period, 8)
    b = head_bits(period - a, 11)
    c = period - a - b
    step(engine.tensor_scalar(turns, x, 1.0 / period, None, ALU.mult))
    step(engine.tensor_scalar(turns, turns, ROUND, None, ALU.add))
    step(engine.tensor_scalar(turns, turns, -ROUND, None, ALU.add))
    scaled_product(step, engine, out, turns, -a, x, temp, ALU.add)
    scaled_product(step, engine, out, turns, -b, out, temp, ALU.add)
    scaled_product(step, engine, out, turns, -c, out, temp, ALU.add)


def horner(step, dve, out, x, coefficients):
    *rest, last = coefficients
    step(dve.tensor_scalar(out, x, last, rest[-1], ALU.mult, ALU.add))
    for c in reversed(rest[:-1]):
        step(dve.tensor_tensor(out, out, x, ALU.mult))
        step(dve.tensor_scalar(out, out, c, None, ALU.add))


QS = GROUPS // 2
LC = SSM_L * SSM_CH
SPAN = 2 * SSM_L - 1
POWERS = SSM_L + 1
SCAN_I = 16
SCAN_J = SSM_J // SCAN_I


class SsmBases:

    def __init__(self, params, memory):
        self.params, self.memory = params, memory
        v = carve(memory, {
            "bbar": (P, (2, 2, QS, SSM_CH)),
            "rising": (P, (2, 2, POWERS, QS)), "falling": (P, (2, 2, POWERS, QS)),
            "leaps": (P, (2, 2, SCAN_I, QS)),
            "bbar_temp": (P, (QS, SSM_CH)), "power_temp": (P, (SSM_L, QS))})
        self.bbar, self.rising, self.falling = v["bbar"], v["rising"], v["falling"]
        self.leaps = [v["leaps"][:, d] for d in range(2)]
        self.bbar_temp, self.power_temp = v["bbar_temp"], v["power_temp"]

    def enter(self, m, temp):
        names = ("lam_re lam_im log_dt dt x em1 turns r scale scale_bits half s c s2 c2 cosm1 a_re a_im am1_re "
                 "den inv co_re co_im t0 t1").split()
        self.op = carve(temp, {**{n: (P, (2, QS)) for n in names}, "b_raw": (P, (2, 2, QS, SSM_CH))})
        self.lam_loaded = m.sem("lam_loaded")
        self.b_loaded = m.sem("b_loaded")
        self.den_ready = m.sem("den_ready")
        self.inv_ready = m.sem("inv_ready")
        self.steps = m.sem("bases_step")

    def load(self, nc, sync):
        op, params = self.op, self.params
        with nc.allow_non_contiguous_dma(reason="2048 values each, once"):
            for d in range(2):
                p_lam_re, p_lam_im, p_log_dt = params[d][:3]
                sync.dma_start(op["lam_re"][:, d], p_lam_re.rearrange("(q e) n -> (e n) q", e=2))\
                    .then_inc(self.lam_loaded, 16)
                sync.dma_start(op["lam_im"][:, d], p_lam_im.rearrange("(q e) n -> (e n) q", e=2))\
                    .then_inc(self.lam_loaded, 16)
                for e in range(2):
                    steps = p_log_dt.rearrange("(a q e) -> e a q", a=1, e=2)[e]
                    sync.dma_start(op["log_dt"][e * SSM_N:(e + 1) * SSM_N, d], steps.broadcast_to([SSM_N, QS]))\
                        .then_inc(self.lam_loaded, 16)
            for d in range(2):
                for r in range(2):
                    sync.dma_start(op["b_raw"][:, d, r], params[d][3 + r].rearrange("(q e) n c -> (e n) q c", e=2))\
                        .then_inc(self.b_loaded, 16)

    def invert(self, dve):
        dve.wait_ge(self.den_ready, 1)
        dve.reciprocal(self.op["inv"], self.op["den"]).then_inc(self.inv_ready, 1)

    def compute(self, engine):
        step = Steps(engine, self.steps)
        op, bbar, rising, falling, leaps = self.op, self.bbar, self.rising, self.falling, self.leaps
        lam_re, lam_im, log_dt, b_raw = op["lam_re"], op["lam_im"], op["log_dt"], op["b_raw"]
        bbar_temp, power_temp = self.bbar_temp, self.power_temp
        scale_int = op["scale_bits"].bitcast(I32)
        for r in range(2):
            step(engine.memset(rising[:, :, r, 0, :], 1.0 - r))
            step(engine.memset(falling[:, :, r, SSM_L, :], 1.0 - r))


        def tt(out, a, b, kind):
            step(engine.tensor_tensor(out, a, b, kind))

        def ts(out, a, x, kind, y=None, kind2=None):
            if y is None:
                step(engine.tensor_scalar(out, a, x, None, kind))
            else:
                step(engine.tensor_scalar(out, a, x, y, kind, kind2))

        def exp_minus_1(out, x):
            ts(op["x"], x, -87.0, ALU.max, 88.0, ALU.min)
            reduce_argument(step, engine, op["r"], op["x"], op["turns"], LN2, op["t1"])
            horner(step, engine, op["t0"], op["r"], [1 / 1, 1 / 2, 1 / 6, 1 / 24, 1 / 120, 1 / 720, 1 / 5040, 1 / 40320])
            tt(op["t0"], op["t0"], op["r"], ALU.mult)
            ts(op["t1"], op["turns"], 127.0, ALU.add, 2.0 ** 23, ALU.mult)
            step(engine.tensor_copy(scale_int, op["t1"]))
            step(engine.tensor_copy(op["scale"], scale_int.bitcast(F32)))
            tt(op["t0"], op["t0"], op["scale"], ALU.mult)
            ts(op["scale"], op["scale"], -1.0, ALU.add)
            tt(out, op["t0"], op["scale"], ALU.add)

        engine.wait_ge(self.lam_loaded, 16 * 8)
        tt(op["den"], lam_re, lam_re, ALU.mult)
        tt(op["t0"], lam_im, lam_im, ALU.mult)
        tt(op["den"], op["den"], op["t0"], ALU.add)
        engine.sem_inc(self.den_ready, 1)
        exp_minus_1(op["dt"], log_dt)
        step(engine.tensor_copy(op["scale"], scale_int.bitcast(F32)))
        tt(op["dt"], op["t0"], op["scale"], ALU.add)
        tt(op["half"], lam_re, op["dt"], ALU.mult)
        exp_minus_1(op["em1"], op["half"])
        tt(op["x"], lam_im, op["dt"], ALU.mult)
        reduce_argument(step, engine, op["r"], op["x"], op["turns"], TWO_PI, op["t1"])
        ts(op["r"], op["r"], 0.25, ALU.mult)
        tt(op["t0"], op["r"], op["r"], ALU.mult)
        horner(step, engine, op["s"], op["t0"], [1.0, -1 / 6, 1 / 120, -1 / 5040, 1 / 362880])
        tt(op["s"], op["s"], op["r"], ALU.mult)
        horner(step, engine, op["c"], op["t0"], [1.0, -1 / 2, 1 / 24, -1 / 720, 1 / 40320, -1 / 3628800])
        scaled_product(step, engine, op["s2"], op["s"], 2.0, op["c"], op["t1"])
        scaled_product(step, engine, op["c2"], op["s"], -2.0, op["s"], op["t1"])
        ts(op["c2"], op["c2"], 1.0, ALU.add)
        scaled_product(step, engine, op["s"], op["s2"], 2.0, op["c2"], op["t1"])
        scaled_product(step, engine, op["cosm1"], op["s2"], -2.0, op["s2"], op["t1"])
        ts(op["c"], op["cosm1"], 1.0, ALU.add)
        ts(op["t1"], op["em1"], 1.0, ALU.add)
        tt(op["a_re"], op["t1"], op["c"], ALU.mult)
        tt(op["a_im"], op["t1"], op["s"], ALU.mult)
        tt(op["am1_re"], op["em1"], op["c"], ALU.mult)
        tt(op["am1_re"], op["am1_re"], op["cosm1"], ALU.add)
        engine.wait_ge(self.inv_ready, 1)
        tt(op["co_re"], op["am1_re"], lam_re, ALU.mult)
        tt(op["t0"], op["a_im"], lam_im, ALU.mult)
        tt(op["co_re"], op["co_re"], op["t0"], ALU.add)
        tt(op["co_re"], op["co_re"], op["inv"], ALU.mult)
        tt(op["co_im"], op["a_im"], lam_re, ALU.mult)
        tt(op["t0"], op["am1_re"], lam_im, ALU.mult)
        tt(op["co_im"], op["co_im"], op["t0"], ALU.subtract)
        tt(op["co_im"], op["co_im"], op["inv"], ALU.mult)
        engine.wait_ge(self.b_loaded, 16 * 4)
        for d in range(2):
            def over_channels(value):
                return value[:, d].rearrange("p (q a) -> p q a", a=1).broadcast_to([P, QS, SSM_CH])
            complex_product(step, engine, [bbar[:, d, r] for r in range(2)],
                            [over_channels(op["co_re"]), over_channels(op["co_im"])],
                            [b_raw[:, d, r] for r in range(2)], bbar_temp)
        for r, part in enumerate(("a_re", "a_im")):
            step(engine.tensor_copy(rising[:, :, r, 1, :], op[part]))
        for n in (1, 2, 4):
            for d in range(2):
                last = [rising[:, d, r, n:n + 1, :].broadcast_to([P, n, QS]) for r in range(2)]
                complex_product(step, engine, [rising[:, d, r, n + 1:2 * n + 1, :] for r in range(2)], last,
                                [rising[:, d, r, 1:n + 1, :] for r in range(2)], power_temp[:, 0:n])
        for k in range(SSM_L):
            step(engine.tensor_copy(falling[:, :, :, k, :], rising[:, :, :, SSM_L - k, :]))
        for d in range(2):
            for r in range(2):
                step(engine.tensor_copy(leaps[d][:, r, 0, :], rising[:, d, r, SSM_L, :]))
            for n in (1, 2, 4, 8):
                last = [leaps[d][:, r, n - 1:n, :].broadcast_to([P, n, QS]) for r in range(2)]
                complex_product(step, engine, [leaps[d][:, r, n:2 * n, :] for r in range(2)], last,
                                [leaps[d][:, r, 0:n, :] for r in range(2)], power_temp[:, 0:n])


def stage_mixers(nc, qkv, sink, attn_scratch, u_scratch, bases, ssm_d, y_scratch):
    with ExitStack() as ctx:
        m = Pool(nc, ctx, "sm")
        outof = [[m.sb(f"outof{d}{r}", [P, QS, POWERS, SSM_CH]) for r in range(2)] for d in range(2)]
        region = m.sb("region", [P, 2 * 2 * QS * P])
        into = region[:].rearrange("p (d r q s) -> p d r q s", d=2, r=2, q=QS)
        local = m.sb("local", [P, GROUPS, LC])
        with ExitStack() as part:
            ssm_tables(nc, Pool(nc, part, "st"), bases, ssm_d, outof, into, local)
        states = [m.sb(f"states{d}", [P, 2, QS, SSM_J + 1]) for d in range(2)]
        scans = [ChunkScan(m, d, states[d], bases.leaps[d], d == 1) for d in range(2)]
        with ExitStack() as part:
            chunks_into_states(nc, Pool(nc, part, "si"), u_scratch, into, states)
        with ExitStack() as part:
            attention_and_scan(nc, Pool(nc, part, "at"), region, qkv, sink, attn_scratch, scans)
        with ExitStack() as part:
            states_to_outputs(nc, Pool(nc, part, "so"), region, u_scratch, y_scratch, outof, local, states)


def ssm_tables(nc, m, bases, ssm_d, outof, into, local):
    ident = m.sb("ident", [P, P])
    params, bbar, rising, falling = bases.params, bases.bbar, bases.rising, bases.falling
    c_rows = m.sb("c_rows", [P, 2, 2, 4, 2 * SSM_N])
    c_t = m.sb("c_t", [P, 2, 2, QS, SSM_CH])
    d_rows = m.sb("d_rows", [SSM_CH, GROUPS, SSM_CH])
    d_diag = m.sb("d_diag", [SSM_CH, GROUPS, SSM_CH])
    b_table = [[m.sb(f"b_table{d}{r}", [P, QS, SSM_L, SSM_CH]) for r in range(2)] for d in range(2)]
    table_temp = m.sb("table_temp", [P, QS, POWERS, SSM_CH])
    kernels = m.sb("kernels", [SSM_CH, GROUPS, SPAN, SSM_CH])
    banks = m.psum("banks", [P, 8, BANK])
    c_loaded = m.sem("c_loaded")
    d_loaded = m.sem("d_loaded")
    ident_ready = m.sem("ident_ready")
    c_turned = m.sem("c_turned")
    c_copied = m.sem("c_copied")
    dve_step = m.sem("dve_step")
    pool_step = m.sem("pool_step")
    b_table_ready = [m.sem("b_table_ready0"), m.sem("b_table_ready1")]
    outof_ready = [m.sem("outof_ready0"), m.sem("outof_ready1")]
    kernels_done = m.sem("kernels_done")
    kernels_copied = m.sem("kernels_copied")
    kernels_ready = m.sem("kernels_ready")
    into_turned = m.sem("into_turned")
    into_copied = m.sem("into_copied")
    local_placed = m.sem("local_placed")
    PER_BANK = BANK // LC
    ON_DVE = 11

    block = m.ctx.enter_context(nc.Block())

    @block.sync
    def _(sync):
        for d in range(2):
            for r in range(2):
                rows = params[d][5 + r].rearrange("(w g) c n -> (g c) w n", w=4)
                for twice in range(2):
                    sync.dma_start(c_rows[:, d, r, :, twice * SSM_N:(twice + 1) * SSM_N], rows).then_inc(c_loaded, 16)
        sync.dma_start(d_rows[:].rearrange("p g c -> p (g c)"), row_broadcast(ssm_d, SSM_CH)).then_inc(d_loaded, 16)

    @block.scalar
    def _(act):
        for d in range(2):
            for r in range(2):
                act.wait_ge(c_turned, d * 2 + r + 1)
                turned = banks[:, d * 2 + r, :].rearrange("p (q e c) -> p q e c", e=2, c=SSM_CH)
                for e in range(2):
                    half = slice(e * SSM_N, (e + 1) * SSM_N)
                    act.activation(c_t[half, d, r], turned[half, :, e], ACT.Copy, scale=1.0 - 2.0 * r).then_inc(c_copied, 1)
        for n in range(4):
            for b in range(4):
                act.wait_ge(into_turned, n * 4 + b + 1)
                d, r = n // 2, n % 2
                act.activation(into[:, d, r, b * 4:(b + 1) * 4].rearrange("p a b -> p (a b)"),
                               banks[:, 4 + b, :], ACT.Copy).then_inc(into_copied, 1)
        for l in range(SSM_L):
            if l == 0:
                act.wait_ge(kernels_ready, 1)
            act.dma_start(local[l * SSM_CH:(l + 1) * SSM_CH, :, :],
                          kernels[:, :, SSM_L - 1 - l:2 * SSM_L - 1 - l, :].rearrange("c g k o -> c g (k o)"))\
                .then_inc(local_placed, 16)
        act.wait_ge(local_placed, SSM_L * 16)

    def tables(engine, step, qs):
        n_q = qs.stop - qs.start

        def power(table, d, k0, n, r):
            return table[:, d, r, k0:k0 + n, qs].rearrange("p k (q a) -> p q k a", a=1)\
                .broadcast_to([P, n_q, n, SSM_CH])

        def per_group(values, n):
            return values[:, qs].rearrange("p q (a c) -> p q a c", a=1).broadcast_to([P, n_q, n, SSM_CH])

        for d in range(2):
            source, k0 = ((falling, 1), (rising, 0))[d]
            complex_product(step, engine, [b_table[d][r][:, qs] for r in range(2)],
                            [power(source, d, k0, SSM_L, r) for r in range(2)],
                            [per_group(bbar[:, d, r], SSM_L) for r in range(2)], table_temp[:, qs, 0:SSM_L])
            engine.sem_inc(b_table_ready[d], 1)
        for d in range(2):
            engine.wait_ge(c_copied, 4 * (d + 1))
            source = (rising, falling)[d]
            complex_product(step, engine, [outof[d][r][:, qs] for r in range(2)],
                            [power(source, d, 0, POWERS, r) for r in range(2)],
                            [per_group(c_t[:, d, r], POWERS) for r in range(2)], table_temp[:, qs], conjugate=True)
            engine.sem_inc(outof_ready[d], 1)

    @block.gpsimd
    def _(pool):
        step = Steps(pool, pool_step)
        step(pool.memset(ident[:], 0.0))
        step(pool.affine_select(out=ident[:], in_=ident[:], compare_op=ALU.not_equal, fill=1.0,
                                base=0, pattern=[[-1, P]], channel_multiplier=1))
        pool.sem_inc(ident_ready, 1)
        tables(pool, step, slice(ON_DVE, QS))
        pool.wait_ge(d_loaded, 16)
        step(pool.tensor_tensor(d_diag[:], d_rows[:],
                                ident[0:SSM_CH, 0:SSM_CH].rearrange("p (a c) -> p a c", a=1)
                                .broadcast_to([SSM_CH, GROUPS, SSM_CH]), ALU.mult))
        pool.sem_inc(ident_ready, 1)

    @block.vector
    def _(dve):
        step = Steps(dve, dve_step)
        tables(dve, step, slice(0, ON_DVE))
        copied = Steps(dve, kernels_copied)
        for d in range(2):
            for b in range(GROUPS // PER_BANK):
                dve.wait_ge(kernels_done, d * (GROUPS // PER_BANK) + b + 1)
                qs = slice(b // 2 * PER_BANK, (b // 2 + 1) * PER_BANK)
                mine = kernels[:].rearrange("c (q e) k o -> c e q k o", e=2)[:, b % 2, qs]
                found = banks[0:SSM_CH, b % 4, :].rearrange("c (g k o) -> c g k o", g=PER_BANK, o=SSM_CH)
                if d == 0:
                    copied(dve.tensor_copy(mine[:, :, SSM_L - 1:SPAN], found))
                else:
                    step(dve.tensor_tensor(mine[:, :, SSM_L - 1], mine[:, :, SSM_L - 1],
                                           found[:, :, SSM_L - 1], ALU.add))
                    copied(dve.tensor_copy(mine[:, :, 0:SSM_L - 1], found[:, :, 0:SSM_L - 1]))
        dve.wait_ge(ident_ready, 2)
        step(dve.tensor_tensor(kernels[:, :, SSM_L - 1], kernels[:, :, SSM_L - 1], d_diag[:], ALU.add))
        dve.sem_inc(kernels_ready, 1)

    @block.tensor
    def _(pe):
        pe.wait_ge(ident_ready, 1)
        pe.wait_ge(c_loaded, 16 * 8)
        for d in range(2):
            for r in range(2):
                for w in range(4):
                    turn = pe.transpose(banks[:, d * 2 + r, w * P:(w + 1) * P], c_rows[:, d, r, w], ident[:])
                turn.then_inc(c_turned, 1)
        for d in range(2):
            pe.wait_ge(b_table_ready[d], 2)
            for r in range(2):
                for b in range(4):
                    n = (d * 2 + r) * 4 + b
                    if n >= 4:
                        pe.wait_ge(into_copied, n - 3)
                    for a in range(4):
                        turn = pe.transpose(banks[:, 4 + b, a * P:(a + 1) * P],
                                            b_table[d][r][:, b * 4 + a].rearrange("p l c -> p (l c)"), ident[:])
                    turn.then_inc(into_turned, 1)
        pe.wait_ge(c_copied, 8)
        for d in range(2):
            pe.wait_ge(outof_ready[d], 2)
            k0 = 0 if d == 0 else 1
            bare = SSM_L - 1 if d == 0 else 0
            for b in range(GROUPS // PER_BANK):
                n = d * (GROUPS // PER_BANK) + b
                if n >= 4:
                    pe.wait_ge(kernels_copied, n - 3)
                for j in range(PER_BANK):
                    q, part = b // 2 * PER_BANK + j, slice(b % 2 * SSM_N, (b % 2 + 1) * SSM_N)
                    for r in range(2):
                        done = pe.matmul(banks[0:SSM_CH, b % 4, j * LC:(j + 1) * LC], b_table[d][r][part, q, bare],
                                         outof[d][r][part, q, k0:k0 + SSM_L].rearrange("p k c -> p (k c)"),
                                         start=r == 0, stop=r == 1)
                done.then_inc(kernels_done, 1)


def attention_and_scan(nc, m, region, qkv, sink, attn_scratch, scans):
    KEYS = 3 * P
    group = N_HEADS // N_KV
    ident = m.sb("ident", [P, P])
    views = carve(region, {"bias": (P, (N_HEADS, KEYS)), "q": (HEAD, (2, N_HEADS, P)), "k": (HEAD, (2, N_KV, KEYS)),
                           "neg_scores": (P, (2, KEYS)), "probs": (P, (2, KEYS))})
    bias = views["bias"]
    q, k, neg_scores, probs = views["q"], views["k"], views["neg_scores"], views["probs"]
    distance = m.sb("distance", [P, KEYS], I32)
    distance_f = m.sb("distance_f", [P, KEYS])
    sinks = m.sb("sinks", [P, N_HEADS])
    neg_sinks = m.sb("neg_sinks", [P, N_HEADS])
    v_rows = m.sb("v_rows", [P, 2, KEYS])
    v = m.sb("v", [P, 2, 3, KV])
    probs_t = m.sb("probs_t", [P, 2, KEYS])
    neg_top = m.sb("neg_top", [P, 2, N_HEADS])
    sums = m.sb("sums", [P, 2, N_HEADS])
    sink_gap = m.sb("sink_gap", [P, N_HEADS])
    sink_exp = m.sb("sink_exp", [P, N_HEADS])
    total = m.sb("total", [P, N_HEADS])
    share = m.sb("share", [P, N_HEADS])
    attn = m.sb("attn", [P, N_HEADS, HEAD])
    attn_t = m.sb("attn_t", [P, 2, ATTN])
    s_psum = m.psum("s_psum", [P, 2, BANK])
    p_psum = m.psum("p_psum", [P, 2, BANK])
    o_psum = m.psum("o_psum", [P, 2, BANK])
    v_psum = m.psum("v_psum", [P, BANK])
    a_psum = m.psum("a_psum", [P, BANK])
    warmed = m.sem("warmed")
    sinks_in = m.sem("sinks_in")
    ident_ready = m.sem("ident_ready")
    iota_ready = m.sem("iota_ready")
    bias_step = m.sem("bias_step")
    bias_ready = m.sem("bias_ready")
    q_in = [m.sem("q_in0"), m.sem("q_in1")]
    k_in = [m.sem("k_in0"), m.sem("k_in1")]
    v_in = [m.sem("v_in0"), m.sem("v_in1")]
    loaded_free = m.sem("loaded_free")
    scores_done = m.sem("scores_done")
    mask_started = m.sem("mask_started")
    masked = m.sem("masked")
    exp_done = m.sem("exp_done")
    turned = m.sem("turned")
    probs_t_ready = m.sem("probs_t_ready")
    pv_done = m.sem("pv_done")
    v_turned = m.sem("v_turned")
    v_ready = m.sem("v_ready")
    gap_ready = m.sem("gap_ready")
    sink_ready = m.sem("sink_ready")
    share_step = m.sem("share_step")
    attn_ready = m.sem("attn_ready")
    attn_turned = m.sem("attn_turned")
    out_ready = m.sem("out_ready")
    stored = [m.sem("stored0"), m.sem("stored1")]
    for scan in scans:
        scan.add_semaphores(m)
    q_rows = qkv[0:ATTN, :].rearrange("(h d) t -> d h t", d=HEAD)
    k_rows = qkv[ATTN:ATTN + KV, :].rearrange("(h d) t -> d h t", d=HEAD)
    v_src = qkv[ATTN + KV:ATTN + 2 * KV, :]
    out_rows = attn_scratch.rearrange("(b p) t -> p b t", p=P)

    def keys_of(kind):
        lo, hi = {"first": (1, 3), "middle": (0, 3), "last": (0, 2)}[kind]
        return lo, hi, slice(lo * P, hi * P)

    def over_blocks(engine, body):
        body(0, 0, "first", "middle")
        body(0, 1, "middle", "middle")
        with engine.Fori(1, TILES // 2 - 1) as i:
            for s in range(2):
                body(i, s, "middle", "middle")
        body(TILES // 2 - 1, 0, "middle", "last")
        body(TILES // 2 - 1, 1, "last", None)

    block = m.ctx.enter_context(nc.Block())

    @block.sync
    def _(sync):
        sync.dma_start(sinks[:], row_broadcast(sink)).then_inc(sinks_in, 16)

        def load(i, s, kind, following):
            lo, hi, part = keys_of(kind)
            b = i * 2 + s
            sync.wait_ge(loaded_free, b + 1)
            sync.dma_start(q[:, s], q_rows[:, :, bass.ds(b * P, P)]).then_inc(q_in[s], 16)
            keys = bass.ds(b * P + (lo - 1) * P, (hi - lo) * P)
            sync.dma_start(k[:, s, :, part], k_rows[:, :, keys]).then_inc(k_in[s], 16)
            sync.dma_start(v_rows[:, s, part], v_src[:, keys]).then_inc(v_in[s], 16)

        over_blocks(sync, load)

    @block.gpsimd
    def _(pool):
        pool.memset(ident[:], 0.0).then_inc(ident_ready, 1)
        pool.iota(distance[:], pattern=[[-1, KEYS]], base=P, channel_multiplier=1).then_inc(iota_ready, 1)
        pool.wait_ge(ident_ready, 1)
        pool.affine_select(out=ident[:], in_=ident[:], compare_op=ALU.not_equal, fill=1.0,
                           base=0, pattern=[[-1, P]], channel_multiplier=1).then_inc(ident_ready, 1)
        pool.wait_ge(bias_step, 2 + N_HEADS)
        pool.affine_select(out=bias[:], in_=bias[:], compare_op=ALU.is_ge, fill=NEG_INF * HEAD ** 0.5,
                           base=WINDOW + P, pattern=[[0, N_HEADS], [-1, KEYS]], channel_multiplier=1)\
            .then_inc(bias_ready, 1)
        pool.wait_ge(bias_ready, 1)
        pool.affine_select(out=bias[:], in_=bias[:], compare_op=ALU.is_ge, fill=NEG_INF * HEAD ** 0.5,
                           base=WINDOW - P, pattern=[[0, N_HEADS], [1, KEYS]], channel_multiplier=-1)\
            .then_inc(bias_ready, 1)
        scans[1].run(pool)

    @block.tensor
    def _(pe):
        def turn_values(i, s, kind):
            lo, hi, part = keys_of(kind)
            pe.wait_ge(v_in[s], i * 16 + 16)
            pe.wait_ge(v_ready, i * 2 + s + 1)
            for j in range(lo, hi):
                turn = pe.transpose(v_psum[:, j * P:(j + 1) * P], v_rows[:, s, j * P:(j + 1) * P], ident[:])
            turn.then_inc(v_turned, 1)

        def score(i, s, kind, h):
            lo, hi, part = keys_of(kind)
            if h == 0:
                pe.wait_ge(q_in[s], i * 16 + 16)
                pe.wait_ge(k_in[s], i * 16 + 16)
            pe.wait_ge(masked, i * (2 * N_HEADS) + (s * N_HEADS + h + 1))
            pe.matmul(s_psum[:, h % 2, part], q[:, s, h, :], k[:, s, h // group, part],
                      start=True, stop=True).then_inc(scores_done, 1)

        def turn_probs(i, s, kind, h):
            lo, hi, part = keys_of(kind)
            n = i * (2 * N_HEADS) + (s * N_HEADS + h)
            pe.wait_ge(exp_done, n + 3)
            pe.wait_ge(probs_t_ready, n + 1)
            for j in range(lo, hi):
                turn = pe.transpose(p_psum[:, h % 2, j * P:(j + 1) * P], probs[:, h % 2, j * P:(j + 1) * P],
                                    ident[:])
            turn.then_inc(turned, 1)

        def weigh(i, s, kind, h):
            lo, hi, part = keys_of(kind)
            pe.wait_ge(probs_t_ready, i * (2 * N_HEADS) + (s * N_HEADS + h + 3))
            if h == 0:
                pe.wait_ge(v_ready, i * 2 + s + 2)
                pe.wait_ge(attn_ready, i * 2 + s + 1)
            g = h // group
            for j in range(lo, hi):
                pv = pe.matmul(o_psum[:, s, h * HEAD:(h + 1) * HEAD], probs_t[:, h % 2, j * P:(j + 1) * P],
                               v[:, s, j, g * HEAD:(g + 1) * HEAD], start=j == lo, stop=j == hi - 1)
            pv.then_inc(pv_done, 1)

        def turn_attn(i, s):
            b = i * 2 + s
            pe.wait_ge(attn_ready, b + 3)
            if not isinstance(b, int) or b:
                pe.wait_ge(out_ready, b)
            for j in range(ATTN // P):
                turn = pe.transpose(a_psum[:, j * P:(j + 1) * P],
                                    attn[:, 2 * j:2 * j + 2, :].rearrange("p h d -> p (h d)"), ident[:])
            turn.then_inc(attn_turned, 1)

        def attend(i, s, kind, following):
            later, before = (i + s, 1 - s), (i + (s - 1), 1 - s)
            for h in range(N_HEADS):
                if h + 2 < N_HEADS:
                    score(i, s, kind, h + 2)
                elif following:
                    score(*later, following, h + 2 - N_HEADS)
                turn_probs(i, s, kind, h)
                if h:
                    weigh(i, s, kind, h - 1)
                elif kind != "first":
                    weigh(*before, "first" if isinstance(i, int) and i * 2 + s == 1 else "middle", N_HEADS - 1)
                if h == 4 and kind != "first":
                    turn_attn(*before)
                if h == N_HEADS - 2:
                    pe.wait_ge(scores_done, (i * 2 + s) * N_HEADS + N_HEADS)
                    pe.wait_ge(v_turned, i * 2 + s + 1)
                    pe.sem_inc(loaded_free, 1)
                    if following:
                        turn_values(*later, following)

        pe.sem_inc(loaded_free, 2)
        pe.sem_inc(turned, 2)
        pe.sem_inc(pv_done, 2)
        pe.wait_ge(ident_ready, 2)
        for n in range(WARM_UP):
            warm = pe.transpose(a_psum[:, 0:P], ident[:], ident[:])
        warm.then_inc(warmed, 1)
        pe.wait_ge(warmed, 1)
        turn_values(0, 0, "first")
        score(0, 0, "first", 0)
        score(0, 0, "first", 1)
        over_blocks(pe, attend)
        weigh(TILES // 2 - 1, 1, "last", N_HEADS - 1)
        turn_attn(TILES // 2 - 1, 1)

    @block.vector
    def _(dve):
        def mask(i, s, kind, h):
            part = keys_of(kind)[2]
            n = i * (2 * N_HEADS) + (s * N_HEADS + h)
            dve.wait_ge(exp_done, n + 1)
            dve.wait_ge(scores_done, n + 1)
            dve.sem_inc(mask_started, 1)
            dve.tensor_tensor_reduce(neg_scores[:, h % 2, part], s_psum[:, h % 2, part], bias[:, h, part],
                                     -HEAD ** -0.5, neg_sinks[:, h:h + 1], ALU.add, ALU.min,
                                     neg_top[:, s, h:h + 1]).then_inc(masked, 1)

        scan = scans[0]

        def scan_parts(i, s, h, phase):
            b = i * 2 + s
            if phase == "within":
                n = b * 2 + (h // 4 - 1)
                if not isinstance(n, int) or n >= 0:
                    scan.part(dve, scan.within(n), h % 4)
            elif phase == "of last":
                n = (b - TILES // 2) * N_HEADS + h
                if n < SCAN_J - 1:
                    for part in range(4):
                        scan.part(dve, scan.of_last(n), part)
            elif phase == "into next":
                for part in range(h * 3 // 2, (h + 1) * 3 // 2):
                    n = (b - (TILES // 2 + 2)) * 3 + part // 4
                    scan.part(dve, scan.into_next(n), part % 4)

        def copy_values(i, s, kind):
            lo, hi, part = keys_of(kind)
            dve.wait_ge(v_turned, i * 2 + s + 1)
            dve.tensor_copy(v[:, s, lo:hi].rearrange("p a b -> p (a b)"), v_psum[:, part]).then_inc(v_ready, 1)

        def open_norm(i, s):
            dve.wait_ge(masked, (i * 2 + s) * N_HEADS + (N_HEADS + 2))
            dve.tensor_tensor(sink_gap[:], sinks[:], neg_top[:, s], ALU.add).then_inc(gap_ready, 1)

        def norm(i, s):
            b = i * 2 + s
            dve.wait_ge(sink_ready, b + 1)
            dve.tensor_tensor(total[:], sums[:, s], sink_exp[:], ALU.add).then_inc(share_step, 1)
            dve.wait_ge(share_step, b * 2 + 1)
            dve.reciprocal(share[:], total[:]).then_inc(share_step, 1)
            dve.wait_ge(share_step, b * 2 + 2)
            dve.wait_ge(pv_done, b * N_HEADS + (N_HEADS + 2))
            if not isinstance(b, int) or b:
                dve.wait_ge(attn_turned, b)
            dve.tensor_tensor(attn[:], o_psum[:, s].rearrange("p (h d) -> p h d", d=HEAD),
                              share[:].rearrange("p (h a) -> p h a", a=1).broadcast_to([P, N_HEADS, HEAD]),
                              ALU.mult).then_inc(attn_ready, 1)

        def attend(i, s, kind, following, phase):
            later, before = (i + s, 1 - s), (i + (s - 1), 1 - s)
            for h in range(N_HEADS):
                if h + 1 < N_HEADS:
                    mask(i, s, kind, h + 1)
                elif following:
                    mask(*later, following, 0)
                scan_parts(i, s, h, phase)
                if kind != "first":
                    if h == 0:
                        open_norm(*before)
                    if h == 2:
                        norm(*before)
                if h == N_HEADS - 1 and following:
                    copy_values(*later, following)

        dve.wait_ge(iota_ready, 1)
        dve.tensor_copy(distance_f[:], distance[:]).then_inc(bias_step, 1)
        dve.wait_ge(bias_step, 1)
        dve.scalar_tensor_tensor(out=distance_f[:], in0=distance_f[:], scalar=-1.0, in1=distance_f[:],
                                 op0=ALU.mult, op1=ALU.max).then_inc(bias_step, 1)
        dve.wait_ge(bias_step, 2)
        for h in range(N_HEADS):
            slope = 2.0 ** (-8.0 * (h + 1) / N_HEADS)
            dve.tensor_scalar(bias[:, h, :], distance_f[:], -slope * HEAD ** 0.5, None, ALU.mult)\
                .then_inc(bias_step, 1)
        dve.wait_ge(sinks_in, 16)
        dve.tensor_scalar(neg_sinks[:], sinks[:], -1.0, None, ALU.mult).then_inc(bias_step, 1)
        dve.wait_ge(bias_step, 3 + N_HEADS)
        dve.wait_ge(bias_ready, 2)
        dve.sem_inc(masked, 2)
        dve.sem_inc(scans[0].done, 1)
        dve.sem_inc(v_ready, 1)
        dve.sem_inc(attn_ready, 2)
        copy_values(0, 0, "first")
        mask(0, 0, "first", 0)
        attend(0, 0, "first", "middle", "within")
        attend(0, 1, "middle", "middle", "within")
        with dve.Fori(1, TILES // 4) as i:
            for s in range(2):
                attend(i, s, "middle", "middle", "within")
        for s in range(2):
            attend(TILES // 4, s, "middle", "middle", "of last")
        with dve.Fori(TILES // 4 + 1, TILES // 2 - 1) as i:
            for s in range(2):
                attend(i, s, "middle", "middle", "into next")
        attend(TILES // 2 - 1, 0, "middle", "last", "into next")
        attend(TILES // 2 - 1, 1, "last", None, None)
        open_norm(TILES // 2 - 1, 1)
        norm(TILES // 2 - 1, 1)

    @block.scalar
    def _(act):
        def exponentials(i, s, kind, h):
            part = keys_of(kind)[2]
            n = i * (2 * N_HEADS) + (s * N_HEADS + h)
            act.wait_ge(masked, n + 3)
            act.wait_ge(turned, n + 1)
            act.activation(probs[:, h % 2, part], neg_scores[:, h % 2, part], ACT.Exp, scale=-1.0,
                           bias=neg_top[:, s, h:h + 1], accum_out=sums[:, s, h:h + 1]).then_inc(exp_done, 1)

        def copy_turned(i, s, kind, h):
            part = keys_of(kind)[2]
            n = i * (2 * N_HEADS) + (s * N_HEADS + h)
            act.wait_ge(turned, n + 3)
            act.wait_ge(pv_done, n + 1)
            act.activation(probs_t[:, h % 2, part], p_psum[:, h % 2, part], ACT.Copy).then_inc(probs_t_ready, 1)

        def sink_part(i, s):
            act.wait_ge(gap_ready, i * 2 + s + 1)
            act.activation(sink_exp[:], sink_gap[:], ACT.Exp).then_inc(sink_ready, 1)

        def copy_out(i, s):
            b = i * 2 + s
            act.wait_ge(attn_turned, b + 1)
            act.wait_ge(stored[s], i * 16 + 16)
            act.activation(attn_t[:, s], a_psum[:], ACT.Copy).then_inc(out_ready, 1)
            act.wait_ge(out_ready, b + 1)
            act.dma_start(out_rows[:, :, bass.ds(b * P, P)], attn_t[:, s].rearrange("p (a t) -> p a t", t=P))\
                .then_inc(stored[s], 16)

        def attend(i, s, kind, following):
            later, before = (i + s, 1 - s), (i + (s - 1), 1 - s)
            for h in range(N_HEADS):
                if h + 1 < N_HEADS:
                    exponentials(i, s, kind, h + 1)
                elif following:
                    exponentials(*later, following, 0)
                copy_turned(i, s, kind, h)
                if kind != "first":
                    if h == 1:
                        sink_part(*before)
                    if h == 5:
                        copy_out(*before)

        act.sem_inc(exp_done, 2)
        act.sem_inc(probs_t_ready, 2)
        for s in range(2):
            act.sem_inc(stored[s], 16)
        exponentials(0, 0, "first", 0)
        over_blocks(act, attend)
        sink_part(TILES // 2 - 1, 1)
        copy_out(TILES // 2 - 1, 1)
        for s in range(2):
            act.wait_ge(stored[s], (TILES // 2 + 1) * 16)


class ChunkScan:
    PER_STEP = 5

    def __init__(self, m, d, states, leaps, on_pool):
        self.d, self.on_pool, self.leaps = d, on_pool, leaps
        self.grid = states[:, :, :, 1 - d:1 - d + SSM_J].rearrange("p r q (j i) -> p r q j i", i=SCAN_I)
        self.end = SCAN_I - 1 if d == 0 else 0
        self.by_re = m.sb(f"by_re{d}", [P, 2, QS, SCAN_J])
        self.by_im = m.sb(f"by_im{d}", [P, 2, QS, SCAN_J])

    def add_semaphores(self, m):
        self.done = m.sem(f"scan_done{self.d}")
        self.start = m.sem(f"scan_start{self.d}")

    def within(self, i):
        now, last = (i + 1, i) if self.d == 0 else (SCAN_I - 2 - i, SCAN_I - 1 - i)
        target, source = (self.grid[:, :, :, :, bass.ds(n, 1)].rearrange("p r q j i -> p r q (j i)")
                          for n in (now, last))
        return target, source, slice(0, 1), SCAN_J, i * self.PER_STEP + 1

    def of_last(self, i):
        now, last = (i + 1, i) if self.d == 0 else (SCAN_J - 2 - i, SCAN_J - 1 - i)
        target, source = (self.grid[:, :, :, bass.ds(n, 1), self.end] for n in (now, last))
        return target, source, slice(SCAN_I - 1, SCAN_I), 1, i * self.PER_STEP + (self.PER_STEP * (SCAN_I - 1) + 1)

    def into_next(self, i):
        targets, sources = slice(1, SCAN_J), slice(0, SCAN_J - 1)
        now = i
        if self.d == 1:
            targets, sources = sources, targets
            now = SCAN_I - 1 - i
        target = self.grid[:, :, :, targets, bass.ds(now, 1)].rearrange("p r q j i -> p r q (j i)")
        return (target, self.grid[:, :, :, sources, self.end], bass.ds(i, 1), SCAN_J - 1,
                i * self.PER_STEP + (self.PER_STEP * (SCAN_I + SCAN_J - 2) + 1))

    def part(self, engine, step, n):
        target, source, power, blocks, before = step
        by_re, by_im = self.by_re[:, :, :, 0:blocks], self.by_im[:, :, :, 0:blocks]
        done = self.done
        engine.wait_ge(done, before + n)
        if self.on_pool:
            engine.sem_inc(self.start, 1)
        if n < 2:
            factor = self.leaps[:, n, power, :].rearrange("p k (q b) -> p k q b", b=1)\
                .broadcast_to([P, 2, QS, blocks])
            engine.tensor_tensor((by_re, by_im)[n], source, factor, ALU.mult).then_inc(done, 1)
        elif n == 2:
            engine.tensor_tensor(target, target, by_re, ALU.add).then_inc(done, 1)
        else:
            engine.tensor_tensor(target[:, 0:1], target[:, 0:1], by_im[:, 1:2], ALU.subtract).then_inc(done, 1)
            engine.tensor_tensor(target[:, 1:2], target[:, 1:2], by_im[:, 0:1], ALU.add).then_inc(done, 1)

    def over_blocks(self, engine):
        with engine.Fori(0, SCAN_J - 1) as i:
            for n in range(4):
                self.part(engine, self.of_last(i), n)

    def run(self, engine):
        engine.sem_inc(self.done, 1)
        with engine.Fori(0, SCAN_I - 1) as i:
            for n in range(4):
                self.part(engine, self.within(i), n)
        self.over_blocks(engine)
        with engine.Fori(0, SCAN_I - 1) as i:
            for n in range(4):
                self.part(engine, self.into_next(i), n)


def load_chunks(engine, u, u_scratch, u_in, side):
    u_chunks = u_scratch.rearrange("(g c) (l j) -> l c g j", c=SSM_CH, l=SSM_L)
    for half in range(2):
        groups = slice(half * GROUPS // 2, (half + 1) * GROUPS // 2)
        for l in range(side, SSM_L, 2):
            engine.dma_start(u[l * SSM_CH:(l + 1) * SSM_CH, groups], u_chunks[l, :, groups]).then_inc(u_in[half], 16)


def chunks_into_states(nc, m, u_scratch, into, states):
    u = m.sb("u", [P, GROUPS, SSM_J])
    banks = m.psum("banks", [P, 8, BANK])
    u_in = [m.sem("u_in0"), m.sem("u_in1")]
    edge_zero = m.sem("edge_zero")
    into_done = m.sem("into_done")
    into_copied = m.sem("into_copied")
    block = m.ctx.enter_context(nc.Block())

    @block.sync
    def _(sync):
        load_chunks(sync, u, u_scratch, u_in, 0)

    @block.tensor
    def _(pe):
        for q in range(QS):
            if q % (QS // 2) == 0:
                pe.wait_ge(u_in[q // (QS // 2)], 16 * SSM_L)
            for d in range(2):
                n = q * 2 + d
                if n >= 8:
                    pe.wait_ge(into_copied, n - 7)
                for r in range(2):
                    for e in range(2):
                        half = slice(e * SSM_N, (e + 1) * SSM_N)
                        done = pe.matmul(banks[half, n % 8, r * SSM_J:(r + 1) * SSM_J], into[:, d, r, q, half],
                                         u[:, 2 * q + e, :], start=True, stop=True)
                done.then_inc(into_done, 1)

    @block.scalar
    def _(act):
        load_chunks(act, u, u_scratch, u_in, 1)
        for n in range(2 * QS):
            q, d = n // 2, n % 2
            act.wait_ge(into_done, n + 1)
            act.activation(states[d][:, :, q, 1 - d:1 - d + SSM_J],
                           banks[:, n % 8, :].rearrange("p (r j) -> p r j", r=2), ACT.Copy).then_inc(into_copied, 1)

    @block.vector
    def _(dve):
        dve.memset(states[0][:, :, :, 0:1], 0.0).then_inc(edge_zero, 1)
        dve.memset(states[1][:, :, :, SSM_J:SSM_J + 1], 0.0).then_inc(edge_zero, 1)


def states_to_outputs(nc, m, region, u_scratch, y_scratch, outof, local, states):
    u = region[:].rearrange("p (g j) -> p g j", g=GROUPS)
    y = m.sb("y", [P, 2, 4, SSM_J])
    banks = m.psum("banks", [P, 8, BANK])
    u_in = [m.sem("u_in0"), m.sem("u_in1")]
    y_done = m.sem("y_done")
    y_ready = m.sem("y_ready")
    stored = [m.sem("stored0"), m.sem("stored1")]
    y_chunks = y_scratch.rearrange("(g c) (l j) -> l c g j", c=SSM_CH, l=SSM_L)
    block = m.ctx.enter_context(nc.Block())

    @block.sync
    def _(sync):
        load_chunks(sync, u, u_scratch, u_in, 0)
        with sync.Fori(0, QS // 4) as i:
            for s in range(2):
                sync.wait_ge(y_ready, i * 4 + s * 2 + 2)
                for l in range(SSM_L):
                    sync.dma_start(y_chunks[l, :, bass.ds((i * 2 + s) * 4, 4), :], y[l * SSM_CH:(l + 1) * SSM_CH, s])\
                        .then_inc(stored[s], 16)
        for s in range(2):
            sync.wait_ge(stored[s], QS // 4 * SSM_L * 16)

    @block.tensor
    def _(pe):
        def own_tokens(q):
            for e in range(2):
                pe.matmul(banks[:, q % 4 * 2 + e, 0:SSM_J], local[:, 2 * q + e, :], u[:, 2 * q + e, :],
                          start=True, stop=False)

        pe.wait_ge(u_in[0], 16 * SSM_L)
        for q in range(4):
            own_tokens(q)
        for q in range(QS):
            for e in range(2):
                half = slice(e * SSM_N, (e + 1) * SSM_N)
                bank = banks[:, q % 4 * 2 + e, 0:SSM_J]
                for d in range(2):
                    for r in range(2):
                        done = pe.matmul(bank, outof[d][r][half, q, 1 - d:1 - d + SSM_L].rearrange("p k c -> p (k c)"),
                                         states[d][half, r, q, d:d + SSM_J],
                                         start=False, stop=d == 1 and r == 1)
            done.then_inc(y_done, 1)
            if 1 <= q < QS - 3:
                pe.wait_ge(y_ready, q)
                if q + 3 == QS // 2:
                    pe.wait_ge(u_in[1], 16 * SSM_L)
                own_tokens(q + 3)

    @block.scalar
    def _(act):
        load_chunks(act, u, u_scratch, u_in, 1)
        for q in range(QS):
            act.wait_ge(y_done, q + 1)
            if q >= 4 and q % 2 == 0:
                act.wait_ge(stored[q // 2 % 2], q // 4 * SSM_L * 16)
            act.activation(y[:, q // 2 % 2, q % 2 * 2:q % 2 * 2 + 2], banks[:, q % 4 * 2:q % 4 * 2 + 2, 0:SSM_J],
                           ACT.Gelu_apprx_tanh).then_inc(y_ready, 1)


LAM_NAMES = ("lam_re", "lam_im", "log_dt", "b_re", "b_im", "c_re", "c_im")


def hybrid_layer(nc, t):
    def scratch(name, shape):
        return nc.dram_tensor(name, shape, F32, kind="Internal").ap()

    qkv = scratch("qkv", (ATTN + 2 * KV, TOK))
    u = scratch("u", (SSM, TOK))
    gates = scratch("gates", (2 * D, TOK))
    attn = scratch("attn", (ATTN, TOK))
    y = scratch("y_ssm", (SSM, TOK))
    merged = scratch("merged", (D, TOK))
    x_mid = scratch("x_mid", (TOK, D))
    f = scratch("f", (FF, TOK))
    params = [[t[f"{name}_{direction}"] for name in LAM_NAMES] for direction in "fb"]

    with nc.sbuf_tensor("bases", [P, RING * D], F32) as memory:
        bases = SsmBases(params, memory)
        stage_project_in(nc, t["x"], t["norm_mix_pre"], t["w_in"], qkv, u, gates, bases)
        stage_mixers(nc, qkv, t["attn_sink"], attn, u, bases, t["ssm_d"], y)
    stage_branches(nc, attn, y, gates, t["w_glu"], t["b_glu"], t["w_branch_attn"], t["w_branch_ssm"], merged)
    stage_out(nc, merged, t["w_out"], t["norm_mix_post"], t["x"], x_mid)
    stage_gate_up(nc, x_mid, t["norm_ffn_pre"], t["w_ffn_gate"], t["w_ffn_up"], t["conv_w"], t["conv_b"], f)
    stage_down(nc, f, t["w_ffn_down"], t["norm_ffn_post"], x_mid, t["out"])


def kernel(**inputs):
    import numpy as np
    from concourse import bacc
    from concourse.bass_utils import run_bass_kernel_spmd

    nc = bacc.Bacc("TRN2", target_bir_lowering=False, num_devices=1)
    arrays, tensors = {}, {}
    for name, value in inputs.items():
        array = np.ascontiguousarray(value)
        arrays[f"in_{name}"] = array
        handle = nc.dram_tensor(f"in_{name}", array.shape, mybir.dt.from_np(array.dtype), kind="ExternalInput").ap()
        tensors[name] = handle[0]
    out = nc.dram_tensor("out", (1, TOK, D), F32, kind="ExternalOutput").ap()
    tensors["out"] = out[0]
    hybrid_layer(nc, tensors)
    result = run_bass_kernel_spmd(nc, [arrays], core_ids=[0])
    return result.results[0]["out"]
```

```python
import math
from contextlib import ExitStack

import concourse.bass as bass
import concourse.mybir as mybir

F32 = mybir.dt.float32
F32R = mybir.dt.float32r
BF16 = mybir.dt.bfloat16
I32 = mybir.dt.int32
ALU = mybir.AluOpType
ACT = mybir.ActivationFunctionType

P = 128
TOK = 2048
D = 1024
KD = D // P
N_HEADS, N_KV, HEAD = 8, 2, 64
ATTN = N_HEADS * HEAD
KV = N_KV * HEAD
WINDOW = 128
SSM, SSM_CH, SSM_N = 512, 16, 64
GROUPS = SSM // SSM_CH
FF = 2816
KF = FF // P
EPS = 1e-6
NEG_INF = -1e30
BANK = 512
TILES = TOK // P
CHUNKS = TOK // BANK
WARM_UP = 72

SSM_L = 8
SSM_J = TOK // SSM_L


class Pool:

    def __init__(self, nc, ctx, tag):
        self.nc, self.ctx, self.tag = nc, ctx, tag
        self.handles = []
        self.lowest = min(nc.free_semaphores)
        ctx.callback(self.zero)

    def zero(self):
        if self.handles:
            self.nc.all_engine_barrier(sems_to_clear=range(self.lowest, self.lowest + len(self.handles)))
            for handle in self.handles:
                self.nc.release_semaphore(handle)

    def sb(self, name, shape, dt=F32):
        return self.ctx.enter_context(self.nc.sbuf_tensor(f"{self.tag}_{name}", shape, dt))

    def psum(self, name, shape, dt=F32):
        return self.ctx.enter_context(self.nc.psum_tensor(f"{self.tag}_{name}", shape, dt))

    def sem(self, name):
        self.handles.append(self.nc.alloc_semaphore(f"{self.tag}_{name}", self.lowest + len(self.handles)))
        return self.handles[-1]

    def pool_dma_sem(self, name):
        return self.nc.alloc_semaphore(f"{self.tag}_{name}", max(self.nc.free_semaphores))


def carve(region, shapes):
    views, used = {}, 0
    for name, (partitions, sizes) in shapes.items():
        axes = "abcde"[:len(sizes)]
        views[name] = region[0:partitions, used:used + math.prod(sizes)].rearrange(
            f"p ({' '.join(axes)}) -> p {' '.join(axes)}", **dict(zip(axes, sizes)))
        used += math.prod(sizes)
    return views


def row_broadcast(vector, n=P):
    return vector.rearrange("(a d) -> a d", a=1).broadcast_to([n, vector.shape[0]])


RING = BANK // P


def over_tiles(engine, step, ahead=None, after_first=None):
    last = TILES // RING - 1
    if ahead:
        ahead(0, 0)
    if after_first:
        for s in range(RING):
            if ahead:
                ahead((s + 1) // RING, (s + 1) % RING)
            step(0, s)
        after_first()
    with engine.Fori(1 if after_first else 0, last) as i:
        for s in range(RING):
            if ahead:
                ahead(i + (s + 1) // RING, (s + 1) % RING)
            step(i, s)
    for s in range(RING):
        if ahead and s + 1 < RING:
            ahead(last, s + 1)
        step(last, s)


def rms_constants(pool, consts, ready):
    for n, value in enumerate((1.0 / D, EPS, -0.5)):
        pool.memset(consts[:, n:n + 1], value).then_inc(ready, 1)


class NormTranspose:

    def __init__(self, m, src, gain, rows=None):
        self.src, self.gain = src, gain
        self.feat_hi = m.sb("feat_hi", [P, KD, TOK], F32R)
        self.feat_lo = m.sb("feat_lo", [P, KD, TOK], F32R)
        self.rows = rows or m.sb("rows", [P, RING, D])
        self.normed = m.sb("normed", [P, 2, D])
        self.squares = m.sb("squares", [P, D], BF16)
        self.gain_rows = m.sb("gain_rows", [P, D])
        self.ident = m.sb("ident", [P, P])
        self.consts = m.sb("consts", [P, 3])
        self.stat = m.sb("stat", [P, RING, 4])
        self.rows_in = [m.sem(f"rows_in{s}") for s in range(RING)]
        self.gain_in = m.sem("gain_in")
        self.const_ready = m.sem("const_ready")
        self.square_sum = m.sem("square_sum")
        self.mean_square = m.sem("mean_square")
        self.rstd = m.sem("rstd")
        self.normed_ready = m.sem("normed_ready")
        self.turned = m.sem("turned")
        self.hi_ready = m.sem("hi_ready")
        self.lo_ready = m.sem("lo_ready")

    def load(self, sync, ws, first_weights):
        def load_tile(i, s):
            t = i * RING + s
            sync.wait_ge(self.normed_ready, t + 1)
            sync.dma_start(self.rows[:, s, :], self.src[bass.ds(t * P, P), :]).then_inc(self.rows_in[s], 16)
            if isinstance(i, int) and t == 0:
                sync.dma_start(self.gain_rows[:], row_broadcast(self.gain)).then_inc(self.gain_in, 16)

        load_tile(0, 0)
        for s in range(1, RING):
            load_tile(0, s)
        for s, weights, columns in first_weights:
            ws.load(sync, weights, s, s, columns)
        with sync.Fori(1, TILES // RING) as i:
            for s in range(RING):
                load_tile(i, s)

    def gpsimd(self, pool):
        pool.memset(self.ident[:], 0.0).then_inc(self.const_ready, 1)
        rms_constants(pool, self.consts, self.const_ready)
        pool.wait_ge(self.const_ready, 4)
        pool.affine_select(out=self.ident[:], in_=self.ident[:], compare_op=ALU.not_equal, fill=1.0,
                           base=0, pattern=[[-1, P]], channel_multiplier=1).then_inc(self.const_ready, 1)

        def inverse_root(i, s):
            t = i * RING + s
            stat = self.stat
            pool.wait_ge(self.square_sum, t + 2)
            pool.tensor_tensor(stat[:, s, 1:2], stat[:, s, 0:1], self.consts[:, 0:1], ALU.mult)\
                .then_inc(self.mean_square, 1)
            pool.wait_ge(self.mean_square, t * 2 + 1)
            pool.tensor_tensor(stat[:, s, 2:3], stat[:, s, 1:2], self.consts[:, 1:2], ALU.add)\
                .then_inc(self.mean_square, 1)
            pool.wait_ge(self.mean_square, t * 2 + 2)
            pool.tensor_tensor(stat[:, s, 3:4], stat[:, s, 2:3], self.consts[:, 2:3], ALU.pow)\
                .then_inc(self.rstd, 1)

        over_tiles(pool, inverse_root)

    def scalar(self, act, psum):
        def square(i, s):
            t = i * RING + s
            act.wait_ge(self.square_sum, t + 1)
            act.wait_ge(self.rows_in[s], i * 16 + 16)
            act.wait_ge(self.normed_ready, t + 1)
            act.activation(self.squares[:], self.rows[:, s, :], ACT.Square,
                           accum_out=self.stat[:, s, 0:1]).then_inc(self.square_sum, 1)

        def keep_hi(i, s):
            t = i * RING + s
            act.wait_ge(self.turned, t + 3)
            act.activation(self.feat_hi[:, :, bass.ds(t * P, P)], psum[:, s % 2, :, :], ACT.Copy)\
                .then_inc(self.hi_ready, 1)

        act.sem_inc(self.square_sum, 1)
        over_tiles(act, keep_hi, square)

    def vector(self, dve, psum, ws):
        def norm(i, s):
            t = i * RING + s
            dve.wait_ge(self.rstd, t + 1)
            dve.wait_ge(self.turned, t + 1)
            dve.scalar_tensor_tensor(out=self.normed[:, s % 2, :], in0=self.rows[:, s, :],
                                     scalar=self.stat[:, s, 3:4], in1=self.gain_rows[:],
                                     op0=ALU.mult, op1=ALU.mult).then_inc(self.normed_ready, 1)

        def keep_lo(i, s):
            t = i * RING + s
            dve.wait_ge(self.hi_ready, t + 1)
            cols = bass.ds(t * P, P)
            dve.tensor_tensor(self.feat_lo[:, :, cols], psum[:, s % 2, :, :],
                              self.feat_hi[:, :, cols].bitcast(F32), ALU.subtract).then_inc(self.lo_ready, 1)

        dve.sem_inc(self.normed_ready, RING)
        dve.sem_inc(self.lo_ready, 2)
        dve.sem_inc(ws.raw_free, 2)
        dve.wait_ge(self.gain_in, 16)
        over_tiles(dve, keep_lo, norm, lambda: ws.vector(dve, 0, 0, 0))
        ws.vector(dve, 1, 0, 1)

    def tensor(self, pe, psum, banks, ws):
        def turn_tile(i, s):
            t = i * RING + s
            pe.wait_ge(self.normed_ready, t + (RING + 1))
            pe.wait_ge(self.lo_ready, t + 1)
            for k in range(KD):
                turn = pe.transpose(psum[:, s % 2, k, :], self.normed[:, s % 2, k * P:(k + 1) * P], self.ident[:])
            turn.then_inc(self.turned, 1)

        def quarter(i, s):
            cols = bass.ds(i * BANK, BANK)
            for k in range(s * KD // RING, (s + 1) * KD // RING):
                last = split_products(pe, banks[:, bass.ds(i, 1), :], ws.hi[:, 0, k], ws.lo[:, 0, k],
                                      self.feat_hi[:, k, cols], self.feat_lo[:, k, cols], k == 0, k == KD - 1)
            if s == RING - 1:
                last.then_inc(ws.chunk_done, 1)

        pe.sem_inc(self.turned, 2)
        ws.start(pe)
        pe.wait_ge(self.const_ready, 5)
        for s in range(RING):
            turn_tile(0, s)
        with pe.Fori(1, TILES // RING) as i:
            pe.wait_ge(ws.lo_ready, 1)
            pe.wait_ge(self.lo_ready, i * RING + 2)
            for s in range(RING):
                turn_tile(i, s)
                quarter(i - 1, s)
        pe.wait_ge(self.lo_ready, TILES + 2)
        for s in range(RING):
            quarter(TILES // RING - 1, s)


class WeightStream:

    def __init__(self, m, k):
        self.raw = m.sb("w_raw", [P, 2, k, P])
        self.hi = m.sb("w_hi", [P, 2, k, P], F32R)
        self.lo = m.sb("w_lo", [P, 2, k, P], F32R)
        self.raw_in = [m.sem("w_raw_in0"), m.sem("w_raw_in1")]
        self.raw_free = m.sem("w_raw_free")
        self.hi_ready = m.sem("w_hi_ready")
        self.lo_ready = m.sem("w_lo_ready")
        self.chunk_done = m.sem("w_chunk_done")

    def load(self, sync, weights, s, n, columns):
        sync.wait_ge(self.raw_free, n + 1)
        sync.dma_start(self.raw[:, s], weights.rearrange("(k p) n -> p k n", p=P)[:, :, columns])\
            .then_inc(self.raw_in[s], 16)

    def start(self, pe):
        pe.sem_inc(self.chunk_done, 2 * CHUNKS)

    def wait_chunk(self, engine, n, c):
        engine.wait_ge(self.chunk_done, n * CHUNKS + (2 * CHUNKS + c + 1))

    def vector(self, dve, s, uses, n):
        dve.wait_ge(self.raw_in[s], uses * 16 + 16)
        dve.wait_ge(self.chunk_done, n * CHUNKS + CHUNKS)
        dve.tensor_copy(self.hi[:, s], self.raw[:, s]).then_inc(self.hi_ready, 1)
        dve.wait_ge(self.hi_ready, n + 1)
        dve.tensor_tensor(self.lo[:, s], self.raw[:, s], self.hi[:, s].bitcast(F32), ALU.subtract)\
            .then_inc(self.lo_ready, 1)
        dve.wait_ge(self.lo_ready, n + 1)
        dve.sem_inc(self.raw_free, 1)


def split_products(pe, out, w_hi, w_lo, x_hi, x_lo, first, last):
    pe.matmul(out, w_hi, x_hi, start=first, stop=False)
    pe.matmul(out, w_lo, x_hi, start=False, stop=False)
    return pe.matmul(out, w_hi, x_lo, start=False, stop=last)


def stage_project_in(nc, x, gain, w_in, qkv, u_scratch, gate_scratch, bases):
    with ExitStack() as ctx:
        m = Pool(nc, ctx, "pi")
        nt = NormTranspose(m, x, gain, bases.memory[:].rearrange("p (s d) -> p s d", s=RING))
        bases.enter(m, nt.normed[:].rearrange("p s d -> p (s d)"))
        ws = WeightStream(m, KD)
        rows_out = m.sb("rows_out", [P, 2, TOK])
        banks = m.psum("banks", [P, 8, BANK])
        turn_psum = banks[:, 4:8, :].rearrange("p (s b) (k t) -> p s (b k) t", s=2, t=P)
        chunk_free = m.sem("chunk_free")
        stored = [m.sem("stored0"), m.sem("stored1")]
        n_qkv, n_u, n_gate = qkv.shape[0] // P, SSM // P, 2 * D // P
        parts = [(0, n_qkv, qkv, "plain"), (n_qkv, n_u, u_scratch, "by chunk"),
                 (n_qkv + n_u, n_gate, gate_scratch, "sigmoid")]
        n_blocks = n_qkv + n_u + n_gate
        block = ctx.enter_context(nc.Block())

        @block.gpsimd
        def _(pool):
            nt.gpsimd(pool)
            pool.wait_ge(nt.normed_ready, TILES + RING)
            bases.compute(pool)

        @block.sync
        def _(sync):
            nt.load(sync, ws, [(s, w_in, slice(s * P, (s + 1) * P)) for s in range(2)])
            sync.wait_ge(nt.turned, TILES + 2)
            bases.load(nc, sync)
            with sync.Fori(1, n_blocks // 2) as i:
                for s in range(2):
                    ws.load(sync, w_in, s, i * 2 + s, bass.ds((i * 2 + s) * P, P))

        @block.vector
        def _(dve):
            nt.vector(dve, turn_psum, ws)
            bases.invert(dve)
            with dve.Fori(1, n_blocks // 2) as i:
                for s in range(2):
                    ws.vector(dve, s, i, i * 2 + s)

        @block.tensor
        def _(pe):
            def product(i, s):
                b = i * 2 + s
                pe.wait_ge(ws.lo_ready, b + 1)
                for c in range(CHUNKS):
                    pe.wait_ge(chunk_free, b * CHUNKS + c + 1)
                    for k in range(KD):
                        cols = slice(c * BANK, (c + 1) * BANK)
                        last = split_products(pe, banks[:, s * CHUNKS + c, :], ws.hi[:, s, k], ws.lo[:, s, k],
                                              nt.feat_hi[:, k, cols], nt.feat_lo[:, k, cols],
                                              k == 0, k == KD - 1)
                    last.then_inc(ws.chunk_done, 1)

            nt.tensor(pe, turn_psum, banks, ws)
            product(0, 1)
            with pe.Fori(1, n_blocks // 2) as i:
                for s in range(2):
                    product(i, s)

        @block.scalar
        def _(act):
            nt.scalar(act, turn_psum)
            act.sem_inc(chunk_free, 2 * CHUNKS)
            for s in range(2):
                act.sem_inc(stored[s], 16)
            for first, count, dest, kind in parts:
                dest_rows = dest.rearrange("(b p) t -> b p t", p=P)
                with act.Fori(0, count // 2) as i:
                    for s in range(2):
                        b = i * 2 + s
                        uses = i + first // 2
                        act.wait_ge(stored[s], uses * 16 + 16)
                        for c in range(CHUNKS):
                            ws.wait_chunk(act, b + first, c)
                            if kind == "by chunk":
                                out = rows_out[:, s, :].rearrange("p (l j) -> p j l", l=SSM_L)
                                n = BANK // SSM_L
                                out = out[:, c * n:(c + 1) * n, :]
                                src = banks[:, s * CHUNKS + c, :].rearrange("p (j l) -> p j l", l=SSM_L)
                            else:
                                out = rows_out[:, s, c * BANK:(c + 1) * BANK]
                                src = banks[:, s * CHUNKS + c, :]
                            func = ACT.Sigmoid if kind == "sigmoid" else ACT.Copy
                            act.activation(out, src, func).then_inc(chunk_free, 1)
                        act.wait_ge(chunk_free, (b + first) * CHUNKS + 3 * CHUNKS)
                        act.dma_start(dest_rows[b], rows_out[:, s, :]).then_inc(stored[s], 16)
            for s in range(2):
                act.wait_ge(stored[s], (n_blocks // 2) * 16 + 16)


def stage_gate_up(nc, x_mid, gain, w_gate, w_up, conv_w, conv_b, f_scratch):
    with ExitStack() as ctx:
        m = Pool(nc, ctx, "gu")
        nt = NormTranspose(m, x_mid, gain)
        ws = WeightStream(m, KD)
        gate = m.sb("gate", [P, TOK + 2])
        conv = m.sb("conv", [P, TOK])
        taps = m.sb("taps", [P, 4, KF])
        banks = m.psum("banks", [P, 8, BANK])
        turn_psum = banks[:, 4:8, :].rearrange("p (s b) (k t) -> p s (b k) t", s=2, t=P)
        taps_in = m.sem("taps_in")
        edges_zero = m.sem("edges_zero")
        gate_read = m.sem("gate_read")
        up_read = m.sem("up_read")
        gate_free = m.sem("gate_free")
        tap = m.sem("tap")
        gelu_done = m.sem("gelu_done")
        stored = m.pool_dma_sem("stored")
        conv_free = m.sem("conv_free")
        f_rows = f_scratch.rearrange("(b p) t -> b p t", p=P)
        block = ctx.enter_context(nc.Block())

        @block.gpsimd
        def _(pool):
            pool.memset(gate[:, 0:1], 0.0).then_inc(edges_zero, 1)
            pool.memset(gate[:, TOK + 1:TOK + 2], 0.0).then_inc(edges_zero, 1)
            nt.gpsimd(pool)

        @block.sync
        def _(sync):
            nt.load(sync, ws, [(s, weights, slice(0, P)) for s, weights in enumerate((w_gate, w_up))])
            with sync.Fori(1, KF) as i:
                ws.load(sync, w_gate, 0, i * 2, bass.ds(i * P, P))
                ws.load(sync, w_up, 1, i * 2 + 1, bass.ds(i * P, P))

        @block.tensor
        def _(pe):
            def product(i, s):
                pe.wait_ge(ws.lo_ready, i * 2 + s + 1)
                for c in range(CHUNKS):
                    pe.wait_ge(up_read if s else gate_read, i * CHUNKS + c + 1)
                    for k in range(KD):
                        cols = slice(c * BANK, (c + 1) * BANK)
                        last = split_products(pe, banks[:, s * CHUNKS + c, :], ws.hi[:, s, k], ws.lo[:, s, k],
                                              nt.feat_hi[:, k, cols], nt.feat_lo[:, k, cols],
                                              k == 0, k == KD - 1)
                    last.then_inc(ws.chunk_done, 1)

            nt.tensor(pe, turn_psum, banks, ws)
            product(0, 1)
            with pe.Fori(1, KF) as i:
                for s in range(2):
                    product(i, s)

        @block.scalar
        def _(act):
            with nc.allow_non_contiguous_dma(reason="small"):
                for j in range(3):
                    act.dma_start(taps[:, j, :], conv_w[j].rearrange("(b p) -> p b", p=P)).then_inc(taps_in, 16)
                act.dma_start(taps[:, 3, :], conv_b.rearrange("(b p) -> p b", p=P)).then_inc(taps_in, 16)
            nt.scalar(act, turn_psum)
            act.sem_inc(gate_read, CHUNKS)
            act.sem_inc(gelu_done, 1)
            act.wait_ge(taps_in, 64)
            with act.Fori(0, KF) as i:
                act.wait_ge(gate_free, i + 1)
                for c in range(CHUNKS):
                    ws.wait_chunk(act, i * 2, c)
                    act.activation(gate[:, 1 + c * BANK:1 + (c + 1) * BANK], banks[:, c, :], ACT.Copy)\
                        .then_inc(gate_read, 1)
                act.wait_ge(tap, i * 3 + 3)
                act.activation(conv[:], conv[:], ACT.Gelu_apprx_tanh, bias=taps[:, 3, bass.ds(i, 1)])\
                    .then_inc(gelu_done, 1)

        @block.vector
        def _(dve):
            nt.vector(dve, turn_psum, ws)
            dve.sem_inc(gate_free, 1)
            dve.sem_inc(up_read, CHUNKS)
            dve.wait_ge(taps_in, 64)
            dve.wait_ge(edges_zero, 2)
            dve.sem_inc(conv_free, 1)

            def finish(i):
                dve.wait_ge(gate_read, i * CHUNKS + 2 * CHUNKS)
                dve.wait_ge(conv_free, i + 1)
                dve.tensor_scalar(conv[:], gate[:, 0:TOK], taps[:, 0, bass.ds(i, 1)], None,
                                  ALU.mult).then_inc(tap, 1)
                dve.wait_ge(tap, i * 3 + 1)
                dve.scalar_tensor_tensor(out=conv[:], in0=gate[:, 1:TOK + 1], scalar=taps[:, 1, bass.ds(i, 1)],
                                         in1=conv[:], op0=ALU.mult, op1=ALU.add).then_inc(tap, 1)
                dve.wait_ge(tap, i * 3 + 2)
                dve.scalar_tensor_tensor(out=conv[:], in0=gate[:, 2:TOK + 2], scalar=taps[:, 2, bass.ds(i, 1)],
                                         in1=conv[:], op0=ALU.mult, op1=ALU.add).then_inc(tap, 1)

            def times_up(i):
                dve.wait_ge(gelu_done, i + 2)
                for c in range(CHUNKS):
                    cols = slice(c * BANK, (c + 1) * BANK)
                    ws.wait_chunk(dve, i * 2 + 1, c)
                    dve.tensor_tensor(conv[:, cols], conv[:, cols], banks[:, CHUNKS + c, :], ALU.mult)\
                        .then_inc(up_read, 1)

            with dve.Fori(0, KF - 1) as i:
                ws.vector(dve, 0, i + 1, i * 2 + 2)
                finish(i)
                dve.wait_ge(tap, i * 3 + 3)
                dve.sem_inc(gate_free, 1)
                ws.vector(dve, 1, i + 1, i * 2 + 3)
                times_up(i)
            finish(KF - 1)
            times_up(KF - 1)

        @block.gpsimd
        def _(pool):
            with pool.Fori(0, KF) as i:
                pool.wait_ge(up_read, i * CHUNKS + 2 * CHUNKS)
                pool.dma_start(f_rows[i], conv[:]).then_inc(stored, 16)
                pool.wait_ge(stored, i * 16 + 16)
                pool.sem_inc(conv_free, 1)


class PostNorm:

    def __init__(self, m, residual, gain, out):
        self.residual = residual.rearrange("(t p) d -> t p d", p=P)
        self.out = out.rearrange("(t p) d -> t p d", p=P)
        self.gain = gain
        self.gain_rows = m.sb("gain_rows", [P, 2, BANK])
        self.rows = m.sb("rows", [P, 2, 2, BANK])
        self.scaled = m.sb("scaled", [P, 2, BANK])
        self.stat = m.sb("stat", [P, 2, 6])
        self.consts = m.sb("consts", [P, 3])
        self.gain_in = m.sem("gain_in")
        self.rows_in = [m.sem("rows_in0"), m.sem("rows_in1")]
        self.square_sum = m.sem("square_sum")
        self.mean_square = m.sem("mean_square")
        self.const_ready = m.sem("const_ready")
        self.rstd = m.sem("rstd")
        self.scaled_ready = m.sem("scaled_ready")
        self.sum_ready = m.sem("sum_ready")
        self.stored = m.pool_dma_sem("stored")
        self.rows_free = m.sem("rows_free")

    def load_gain(self, sync):
        sync.dma_start(self.gain_rows[:].rearrange("p a b -> p (a b)"), row_broadcast(self.gain))\
            .then_inc(self.gain_in, 16)
        sync.sem_inc(self.rows_free, 2)

    def load(self, sync, t, s):
        sync.wait_ge(self.rows_free, t + 1)
        sync.dma_start(self.rows[:, s].rearrange("p a b -> p (a b)"), self.residual[t]).then_inc(self.rows_in[s], 16)

    def scalar(self, act, t, s, halves):
        act.wait_ge(self.sum_ready, t + 1)
        for h in range(2):
            act.activation(self.scaled[:, h, :], halves[h], ACT.Square,
                           accum_out=self.stat[:, s, h:h + 1]).then_inc(self.square_sum, 1)

    def inverse_root(self, pool, t, s):
        stat = self.stat
        pool.wait_ge(self.square_sum, t * 2 + 2)
        pool.tensor_tensor(stat[:, s, 2:3], stat[:, s, 0:1], stat[:, s, 1:2], ALU.add).then_inc(self.mean_square, 1)
        pool.wait_ge(self.mean_square, t * 3 + 1)
        pool.tensor_tensor(stat[:, s, 3:4], stat[:, s, 2:3], self.consts[:, 0:1], ALU.mult)\
            .then_inc(self.mean_square, 1)
        pool.wait_ge(self.mean_square, t * 3 + 2)
        pool.tensor_tensor(stat[:, s, 4:5], stat[:, s, 3:4], self.consts[:, 1:2], ALU.add)\
            .then_inc(self.mean_square, 1)
        pool.wait_ge(self.mean_square, t * 3 + 3)
        pool.tensor_tensor(stat[:, s, 5:6], stat[:, s, 4:5], self.consts[:, 2:3], ALU.pow).then_inc(self.rstd, 1)

    def gpsimd_start(self, pool):
        rms_constants(pool, self.consts, self.const_ready)
        pool.wait_ge(self.const_ready, 3)

    def vector(self, dve, t, s, uses, halves):
        dve.wait_ge(self.rstd, t + 1)
        for h in range(2):
            dve.scalar_tensor_tensor(out=self.scaled[:, h, :], in0=halves[h], scalar=self.stat[:, s, 5:6],
                                     in1=self.gain_rows[:, h, :], op0=ALU.mult, op1=ALU.mult)\
                .then_inc(self.scaled_ready, 1)
        dve.wait_ge(self.scaled_ready, t * 2 + 2)
        dve.wait_ge(self.rows_in[s], uses * 16 + 16)
        dve.tensor_tensor(self.rows[:, s], self.rows[:, s], self.scaled[:], ALU.add).then_inc(self.sum_ready, 1)

    def vector_start(self, dve):
        dve.wait_ge(self.gain_in, 16)
        dve.sem_inc(self.sum_ready, 1)

    def store(self, pool, t, s):
        pool.wait_ge(self.sum_ready, t + 2)
        pool.dma_start(self.out[t], self.rows[:, s].rearrange("p a b -> p (a b)")).then_inc(self.stored, 16)
        pool.wait_ge(self.stored, t * 16 + 16)
        pool.sem_inc(self.rows_free, 1)


def stage_down(nc, f_scratch, w_down, gain, x_mid, out):
    with ExitStack() as ctx:
        m = Pool(nc, ctx, "dn")
        pn = PostNorm(m, x_mid, gain, out)
        KH = KF // 2
        PAIRS = KF // 2
        RAW = 4
        w_raw = m.sb("w_raw", [P, RAW, 2, BANK])
        w_hi = m.sb("w_hi", [P, KF, BANK], F32R)
        w_lo = m.sb("w_lo", [P, KF, BANK], F32R)
        f_raw = m.sb("f_raw", [P, 2, KH, P])
        f_hi = m.sb("f_hi", [P, 2, KF, P], F32R)
        f_lo = m.sb("f_lo", [P, 2, KF, P], F32R)
        y_first = m.sb("y_first", [P, TILES, BANK])
        y = m.psum("y", [P, 2, BANK])
        w_in = [m.pool_dma_sem(f"w_in{s}") for s in range(RAW)]
        w_hi_ready = m.sem("w_hi_ready")
        w_lo_ready = m.sem("w_lo_ready")
        f_in = [m.sem(f"f_in{h}") for h in range(2)]
        f_hi_ready = m.sem("f_hi_ready")
        f_lo_ready = m.sem("f_lo_ready")
        y_done = m.sem("y_done")
        y_copied = m.sem("y_copied")
        y_free = m.sem("y_free")
        w_used = m.sem("w_used")
        f_tiles = f_scratch.rearrange("(h k p) (t c) -> t h p k c", p=P, h=2, c=P)
        w_pairs = w_down.rearrange("(a k p) (h n) -> h a p k n", k=2, p=P, h=2)
        block = ctx.enter_context(nc.Block())


        @block.sync
        def _(sync):
            def load_tile(half, t):
                for h in range(2):
                    sync.wait_ge(f_lo_ready, t * 2 + (half * TILES * 2 + h + 1))
                    sync.dma_start(f_raw[:, h], f_tiles[t, h]).then_inc(f_in[h], 16)

            load_tile(0, 0)
            pn.load_gain(sync)
            with sync.Fori(1, TILES) as t:
                load_tile(0, t)
            load_tile(1, 0)
            load_tile(1, 1)
            with sync.Fori(1, TILES // 2) as i:
                for s in range(2):
                    load_tile(1, i * 2 + s)
                    pn.load(sync, i * 2 + (s - 2), s)
            for s in range(2):
                pn.load(sync, TILES - 2 + s, s)

        @block.gpsimd
        def _(pool):
            for g in range(2 * PAIRS):
                if g >= RAW:
                    pool.wait_ge(w_lo_ready, g - RAW + 1)
                pool.dma_start(w_raw[:, g % RAW], w_pairs[g // PAIRS, g % PAIRS]).then_inc(w_in[g % RAW], 16)
            pn.gpsimd_start(pool)
            with pool.Fori(0, TILES // 2) as i:
                for s in range(2):
                    pn.inverse_root(pool, i * 2 + s, s)
                    pn.store(pool, i * 2 + s, s)

        @block.tensor
        def _(pe):
            def tile(i, s, half, first=False, last=False):
                n = i * 2 + (half * TILES + s)
                pe.wait_ge(y_free, n + 1)
                for k in range(KF):
                    if k % KH == 0:
                        pe.wait_ge(f_lo_ready, n * 2 + (k // KH + 3))
                    if first and k % 2 == 0:
                        pe.wait_ge(w_lo_ready, half * PAIRS + k // 2 + 1)
                    done = split_products(pe, y[:, s], f_hi[:, s, k], f_lo[:, s, k],
                                          w_hi[:, k], w_lo[:, k], k == 0, k == KF - 1)
                    if last and k % 2 and k < KF - 1:
                        done.then_inc(w_used, 1)
                done.then_inc(y_done, 1)

            for half in range(2):
                tile(0, 0, half, first=True)
                tile(0, 1, half)
                with pe.Fori(1, TILES // 2 - 1) as i:
                    for s in range(2):
                        tile(i, s, half)
                tile(TILES // 2 - 1, 0, half)
                tile(TILES // 2 - 1, 1, half, last=half == 0)

        @block.scalar
        def _(act):
            def split_hi(i, s, halves=range(2)):
                n = i * 2 + s
                for h in halves:
                    act.wait_ge(y_done, n + 1)
                    act.wait_ge(f_in[h], n * 16 + 16)
                    act.activation(f_hi[:, s, h * KH:(h + 1) * KH], f_raw[:, h], ACT.Copy)\
                        .then_inc(f_hi_ready, 1)

            def split_weights_hi(half, pairs):
                for a in pairs:
                    g = half * PAIRS + a
                    act.wait_ge(w_in[g % RAW], g // RAW * 16 + 16)
                    if half and a < PAIRS - 1:
                        act.wait_ge(w_used, a + 1)
                    elif half:
                        act.wait_ge(y_done, TILES + 2)
                    act.activation(w_hi[:, 2 * a:2 * a + 2], w_raw[:, g % RAW], ACT.Copy).then_inc(w_hi_ready, 1)

            def norm(i, s):
                t = i * 2 + s
                act.wait_ge(y_done, t + (TILES + 3))
                pn.scalar(act, t, s, [y_first[:, bass.ds(t, 1), :], y[:, s]])

            act.sem_inc(y_done, 2)
            split_hi(0, 0, [0])
            split_weights_hi(0, range(0, 2))
            split_hi(0, 0, [1])
            split_weights_hi(0, range(2, PAIRS))
            split_hi(0, 1)
            with act.Fori(1, TILES // 2) as i:
                for s in range(2):
                    split_hi(i, s)
            split_hi(TILES // 2, 0)
            split_weights_hi(1, range(PAIRS))
            split_hi(TILES // 2, 1)
            with act.Fori(0, TILES // 2 - 1) as i:
                for s in range(2):
                    norm(i, s)
                    split_hi(i + (TILES // 2 + 1), s)
            for s in range(2):
                norm(TILES // 2 - 1, s)

        @block.vector
        def _(dve):
            def split_lo(i, s, halves=range(2)):
                n = i * 2 + s
                for h in halves:
                    dve.wait_ge(f_hi_ready, n * 2 + h + 1)
                    part = slice(h * KH, (h + 1) * KH)
                    dve.tensor_tensor(f_lo[:, s, part], f_raw[:, h], f_hi[:, s, part].bitcast(F32),
                                      ALU.subtract).then_inc(f_lo_ready, 1)

            def split_weights_lo(half, pairs):
                for a in pairs:
                    g = half * PAIRS + a
                    dve.wait_ge(w_hi_ready, g + 1)
                    dve.tensor_tensor(w_lo[:, 2 * a:2 * a + 2], w_raw[:, g % RAW],
                                      w_hi[:, 2 * a:2 * a + 2].bitcast(F32), ALU.subtract).then_inc(w_lo_ready, 1)

            def keep(i, s):
                t = i * 2 + s
                dve.wait_ge(y_done, t + 3)
                dve.tensor_copy(y_first[:, bass.ds(t, 1), :], y[:, s:s + 1]).then_inc(y_copied, 1)
                dve.wait_ge(y_copied, t + 1)
                dve.sem_inc(y_free, 1)

            def finish(i, s):
                t = i * 2 + s
                pn.vector(dve, t, s, i, [y_first[:, bass.ds(t, 1), :], y[:, s]])
                dve.sem_inc(y_free, 1)

            dve.sem_inc(f_lo_ready, 2)
            dve.sem_inc(y_free, 2)
            split_lo(0, 0, [0])
            split_weights_lo(0, range(0, 2))
            split_lo(0, 0, [1])
            split_weights_lo(0, range(2, PAIRS))
            split_lo(0, 1)
            pn.vector_start(dve)
            with dve.Fori(0, TILES // 2 - 1) as i:
                for s in range(2):
                    keep(i, s)
                    split_lo(i + 1, s)
            keep(TILES // 2 - 1, 0)
            split_lo(TILES // 2, 0)
            split_weights_lo(1, range(PAIRS))
            keep(TILES // 2 - 1, 1)
            split_lo(TILES // 2, 1)
            with dve.Fori(0, TILES // 2 - 1) as i:
                for s in range(2):
                    finish(i, s)
                    split_lo(i + (TILES // 2 + 1), s)
            for s in range(2):
                finish(TILES // 2 - 1, s)


def stage_branches(nc, attn_scratch, y_scratch, gate_scratch, w_glu, b_glu, w_attn, w_ssm, merged_scratch):
    with ExitStack() as ctx:
        m = Pool(nc, ctx, "br")
        K = SSM // P
        ws = WeightStream(m, K)
        attn_hi = m.sb("attn_hi", [P, K, TOK], F32R)
        attn_lo = m.sb("attn_lo", [P, K, TOK], F32R)
        y = m.sb("y", [P, K, TOK])
        y_hi = m.sb("y_hi", [P, K, TOK], F32R)
        y_lo = m.sb("y_lo", [P, K, TOK], F32R)
        rows = m.sb("rows", [P, 4, TOK])
        bias = m.sb("bias", [P, K])
        banks = m.psum("banks", [P, 8, BANK])
        bias_in = m.sem("bias_in")
        y_in = [m.sem(f"y_in{c}") for c in range(CHUNKS)]
        rows_in = [m.sem(f"rows_in{k}") for k in range(4)]
        hi_ready = m.sem("hi_ready")
        lo_ready = m.sem("lo_ready")
        sigmoid_ready = m.sem("sigmoid_ready")
        glu_done = m.sem("glu_done")
        chunk_free = m.sem("chunk_free")
        gated = m.sem("gated")
        merged_ready = m.sem("merged_ready")
        stored = m.sem("stored")
        rows_free = m.sem("rows_free")
        gates_in = [[m.pool_dma_sem(f"gates_in{s}{h}") for h in range(2)] for s in range(2)]
        gates = gate_scratch.rearrange("(h b p) t -> h b p t", h=2, p=P)
        merged_rows = merged_scratch.rearrange("(b p) t -> b p t", p=P)
        n_out = D // P
        by_token = "p (j l) -> p l j"
        by_chunk = "p (l j) -> p l j"
        block = ctx.enter_context(nc.Block())

        @block.sync
        def _(sync):
            with nc.allow_non_contiguous_dma(reason="512 bias values"):
                sync.dma_start(bias[:], b_glu.rearrange("(k p) -> p k", p=P)).then_inc(bias_in, 16)
            ws.load(sync, w_glu, 0, 0, slice(0, P))
            for c in range(CHUNKS):
                cols = slice(c * BANK, (c + 1) * BANK)
                sync.dma_start(y[:, :, cols], y_scratch.rearrange("(k p) t -> p k t", p=P)[:, :, cols])\
                    .then_inc(y_in[c], 16)
            ws.load(sync, w_glu, 1, 1, slice(P, 2 * P))
            for k in range(K):
                sync.dma_start(rows[:, k], attn_scratch[k * P:(k + 1) * P, :]).then_inc(rows_in[k], 16)
            with sync.Fori(1, K // 2) as i:
                for s in range(2):
                    ws.load(sync, w_glu, s, i * 2 + s, bass.ds((i * 2 + s) * P, P))
            with sync.Fori(0, n_out) as i:
                ws.load(sync, w_attn, 0, i * 2 + K, bass.ds(i * P, P))
                ws.load(sync, w_ssm, 1, i * 2 + K + 1, bass.ds(i * P, P))

        @block.gpsimd
        def _(pool):
            pool.wait_ge(lo_ready, CHUNKS + K)
            with pool.Fori(0, n_out // 2) as i:
                for s in range(2):
                    pool.wait_ge(rows_free, i * 2 + s + 1)
                    for h in range(2):
                        pool.dma_start(rows[:, 2 * s + h], gates[h, i * 2 + s]).then_inc(gates_in[s][h], 16)

        @block.tensor
        def _(pe):
            ws.start(pe)

            def product(b, s, x_hi, x_lo, first=False):
                pe.wait_ge(ws.lo_ready, b + 1)
                for c in range(CHUNKS):
                    if first:
                        pe.wait_ge(lo_ready, c + 1)
                    pe.wait_ge(chunk_free, b * CHUNKS + c + 1)
                    for k in range(K):
                        cols = slice(c * BANK, (c + 1) * BANK)
                        last = split_products(pe, banks[:, s * CHUNKS + c, :], ws.hi[:, s, k], ws.lo[:, s, k],
                                              x_hi[:, k, cols], x_lo[:, k, cols], k == 0, k == K - 1)
                    last.then_inc(ws.chunk_done, 1)

            product(0, 0, y_hi, y_lo, first=True)
            product(1, 1, y_hi, y_lo)
            with pe.Fori(1, K // 2) as i:
                for s in range(2):
                    product(i * 2 + s, s, y_hi, y_lo)
            pe.wait_ge(lo_ready, CHUNKS + K)
            product(K, 0, attn_hi, attn_lo)
            pe.wait_ge(lo_ready, CHUNKS + 2 * K)
            product(K + 1, 1, y_hi, y_lo)
            with pe.Fori(1, n_out) as i:
                product(i * 2 + K, 0, attn_hi, attn_lo)
                product(i * 2 + K + 1, 1, y_hi, y_lo)

        @block.scalar
        def _(act):
            act.wait_ge(bias_in, 16)
            for c in range(CHUNKS):
                cols = slice(c * BANK, (c + 1) * BANK)
                act.wait_ge(y_in[c], 16)
                act.activation(y_hi[:, :, cols], y[:, :, cols], ACT.Copy).then_inc(hi_ready, 1)
            for k in range(K):
                act.wait_ge(rows_in[k], 16)
                act.activation(attn_hi[:, k], rows[:, k], ACT.Copy).then_inc(hi_ready, 1)
            for b in range(K):
                for c in range(CHUNKS):
                    ws.wait_chunk(act, b, c)
                    bank = banks[:, b % 2 * CHUNKS + c, :]
                    act.activation(bank, bank, ACT.Sigmoid, bias=bias[:, b:b + 1]).then_inc(sigmoid_ready, 1)
            for k in range(K):
                act.wait_ge(glu_done, K * CHUNKS)
                act.activation(y_hi[:, k].rearrange(by_token, l=SSM_L), y[:, k].rearrange(by_chunk, l=SSM_L),
                               ACT.Copy).then_inc(hi_ready, 1)
            with act.Fori(0, n_out // 2) as i:
                for s in range(2):
                    n = i * 2 + s
                    act.wait_ge(merged_ready, n + 1)
                    act.dma_start(merged_rows[n], rows[:, 2 * s]).then_inc(stored, 16)
                    act.wait_ge(stored, n * 16 + 16)
                    act.sem_inc(rows_free, 1)

        @block.vector
        def _(dve):
            dve.sem_inc(ws.raw_free, 2)
            dve.sem_inc(chunk_free, 2 * CHUNKS)
            dve.sem_inc(rows_free, 2)
            ws.vector(dve, 0, 0, 0)
            for c in range(CHUNKS):
                cols = slice(c * BANK, (c + 1) * BANK)
                dve.wait_ge(hi_ready, c + 1)
                dve.tensor_tensor(y_lo[:, :, cols], y[:, :, cols], y_hi[:, :, cols].bitcast(F32), ALU.subtract)\
                    .then_inc(lo_ready, 1)
            ws.vector(dve, 1, 0, 1)
            for k in range(K):
                dve.wait_ge(hi_ready, CHUNKS + k + 1)
                dve.tensor_tensor(attn_lo[:, k], rows[:, k], attn_hi[:, k].bitcast(F32), ALU.subtract)\
                    .then_inc(lo_ready, 1)
            for b in range(K):
                for c in range(CHUNKS):
                    dve.wait_ge(sigmoid_ready, b * CHUNKS + c + 1)
                    cols = slice(c * BANK, (c + 1) * BANK)
                    dve.tensor_tensor(y[:, b, cols], y[:, b, cols], banks[:, b % 2 * CHUNKS + c, :], ALU.mult)\
                        .then_inc(glu_done, 1)
                    dve.wait_ge(glu_done, b * CHUNKS + c + 1)
                    dve.sem_inc(chunk_free, 1)
                ws.vector(dve, b % 2, b // 2 + 1, b + 2)
            for k in range(K):
                dve.wait_ge(hi_ready, CHUNKS + K + k + 1)
                dve.tensor_tensor(y_lo[:, k].rearrange(by_token, l=SSM_L), y[:, k].rearrange(by_chunk, l=SSM_L),
                                  y_hi[:, k].bitcast(F32).rearrange(by_token, l=SSM_L), ALU.subtract)\
                    .then_inc(lo_ready, 1)

            def merge(i, s, last=False):
                n = i * 2 + s
                for h in range(2):
                    dve.wait_ge(gates_in[s][h], i * 16 + 16)
                    for c in range(CHUNKS):
                        ws.wait_chunk(dve, n * 2 + (K + h), c)
                        cols = slice(c * BANK, (c + 1) * BANK)
                        dve.tensor_tensor(rows[:, 2 * s + h, cols], rows[:, 2 * s + h, cols],
                                          banks[:, h * CHUNKS + c, :], ALU.mult).then_inc(gated, 1)
                        dve.wait_ge(gated, n * (2 * CHUNKS) + (h * CHUNKS + c + 1))
                        dve.sem_inc(chunk_free, 1)
                    if not last:
                        ws.vector(dve, h, n + (K // 2 + 1), n * 2 + (K + 2 + h))
                dve.tensor_tensor(rows[:, 2 * s], rows[:, 2 * s], rows[:, 2 * s + 1], ALU.add)\
                    .then_inc(merged_ready, 1)

            with dve.Fori(0, n_out // 2 - 1) as i:
                for s in range(2):
                    merge(i, s)
            merge(n_out // 2 - 1, 0)
            merge(n_out // 2 - 1, 1, last=True)


def stage_out(nc, merged_scratch, w_out, gain, x, x_mid):
    with ExitStack() as ctx:
        m = Pool(nc, ctx, "ou")
        pn = PostNorm(m, x, gain, x_mid)
        w_raw = m.sb("w_raw", [P, KD, D])
        w_hi = m.sb("w_hi", [P, KD, D], F32R)
        w_lo = m.sb("w_lo", [P, KD, D], F32R)
        g_raw = m.sb("g_raw", [P, 2, KD, P])
        g_hi = m.sb("g_hi", [P, 2, KD, P], F32R)
        g_lo = m.sb("g_lo", [P, 2, KD, P], F32R)
        y = m.psum("y", [P, 2, 2, BANK])
        w_in = [m.sem(f"w_in{k}") for k in range(KD)]
        w_hi_ready = m.sem("w_hi_ready")
        w_lo_ready = m.sem("w_lo_ready")
        g_in = [m.sem("g_in0"), m.sem("g_in1")]
        g_hi_ready = m.sem("g_hi_ready")
        g_lo_ready = m.sem("g_lo_ready")
        y_done = m.sem("y_done")
        y_free = m.sem("y_free")
        g_tiles = merged_scratch.rearrange("(k p) (t c) -> t p k c", p=P, c=P)
        w_rows = w_out.rearrange("(k p) n -> k p n", p=P)
        block = ctx.enter_context(nc.Block())

        @block.sync
        def _(sync):
            def load_tile(t, s):
                sync.wait_ge(g_lo_ready, t + 1)
                sync.dma_start(g_raw[:, s], g_tiles[t]).then_inc(g_in[s], 16)

            for s in range(2):
                load_tile(s, s)
            pn.load_gain(sync)
            with sync.Fori(1, TILES // 2) as i:
                for s in range(2):
                    load_tile(i * 2 + s, s)
                    pn.load(sync, i * 2 + (s - 2), s)
            for s in range(2):
                pn.load(sync, TILES - 2 + s, s)

        @block.gpsimd
        def _(pool):
            pn.gpsimd_start(pool)
            with pool.Fori(0, TILES // 2) as i:
                for s in range(2):
                    pn.inverse_root(pool, i * 2 + s, s)
                    pn.store(pool, i * 2 + s, s)

        @block.tensor
        def _(pe):
            def tile(i, s, first=False):
                t = i * 2 + s
                pe.wait_ge(g_lo_ready, t + 3)
                pe.wait_ge(y_free, t + 1)
                for k in range(KD):
                    if first:
                        pe.wait_ge(w_lo_ready, k + 1)
                    for h in range(2):
                        cols = slice(h * BANK, (h + 1) * BANK)
                        done = split_products(pe, y[:, s, h], g_hi[:, s, k], g_lo[:, s, k],
                                              w_hi[:, k, cols], w_lo[:, k, cols], k == 0, k == KD - 1)
                done.then_inc(y_done, 1)

            pe.sem_inc(y_done, 2)
            tile(0, 0, first=True)
            tile(0, 1)
            with pe.Fori(1, TILES // 2) as i:
                for s in range(2):
                    tile(i, s)

        @block.scalar
        def _(act):
            def split_hi(i, s):
                act.wait_ge(y_done, i * 2 + s + 1)
                act.wait_ge(g_in[s], i * 16 + 16)
                act.activation(g_hi[:, s], g_raw[:, s], ACT.Copy).then_inc(g_hi_ready, 1)

            def norm(i, s):
                t = i * 2 + s
                act.wait_ge(y_done, t + 3)
                pn.scalar(act, t, s, [y[:, s, 0], y[:, s, 1]])

            for k in range(KD):
                act.dma_start(w_raw[:, k], w_rows[k]).then_inc(w_in[k], 16)
            split_hi(0, 0)
            for k in range(KD):
                act.wait_ge(w_in[k], 16)
                act.activation(w_hi[:, k], w_raw[:, k], ACT.Copy).then_inc(w_hi_ready, 1)
            split_hi(0, 1)
            with act.Fori(0, TILES // 2 - 1) as i:
                for s in range(2):
                    norm(i, s)
                    split_hi(i + 1, s)
            for s in range(2):
                norm(TILES // 2 - 1, s)

        @block.vector
        def _(dve):
            def split_lo(i, s):
                dve.wait_ge(g_hi_ready, i * 2 + s + 1)
                dve.tensor_tensor(g_lo[:, s], g_raw[:, s], g_hi[:, s].bitcast(F32), ALU.subtract)\
                    .then_inc(g_lo_ready, 1)

            def finish(i, s):
                pn.vector(dve, i * 2 + s, s, i, [y[:, s, 0], y[:, s, 1]])
                dve.sem_inc(y_free, 1)

            dve.sem_inc(g_lo_ready, 2)
            dve.sem_inc(y_free, 2)
            split_lo(0, 0)
            for k in range(KD):
                dve.wait_ge(w_hi_ready, k + 1)
                dve.tensor_tensor(w_lo[:, k], w_raw[:, k], w_hi[:, k].bitcast(F32), ALU.subtract)\
                    .then_inc(w_lo_ready, 1)
            split_lo(0, 1)
            pn.vector_start(dve)
            with dve.Fori(0, TILES // 2 - 1) as i:
                for s in range(2):
                    finish(i, s)
                    split_lo(i + 1, s)
            for s in range(2):
                finish(TILES // 2 - 1, s)


class Steps:

    def __init__(self, engine, done):
        self.engine, self.done, self.count = engine, done, 0

    def __call__(self, instruction):
        instruction.then_inc(self.done, 1)
        self.count += 1
        self.engine.wait_ge(self.done, self.count)


def complex_product(step, engine, out, x, y, temp, conjugate=False):
    (out_re, out_im), (x_re, x_im), (y_re, y_im) = out, x, y
    step(engine.tensor_tensor(out_re, x_re, y_re, ALU.mult))
    step(engine.tensor_tensor(temp, x_im, y_im, ALU.mult))
    step(engine.tensor_tensor(out_re, out_re, temp, ALU.add if conjugate else ALU.subtract))
    step(engine.tensor_tensor(out_im, x_re, y_im, ALU.mult))
    step(engine.tensor_tensor(temp, x_im, y_re, ALU.mult))
    step(engine.tensor_tensor(out_im, out_im, temp, ALU.subtract if conjugate else ALU.add))


TWO_PI = 6.283185307179586
ROUND = 1.5 * 2.0 ** 23
LN2 = 0.6931471805599453


def head_bits(x, bits):
    mantissa, exponent = math.frexp(x)
    return math.ldexp(math.floor(mantissa * 2 ** bits), exponent - bits)


def scaled_product(step, engine, out, x, scale, y, temp, kind=ALU.mult):
    step(engine.tensor_scalar(temp, x, scale, None, ALU.mult))
    step(engine.tensor_tensor(out, temp, y, kind))


def reduce_argument(step, engine, out, x, turns, period, temp):
    a = head_bits(period, 8)
    b = head_bits(period - a, 11)
    c = period - a - b
    step(engine.tensor_scalar(turns, x, 1.0 / period, None, ALU.mult))
    step(engine.tensor_scalar(turns, turns, ROUND, None, ALU.add))
    step(engine.tensor_scalar(turns, turns, -ROUND, None, ALU.add))
    scaled_product(step, engine, out, turns, -a, x, temp, ALU.add)
    scaled_product(step, engine, out, turns, -b, out, temp, ALU.add)
    scaled_product(step, engine, out, turns, -c, out, temp, ALU.add)


def horner(step, dve, out, x, coefficients):
    *rest, last = coefficients
    step(dve.tensor_scalar(out, x, last, rest[-1], ALU.mult, ALU.add))
    for c in reversed(rest[:-1]):
        step(dve.tensor_tensor(out, out, x, ALU.mult))
        step(dve.tensor_scalar(out, out, c, None, ALU.add))


QS = GROUPS // 2
LC = SSM_L * SSM_CH
SPAN = 2 * SSM_L - 1
POWERS = SSM_L + 1
SCAN_I = 16
SCAN_J = SSM_J // SCAN_I


class SsmBases:

    def __init__(self, params, memory):
        self.params, self.memory = params, memory
        v = carve(memory, {
            "bbar": (P, (2, 2, QS, SSM_CH)),
            "rising": (P, (2, 2, POWERS, QS)), "falling": (P, (2, 2, POWERS, QS)),
            "leaps": (P, (2, 2, SCAN_I, QS)),
            "bbar_temp": (P, (QS, SSM_CH)), "power_temp": (P, (SSM_L, QS))})
        self.bbar, self.rising, self.falling = v["bbar"], v["rising"], v["falling"]
        self.leaps = [v["leaps"][:, d] for d in range(2)]
        self.bbar_temp, self.power_temp = v["bbar_temp"], v["power_temp"]

    def enter(self, m, temp):
        names = ("lam_re lam_im log_dt dt x em1 turns r scale scale_bits half s c s2 c2 cosm1 a_re a_im am1_re "
                 "den inv co_re co_im t0 t1").split()
        self.op = carve(temp, {**{n: (P, (2, QS)) for n in names}, "b_raw": (P, (2, 2, QS, SSM_CH))})
        self.lam_loaded = m.sem("lam_loaded")
        self.b_loaded = m.sem("b_loaded")
        self.den_ready = m.sem("den_ready")
        self.inv_ready = m.sem("inv_ready")
        self.steps = m.sem("bases_step")

    def load(self, nc, sync):
        op, params = self.op, self.params
        with nc.allow_non_contiguous_dma(reason="2048 values each, once"):
            for d in range(2):
                p_lam_re, p_lam_im, p_log_dt = params[d][:3]
                sync.dma_start(op["lam_re"][:, d], p_lam_re.rearrange("(q e) n -> (e n) q", e=2))\
                    .then_inc(self.lam_loaded, 16)
                sync.dma_start(op["lam_im"][:, d], p_lam_im.rearrange("(q e) n -> (e n) q", e=2))\
                    .then_inc(self.lam_loaded, 16)
                for e in range(2):
                    steps = p_log_dt.rearrange("(a q e) -> e a q", a=1, e=2)[e]
                    sync.dma_start(op["log_dt"][e * SSM_N:(e + 1) * SSM_N, d], steps.broadcast_to([SSM_N, QS]))\
                        .then_inc(self.lam_loaded, 16)
            for d in range(2):
                for r in range(2):
                    sync.dma_start(op["b_raw"][:, d, r], params[d][3 + r].rearrange("(q e) n c -> (e n) q c", e=2))\
                        .then_inc(self.b_loaded, 16)

    def invert(self, dve):
        dve.wait_ge(self.den_ready, 1)
        dve.reciprocal(self.op["inv"], self.op["den"]).then_inc(self.inv_ready, 1)

    def compute(self, engine):
        step = Steps(engine, self.steps)
        op, bbar, rising, falling, leaps = self.op, self.bbar, self.rising, self.falling, self.leaps
        lam_re, lam_im, log_dt, b_raw = op["lam_re"], op["lam_im"], op["log_dt"], op["b_raw"]
        bbar_temp, power_temp = self.bbar_temp, self.power_temp
        scale_int = op["scale_bits"].bitcast(I32)
        for r in range(2):
            step(engine.memset(rising[:, :, r, 0, :], 1.0 - r))
            step(engine.memset(falling[:, :, r, SSM_L, :], 1.0 - r))


        def tt(out, a, b, kind):
            step(engine.tensor_tensor(out, a, b, kind))

        def ts(out, a, x, kind, y=None, kind2=None):
            if y is None:
                step(engine.tensor_scalar(out, a, x, None, kind))
            else:
                step(engine.tensor_scalar(out, a, x, y, kind, kind2))

        def exp_minus_1(out, x):
            ts(op["x"], x, -87.0, ALU.max, 88.0, ALU.min)
            reduce_argument(step, engine, op["r"], op["x"], op["turns"], LN2, op["t1"])
            horner(step, engine, op["t0"], op["r"], [1 / math.factorial(n) for n in range(1, 9)])
            tt(op["t0"], op["t0"], op["r"], ALU.mult)
            ts(op["t1"], op["turns"], 127.0, ALU.add, 2.0 ** 23, ALU.mult)
            step(engine.tensor_copy(scale_int, op["t1"]))
            step(engine.tensor_copy(op["scale"], scale_int.bitcast(F32)))
            tt(op["t0"], op["t0"], op["scale"], ALU.mult)
            ts(op["scale"], op["scale"], -1.0, ALU.add)
            tt(out, op["t0"], op["scale"], ALU.add)

        engine.wait_ge(self.lam_loaded, 16 * 8)
        tt(op["den"], lam_re, lam_re, ALU.mult)
        tt(op["t0"], lam_im, lam_im, ALU.mult)
        tt(op["den"], op["den"], op["t0"], ALU.add)
        engine.sem_inc(self.den_ready, 1)
        exp_minus_1(op["dt"], log_dt)
        step(engine.tensor_copy(op["scale"], scale_int.bitcast(F32)))
        tt(op["dt"], op["t0"], op["scale"], ALU.add)
        tt(op["half"], lam_re, op["dt"], ALU.mult)
        exp_minus_1(op["em1"], op["half"])
        tt(op["x"], lam_im, op["dt"], ALU.mult)
        reduce_argument(step, engine, op["r"], op["x"], op["turns"], TWO_PI, op["t1"])
        ts(op["r"], op["r"], 0.25, ALU.mult)
        tt(op["t0"], op["r"], op["r"], ALU.mult)
        horner(step, engine, op["s"], op["t0"], [1.0, -1 / 6, 1 / 120, -1 / 5040, 1 / 362880])
        tt(op["s"], op["s"], op["r"], ALU.mult)
        horner(step, engine, op["c"], op["t0"], [1.0, -1 / 2, 1 / 24, -1 / 720, 1 / 40320, -1 / 3628800])
        scaled_product(step, engine, op["s2"], op["s"], 2.0, op["c"], op["t1"])
        scaled_product(step, engine, op["c2"], op["s"], -2.0, op["s"], op["t1"])
        ts(op["c2"], op["c2"], 1.0, ALU.add)
        scaled_product(step, engine, op["s"], op["s2"], 2.0, op["c2"], op["t1"])
        scaled_product(step, engine, op["cosm1"], op["s2"], -2.0, op["s2"], op["t1"])
        ts(op["c"], op["cosm1"], 1.0, ALU.add)
        ts(op["t1"], op["em1"], 1.0, ALU.add)
        tt(op["a_re"], op["t1"], op["c"], ALU.mult)
        tt(op["a_im"], op["t1"], op["s"], ALU.mult)
        tt(op["am1_re"], op["em1"], op["c"], ALU.mult)
        tt(op["am1_re"], op["am1_re"], op["cosm1"], ALU.add)
        engine.wait_ge(self.inv_ready, 1)
        tt(op["co_re"], op["am1_re"], lam_re, ALU.mult)
        tt(op["t0"], op["a_im"], lam_im, ALU.mult)
        tt(op["co_re"], op["co_re"], op["t0"], ALU.add)
        tt(op["co_re"], op["co_re"], op["inv"], ALU.mult)
        tt(op["co_im"], op["a_im"], lam_re, ALU.mult)
        tt(op["t0"], op["am1_re"], lam_im, ALU.mult)
        tt(op["co_im"], op["co_im"], op["t0"], ALU.subtract)
        tt(op["co_im"], op["co_im"], op["inv"], ALU.mult)
        engine.wait_ge(self.b_loaded, 16 * 4)
        for d in range(2):
            def over_channels(value):
                return value[:, d].rearrange("p (q a) -> p q a", a=1).broadcast_to([P, QS, SSM_CH])
            complex_product(step, engine, [bbar[:, d, r] for r in range(2)],
                            [over_channels(op["co_re"]), over_channels(op["co_im"])],
                            [b_raw[:, d, r] for r in range(2)], bbar_temp)
        for r, part in enumerate(("a_re", "a_im")):
            step(engine.tensor_copy(rising[:, :, r, 1, :], op[part]))
        for n in (1, 2, 4):
            for d in range(2):
                last = [rising[:, d, r, n:n + 1, :].broadcast_to([P, n, QS]) for r in range(2)]
                complex_product(step, engine, [rising[:, d, r, n + 1:2 * n + 1, :] for r in range(2)], last,
                                [rising[:, d, r, 1:n + 1, :] for r in range(2)], power_temp[:, 0:n])
        for k in range(SSM_L):
            step(engine.tensor_copy(falling[:, :, :, k, :], rising[:, :, :, SSM_L - k, :]))
        for d in range(2):
            for r in range(2):
                step(engine.tensor_copy(leaps[d][:, r, 0, :], rising[:, d, r, SSM_L, :]))
            for n in (1, 2, 4, 8):
                last = [leaps[d][:, r, n - 1:n, :].broadcast_to([P, n, QS]) for r in range(2)]
                complex_product(step, engine, [leaps[d][:, r, n:2 * n, :] for r in range(2)], last,
                                [leaps[d][:, r, 0:n, :] for r in range(2)], power_temp[:, 0:n])


def stage_mixers(nc, qkv, sink, attn_scratch, u_scratch, bases, ssm_d, y_scratch):
    with ExitStack() as ctx:
        m = Pool(nc, ctx, "sm")
        outof = [[m.sb(f"outof{d}{r}", [P, QS, POWERS, SSM_CH]) for r in range(2)] for d in range(2)]
        region = m.sb("region", [P, 2 * 2 * QS * P])
        u_region = m.sb("u_region", [P, GROUPS * SSM_J])
        u = u_region[:].rearrange("p (g j) -> p g j", g=GROUPS)
        into = region[:].rearrange("p (d q e r n) -> p d q e r n", d=2, q=QS, e=2, r=2)
        local = m.sb("local", [P, GROUPS, LC])
        with ExitStack() as part:
            ssm_tables(nc, Pool(nc, part, "st"), bases, ssm_d, u_scratch, u, outof, into, local)
        states = [m.sb(f"states{d}", [P, 2, QS, SSM_J + 1]) for d in range(2)]
        scans = [ChunkScan(m, d, states[d], bases.leaps[d], d == 1) for d in range(2)]
        with ExitStack() as part:
            chunks_into_states(nc, Pool(nc, part, "si"), u, into, states)
        with ExitStack() as part:
            lost = attention_and_scan(nc, Pool(nc, part, "at"), region, u_region, qkv, sink, attn_scratch, scans)
        with ExitStack() as part:
            states_to_outputs(nc, Pool(nc, part, "so"), region, u, lost, u_scratch, y_scratch, outof, local, states)


def ssm_tables(nc, m, bases, ssm_d, u_scratch, u, outof, into, local):
    ident = m.sb("ident", [P, P])
    params, bbar, rising, falling = bases.params, bases.bbar, bases.rising, bases.falling
    late = m.sb("kernels", [P, QS * SPAN * SSM_CH])
    kernels = carve(late, {"kernels": (2 * SSM_CH, (QS, SPAN, SSM_CH))})["kernels"]
    c_rows = carve(late, {"c_rows": (P, (2, 2, 4, 2 * SSM_N))})["c_rows"]
    c_t = m.sb("c_t", [P, 2, 2, QS, SSM_CH])
    d_rows = m.sb("d_rows", [2 * SSM_CH, QS, SSM_CH])
    d_diag = m.sb("d_diag", [2 * SSM_CH, QS, SSM_CH])
    d_mask = m.sb("d_mask", [2 * SSM_CH, SSM_CH])
    b_pair = m.sb("b_pair", [P, 2, 2, QS, 2, SSM_CH])
    b_table = [[m.sb(f"b_table{d}{r}", [P, QS, SSM_L, SSM_CH]) for r in range(2)] for d in range(2)]
    table_temp = m.sb("table_temp", [P, QS, POWERS, SSM_CH])
    banks = m.psum("banks", [P, 8, BANK])
    u_in = [m.sem("u_in0"), m.sem("u_in1")]
    c_loaded = m.sem("c_loaded")
    d_loaded = m.sem("d_loaded")
    ident_ready = m.sem("ident_ready")
    c_turned = m.sem("c_turned")
    c_copied = m.sem("c_copied")
    dve_step = m.sem("dve_step")
    pool_step = m.sem("pool_step")
    b_table_ready = [m.sem("b_table_ready0"), m.sem("b_table_ready1")]
    outof_ready = [m.sem("outof_ready0"), m.sem("outof_ready1")]
    kernels_done = m.sem("kernels_done")
    kernels_copied = m.sem("kernels_copied")
    kernels_ready = m.sem("kernels_ready")
    into_turned = m.sem("into_turned")
    into_copied = m.sem("into_copied")
    local_placed = m.sem("local_placed")
    b_pair_ready = m.sem("b_pair_ready")
    all_groups = [slice(0, GROUPS // 2), slice(GROUPS // 2, GROUPS)]
    PER_BANK = BANK // LC
    B_ON_DVE, OUTOF_ON_DVE = 11, 10

    block = m.ctx.enter_context(nc.Block())

    def place_local(engine, e):
        mine = local.rearrange("p (q e) m -> p e q m", e=2)[:, e]
        engine.wait_ge(kernels_ready, 1)
        for l in range(SSM_L):
            engine.dma_start(mine[l * SSM_CH:(l + 1) * SSM_CH],
                             kernels[e * SSM_CH:(e + 1) * SSM_CH, :, SSM_L - 1 - l:2 * SSM_L - 1 - l, :]
                             .rearrange("c q k o -> c q (k o)")).then_inc(local_placed, 16)
        engine.wait_ge(local_placed, 2 * SSM_L * 16)

    @block.sync
    def _(sync):
        for d in range(2):
            for r in range(2):
                rows = params[d][5 + r].rearrange("(w g) c n -> (g c) w n", w=4)
                for twice in range(2):
                    sync.dma_start(c_rows[:, d, r, :, twice * SSM_N:(twice + 1) * SSM_N], rows).then_inc(c_loaded, 16)
        for e in range(2):
            rows = ssm_d.rearrange("(a q e c) -> e a q c", a=1, e=2, c=SSM_CH)[e]
            sync.dma_start(d_rows[e * SSM_CH:(e + 1) * SSM_CH], rows.broadcast_to([SSM_CH, QS, SSM_CH]))\
                .then_inc(d_loaded, 16)
        sync.wait_ge(c_loaded, 16 * 8)
        load_chunks(sync, u, u_scratch, u_in, 0, all_groups)
        place_local(sync, 0)
        for half in range(2):
            sync.wait_ge(u_in[half], 16 * SSM_L)

    @block.scalar
    def _(act):
        act.wait_ge(c_loaded, 16 * 8)
        load_chunks(act, u, u_scratch, u_in, 1, all_groups)
        act.wait_ge(b_pair_ready, 1)
        for d in range(2):
            for r in range(2):
                for e in range(2):
                    half = slice(e * SSM_N, (e + 1) * SSM_N)
                    act.activation(b_pair[half, d, r, :, e], bbar[half, d, r], ACT.Copy).then_inc(b_pair_ready, 1)
        for d in range(2):
            for r in range(2):
                act.wait_ge(c_turned, d * 2 + r + 1)
                turned = banks[:, d * 2 + r, :].rearrange("p (q e c) -> p q e c", e=2, c=SSM_CH)
                for e in range(2):
                    half = slice(e * SSM_N, (e + 1) * SSM_N)
                    act.activation(c_t[half, d, r], turned[half, :, e], ACT.Copy, scale=1.0 - 2.0 * r)\
                        .then_inc(c_copied, 1)
        for n in range(4):
            for b in range(4):
                act.wait_ge(into_turned, n * 4 + b + 1)
                d, r = n // 2, n % 2
                act.activation(into[:, d, b * 4:(b + 1) * 4, :, r],
                               banks[:, 4 + b, :].rearrange("p (q e n) -> p q e n", q=4, e=2), ACT.Copy)\
                    .then_inc(into_copied, 1)
        place_local(act, 1)

    def tables(engine, step, b_columns, outof_columns):
        def power(table, d, k0, n, r, qs):
            return table[:, d, r, k0:k0 + n, qs].rearrange("p k (q a) -> p q k a", a=1)\
                .broadcast_to([P, qs.stop - qs.start, n, SSM_CH])

        def per_group(values, n, qs):
            return values[:, qs].rearrange("p q (a c) -> p q a c", a=1)\
                .broadcast_to([P, qs.stop - qs.start, n, SSM_CH])

        qs = b_columns
        for d in range(2):
            source, k0 = ((falling, 1), (rising, 0))[d]
            complex_product(step, engine, [b_table[d][r][:, qs] for r in range(2)],
                            [power(source, d, k0, SSM_L, r, qs) for r in range(2)],
                            [per_group(bbar[:, d, r], SSM_L, qs) for r in range(2)], table_temp[:, qs, 0:SSM_L])
            engine.sem_inc(b_table_ready[d], 1)
        qs = outof_columns
        for d in range(2):
            engine.wait_ge(c_copied, 4 * (d + 1))
            engine.wait_ge(b_table_ready[1], 2)
            source = (rising, falling)[d]
            complex_product(step, engine, [outof[d][r][:, qs] for r in range(2)],
                            [power(source, d, 0, POWERS, r, qs) for r in range(2)],
                            [per_group(c_t[:, d, r], POWERS, qs) for r in range(2)], table_temp[:, qs], conjugate=True)
            engine.sem_inc(outof_ready[d], 1)

    @block.gpsimd
    def _(pool):
        step = Steps(pool, pool_step)
        step(pool.memset(ident[:], 0.0))
        step(pool.affine_select(out=ident[:], in_=ident[:], compare_op=ALU.not_equal, fill=1.0,
                                base=0, pattern=[[-1, P]], channel_multiplier=1))
        pool.sem_inc(ident_ready, 1)
        step(pool.memset(b_pair[:], 0.0))
        pool.sem_inc(b_pair_ready, 1)
        tables(pool, step, slice(B_ON_DVE, QS), slice(OUTOF_ON_DVE, QS))
        pool.wait_ge(d_loaded, 32)
        step(pool.tensor_tensor(d_mask[:], ident[0:2 * SSM_CH, 0:SSM_CH], ident[0:2 * SSM_CH, SSM_CH:2 * SSM_CH],
                                ALU.add))
        step(pool.tensor_tensor(d_diag[:], d_rows[:], d_mask[:].rearrange("p (a c) -> p a c", a=1)
                                .broadcast_to([2 * SSM_CH, QS, SSM_CH]), ALU.mult))
        pool.sem_inc(ident_ready, 1)

    @block.vector
    def _(dve):
        step = Steps(dve, dve_step)
        tables(dve, step, slice(0, B_ON_DVE), slice(0, OUTOF_ON_DVE))
        copied = Steps(dve, kernels_copied)
        for d in range(2):
            for b in range(QS // PER_BANK):
                dve.wait_ge(kernels_done, d * (QS // PER_BANK) + b + 1)
                mine = kernels[:, b * PER_BANK:(b + 1) * PER_BANK]
                found = banks[0:2 * SSM_CH, b % 4, :].rearrange("c (q k o) -> c q k o", q=PER_BANK, o=SSM_CH)
                if d == 0:
                    copied(dve.tensor_copy(mine[:, :, SSM_L - 1:SPAN], found))
                else:
                    step(dve.tensor_tensor(mine[:, :, SSM_L - 1], mine[:, :, SSM_L - 1],
                                           found[:, :, SSM_L - 1], ALU.add))
                    copied(dve.tensor_copy(mine[:, :, 0:SSM_L - 1], found[:, :, 0:SSM_L - 1]))
        dve.wait_ge(ident_ready, 2)
        step(dve.tensor_tensor(kernels[:, :, SSM_L - 1], kernels[:, :, SSM_L - 1], d_diag[:], ALU.add))
        dve.sem_inc(kernels_ready, 1)

    @block.tensor
    def _(pe):
        pe.wait_ge(ident_ready, 1)
        pe.wait_ge(c_loaded, 16 * 8)
        for d in range(2):
            for r in range(2):
                for w in range(4):
                    turn = pe.transpose(banks[:, d * 2 + r, w * P:(w + 1) * P], c_rows[:, d, r, w], ident[:])
                turn.then_inc(c_turned, 1)
        for d in range(2):
            pe.wait_ge(b_table_ready[d], 2)
            for r in range(2):
                for b in range(4):
                    n = (d * 2 + r) * 4 + b
                    if n >= 4:
                        pe.wait_ge(into_copied, n - 3)
                    for a in range(4):
                        turn = pe.transpose(banks[:, 4 + b, a * P:(a + 1) * P],
                                            b_table[d][r][:, b * 4 + a].rearrange("p l c -> p (l c)"), ident[:])
                    turn.then_inc(into_turned, 1)
        pe.wait_ge(c_copied, 8)
        pe.wait_ge(b_pair_ready, 9)
        for d in range(2):
            pe.wait_ge(outof_ready[d], 2)
            k0 = 0 if d == 0 else 1
            for b in range(QS // PER_BANK):
                n = d * (QS // PER_BANK) + b
                if n >= 4:
                    pe.wait_ge(kernels_copied, n - 3)
                for j in range(PER_BANK):
                    q = b * PER_BANK + j
                    for r in range(2):
                        done = pe.matmul(banks[0:2 * SSM_CH, b % 4, j * LC:(j + 1) * LC],
                                         b_pair[:, d, r, q].rearrange("p e c -> p (e c)"),
                                         outof[d][r][:, q, k0:k0 + SSM_L].rearrange("p k c -> p (k c)"),
                                         start=r == 0, stop=r == 1)
                done.then_inc(kernels_done, 1)


def attention_and_scan(nc, m, region, region2, qkv, sink, attn_scratch, scans):
    KEYS = 3 * P
    group = N_HEADS // N_KV
    ident = m.sb("ident", [P, P])
    views = carve(region, {"bias": (P, (N_HEADS, KEYS)), "q": (HEAD, (2, N_HEADS, P)), "k": (HEAD, (2, N_KV, KEYS)),
                           "neg_scores": (P, (2, KEYS)), "probs": (P, (2, KEYS))})
    bias = views["bias"]
    q, k, neg_scores, probs = views["q"], views["k"], views["neg_scores"], views["probs"]
    views = carve(region2, {
        "distance": (P, (KEYS,)), "distance_f": (P, (KEYS,)), "v_rows": (P, (2, KEYS)), "v": (P, (2, 3, KV)),
        "probs_t": (P, (2, KEYS)), "attn": (P, (N_HEADS, HEAD)), "attn_t": (P, (2, ATTN))})
    distance, distance_f = views["distance"].bitcast(I32), views["distance_f"]
    v_rows, v, probs_t, attn, attn_t = (views[n] for n in ("v_rows", "v", "probs_t", "attn", "attn_t"))
    sinks = m.sb("sinks", [P, N_HEADS])
    neg_sinks = m.sb("neg_sinks", [P, N_HEADS])
    neg_top = m.sb("neg_top", [P, 2, N_HEADS])
    sums = m.sb("sums", [P, 2, N_HEADS])
    sink_gap = m.sb("sink_gap", [P, N_HEADS])
    sink_exp = m.sb("sink_exp", [P, N_HEADS])
    total = m.sb("total", [P, N_HEADS])
    share = m.sb("share", [P, N_HEADS])
    s_psum = m.psum("s_psum", [P, 2, BANK])
    p_psum = m.psum("p_psum", [P, 2, BANK])
    o_psum = m.psum("o_psum", [P, 2, BANK])
    v_psum = m.psum("v_psum", [P, BANK])
    a_psum = m.psum("a_psum", [P, BANK])
    warmed = m.sem("warmed")
    sinks_in = m.sem("sinks_in")
    ident_ready = m.sem("ident_ready")
    iota_ready = m.sem("iota_ready")
    bias_step = m.sem("bias_step")
    distance_masked = m.sem("distance_masked")
    q_in = [m.sem("q_in0"), m.sem("q_in1")]
    k_in = [m.sem("k_in0"), m.sem("k_in1")]
    v_in = [m.sem("v_in0"), m.sem("v_in1")]
    loaded_free = m.sem("loaded_free")
    scores_done = m.sem("scores_done")
    mask_started = m.sem("mask_started")
    masked = m.sem("masked")
    exp_done = m.sem("exp_done")
    turned = m.sem("turned")
    probs_t_ready = m.sem("probs_t_ready")
    pv_done = m.sem("pv_done")
    v_turned = m.sem("v_turned")
    v_ready = m.sem("v_ready")
    gap_ready = m.sem("gap_ready")
    sink_ready = m.sem("sink_ready")
    share_step = m.sem("share_step")
    attn_ready = m.sem("attn_ready")
    attn_turned = m.sem("attn_turned")
    out_ready = m.sem("out_ready")
    stored = [m.sem("stored0"), m.sem("stored1")]
    for scan in scans:
        scan.add_semaphores(m)
    q_rows = qkv[0:ATTN, :].rearrange("(h d) t -> d h t", d=HEAD)
    k_rows = qkv[ATTN:ATTN + KV, :].rearrange("(h d) t -> d h t", d=HEAD)
    v_src = qkv[ATTN + KV:ATTN + 2 * KV, :]
    out_rows = attn_scratch.rearrange("(b p) t -> p b t", p=P)

    def keys_of(kind):
        lo, hi = {"first": (1, 3), "middle": (0, 3), "last": (0, 2)}[kind]
        return lo, hi, slice(lo * P, hi * P)

    def over_blocks(engine, body):
        body(0, 0, "first", "middle")
        body(0, 1, "middle", "middle")
        with engine.Fori(1, TILES // 2 - 1) as i:
            for s in range(2):
                body(i, s, "middle", "middle")
        body(TILES // 2 - 1, 0, "middle", "last")
        body(TILES // 2 - 1, 1, "last", None)

    block = m.ctx.enter_context(nc.Block())

    @block.sync
    def _(sync):
        sync.dma_start(sinks[:], row_broadcast(sink)).then_inc(sinks_in, 16)

        def load(i, s, kind, following):
            lo, hi, part = keys_of(kind)
            b = i * 2 + s
            sync.wait_ge(loaded_free, b + 1)
            sync.dma_start(q[:, s], q_rows[:, :, bass.ds(b * P, P)]).then_inc(q_in[s], 16)
            keys = bass.ds(b * P + (lo - 1) * P, (hi - lo) * P)
            sync.dma_start(k[:, s, :, part], k_rows[:, :, keys]).then_inc(k_in[s], 16)
            sync.dma_start(v_rows[:, s, part], v_src[:, keys]).then_inc(v_in[s], 16)

        over_blocks(sync, load)

    @block.gpsimd
    def _(pool):
        pool.memset(ident[:], 0.0).then_inc(ident_ready, 1)
        pool.iota(distance[:], pattern=[[-1, KEYS]], base=P, channel_multiplier=1).then_inc(iota_ready, 1)
        pool.wait_ge(ident_ready, 1)
        pool.affine_select(out=ident[:], in_=ident[:], compare_op=ALU.not_equal, fill=1.0,
                           base=0, pattern=[[-1, P]], channel_multiplier=1).then_inc(ident_ready, 1)
        pool.wait_ge(bias_step, 2)
        for n, (base, slope) in enumerate(((WINDOW + P, -1), (WINDOW - P, 1))):
            if n:
                pool.wait_ge(distance_masked, n)
            pool.affine_select(out=distance_f[:], in_=distance_f[:], compare_op=ALU.is_ge,
                               fill=-NEG_INF * 2.0 ** 8, base=base, pattern=[[slope, KEYS]],
                               channel_multiplier=-slope).then_inc(distance_masked, 1)
        scans[1].run(pool)

    @block.tensor
    def _(pe):
        def turn_values(i, s, kind):
            lo, hi, _ = keys_of(kind)
            pe.wait_ge(v_in[s], i * 16 + 16)
            pe.wait_ge(v_ready, i * 2 + s + 1)
            for j in range(lo, hi):
                turn = pe.transpose(v_psum[:, j * P:(j + 1) * P], v_rows[:, s, j * P:(j + 1) * P], ident[:])
            turn.then_inc(v_turned, 1)

        def score(i, s, kind, h):
            part = keys_of(kind)[2]
            if h == 0:
                pe.wait_ge(q_in[s], i * 16 + 16)
                pe.wait_ge(k_in[s], i * 16 + 16)
            pe.wait_ge(masked, i * (2 * N_HEADS) + (s * N_HEADS + h + 1))
            pe.matmul(s_psum[:, h % 2, part], q[:, s, h, :], k[:, s, h // group, part],
                      start=True, stop=True).then_inc(scores_done, 1)

        def turn_probs(i, s, kind, h):
            lo, hi, _ = keys_of(kind)
            n = i * (2 * N_HEADS) + (s * N_HEADS + h)
            pe.wait_ge(exp_done, n + 3)
            pe.wait_ge(probs_t_ready, n + 1)
            for j in range(lo, hi):
                turn = pe.transpose(p_psum[:, h % 2, j * P:(j + 1) * P], probs[:, h % 2, j * P:(j + 1) * P],
                                    ident[:])
            turn.then_inc(turned, 1)

        def weigh(i, s, kind, h):
            lo, hi, _ = keys_of(kind)
            pe.wait_ge(probs_t_ready, i * (2 * N_HEADS) + (s * N_HEADS + h + 3))
            if h == 0:
                pe.wait_ge(v_ready, i * 2 + s + 2)
                pe.wait_ge(attn_ready, i * 2 + s + 1)
            g = h // group
            for j in range(lo, hi):
                pv = pe.matmul(o_psum[:, s, h * HEAD:(h + 1) * HEAD], probs_t[:, h % 2, j * P:(j + 1) * P],
                               v[:, s, j, g * HEAD:(g + 1) * HEAD], start=j == lo, stop=j == hi - 1)
            pv.then_inc(pv_done, 1)

        def turn_attn(i, s):
            b = i * 2 + s
            pe.wait_ge(attn_ready, b + 3)
            if not isinstance(b, int) or b:
                pe.wait_ge(out_ready, b)
            for j in range(ATTN // P):
                turn = pe.transpose(a_psum[:, j * P:(j + 1) * P],
                                    attn[:, 2 * j:2 * j + 2, :].rearrange("p h d -> p (h d)"), ident[:])
            turn.then_inc(attn_turned, 1)

        def attend(i, s, kind, following):
            later, before = (i + s, 1 - s), (i + (s - 1), 1 - s)
            for h in range(N_HEADS):
                if h + 2 < N_HEADS:
                    score(i, s, kind, h + 2)
                elif following:
                    score(*later, following, h + 2 - N_HEADS)
                turn_probs(i, s, kind, h)
                if h:
                    weigh(i, s, kind, h - 1)
                elif kind != "first":
                    weigh(*before, "first" if isinstance(i, int) and i * 2 + s == 1 else "middle", N_HEADS - 1)
                if h == 4 and kind != "first":
                    turn_attn(*before)
                if h == N_HEADS - 2:
                    pe.wait_ge(scores_done, (i * 2 + s) * N_HEADS + N_HEADS)
                    pe.wait_ge(v_turned, i * 2 + s + 1)
                    pe.sem_inc(loaded_free, 1)
                    if following:
                        turn_values(*later, following)

        pe.sem_inc(loaded_free, 2)
        pe.sem_inc(turned, 2)
        pe.sem_inc(pv_done, 2)
        pe.wait_ge(ident_ready, 2)
        for n in range(WARM_UP):
            warm = pe.transpose(a_psum[:, 0:P], ident[:], ident[:])
        warm.then_inc(warmed, 1)
        pe.wait_ge(warmed, 1)
        turn_values(0, 0, "first")
        score(0, 0, "first", 0)
        score(0, 0, "first", 1)
        over_blocks(pe, attend)
        weigh(TILES // 2 - 1, 1, "last", N_HEADS - 1)
        turn_attn(TILES // 2 - 1, 1)

    @block.vector
    def _(dve):
        def mask(i, s, kind, h):
            part = keys_of(kind)[2]
            n = i * (2 * N_HEADS) + (s * N_HEADS + h)
            dve.wait_ge(exp_done, n + 1)
            dve.wait_ge(scores_done, n + 1)
            dve.sem_inc(mask_started, 1)
            dve.tensor_tensor_reduce(neg_scores[:, h % 2, part], s_psum[:, h % 2, part], bias[:, h, part],
                                     -HEAD ** -0.5, neg_sinks[:, h:h + 1], ALU.add, ALU.min,
                                     neg_top[:, s, h:h + 1]).then_inc(masked, 1)

        scan = scans[0]

        def scan_parts(i, s, h, phase):
            b = i * 2 + s
            if phase == "within":
                n = b * 2 + (h // 4 - 1)
                if not isinstance(n, int) or n >= 0:
                    scan.part(dve, scan.within(n), h % 4)
            elif phase == "of last":
                n = (b - TILES // 2) * N_HEADS + h
                if n < SCAN_J - 1:
                    for part in range(4):
                        scan.part(dve, scan.of_last(n), part)
            elif phase == "into next":
                for part in range(h * 3 // 2, (h + 1) * 3 // 2):
                    n = (b - (TILES // 2 + 2)) * 3 + part // 4
                    scan.part(dve, scan.into_next(n), part % 4)

        def copy_values(i, s, kind):
            lo, hi, part = keys_of(kind)
            dve.wait_ge(v_turned, i * 2 + s + 1)
            dve.tensor_copy(v[:, s, lo:hi].rearrange("p a b -> p (a b)"), v_psum[:, part]).then_inc(v_ready, 1)

        def open_norm(i, s):
            dve.wait_ge(masked, (i * 2 + s) * N_HEADS + (N_HEADS + 2))
            dve.tensor_tensor(sink_gap[:], sinks[:], neg_top[:, s], ALU.add).then_inc(gap_ready, 1)

        def norm(i, s):
            b = i * 2 + s
            dve.wait_ge(sink_ready, b + 1)
            dve.tensor_tensor(total[:], sums[:, s], sink_exp[:], ALU.add).then_inc(share_step, 1)
            dve.wait_ge(share_step, b * 2 + 1)
            dve.reciprocal(share[:], total[:]).then_inc(share_step, 1)
            dve.wait_ge(share_step, b * 2 + 2)
            dve.wait_ge(pv_done, b * N_HEADS + (N_HEADS + 2))
            if not isinstance(b, int) or b:
                dve.wait_ge(attn_turned, b)
            dve.tensor_tensor(attn[:], o_psum[:, s].rearrange("p (h d) -> p h d", d=HEAD),
                              share[:].rearrange("p (h a) -> p h a", a=1).broadcast_to([P, N_HEADS, HEAD]),
                              ALU.mult).then_inc(attn_ready, 1)

        def attend(i, s, kind, following, phase):
            later, before = (i + s, 1 - s), (i + (s - 1), 1 - s)
            for h in range(N_HEADS):
                if h + 1 < N_HEADS:
                    mask(i, s, kind, h + 1)
                elif following:
                    mask(*later, following, 0)
                scan_parts(i, s, h, phase)
                if kind != "first":
                    if h == 0:
                        open_norm(*before)
                    if h == 2:
                        norm(*before)
                if h == N_HEADS - 1 and following:
                    copy_values(*later, following)

        dve.wait_ge(iota_ready, 1)
        dve.tensor_copy(distance_f[:], distance[:]).then_inc(bias_step, 1)
        dve.wait_ge(bias_step, 1)
        dve.scalar_tensor_tensor(out=distance_f[:], in0=distance_f[:], scalar=-1.0, in1=distance_f[:],
                                 op0=ALU.mult, op1=ALU.max).then_inc(bias_step, 1)
        dve.wait_ge(distance_masked, 2)
        for h in range(N_HEADS):
            slope = 2.0 ** (-8.0 * (h + 1) / N_HEADS)
            dve.tensor_scalar(bias[:, h, :], distance_f[:], -slope * HEAD ** 0.5, None, ALU.mult)\
                .then_inc(bias_step, 1)
        dve.wait_ge(sinks_in, 16)
        dve.tensor_scalar(neg_sinks[:], sinks[:], -1.0, None, ALU.mult).then_inc(bias_step, 1)
        dve.wait_ge(bias_step, 3 + N_HEADS)
        dve.sem_inc(masked, 2)
        dve.sem_inc(scans[0].done, 1)
        dve.sem_inc(v_ready, 1)
        dve.sem_inc(attn_ready, 2)
        copy_values(0, 0, "first")
        mask(0, 0, "first", 0)
        attend(0, 0, "first", "middle", "within")
        attend(0, 1, "middle", "middle", "within")
        with dve.Fori(1, TILES // 4) as i:
            for s in range(2):
                attend(i, s, "middle", "middle", "within")
        for s in range(2):
            attend(TILES // 4, s, "middle", "middle", "of last")
        with dve.Fori(TILES // 4 + 1, TILES // 2 - 1) as i:
            for s in range(2):
                attend(i, s, "middle", "middle", "into next")
        attend(TILES // 2 - 1, 0, "middle", "last", "into next")
        attend(TILES // 2 - 1, 1, "last", None, None)
        open_norm(TILES // 2 - 1, 1)
        norm(TILES // 2 - 1, 1)

    @block.scalar
    def _(act):
        def exponentials(i, s, kind, h):
            part = keys_of(kind)[2]
            n = i * (2 * N_HEADS) + (s * N_HEADS + h)
            act.wait_ge(masked, n + 3)
            act.wait_ge(turned, n + 1)
            act.activation(probs[:, h % 2, part], neg_scores[:, h % 2, part], ACT.Exp, scale=-1.0,
                           bias=neg_top[:, s, h:h + 1], accum_out=sums[:, s, h:h + 1]).then_inc(exp_done, 1)

        def copy_turned(i, s, kind, h):
            part = keys_of(kind)[2]
            n = i * (2 * N_HEADS) + (s * N_HEADS + h)
            act.wait_ge(turned, n + 3)
            act.wait_ge(pv_done, n + 1)
            act.activation(probs_t[:, h % 2, part], p_psum[:, h % 2, part], ACT.Copy).then_inc(probs_t_ready, 1)

        def sink_part(i, s):
            act.wait_ge(gap_ready, i * 2 + s + 1)
            act.activation(sink_exp[:], sink_gap[:], ACT.Exp).then_inc(sink_ready, 1)

        def copy_out(i, s):
            b = i * 2 + s
            act.wait_ge(attn_turned, b + 1)
            act.wait_ge(stored[s], i * 16 + 16)
            act.activation(attn_t[:, s], a_psum[:], ACT.Copy).then_inc(out_ready, 1)
            act.wait_ge(out_ready, b + 1)
            act.dma_start(out_rows[:, :, bass.ds(b * P, P)], attn_t[:, s].rearrange("p (a t) -> p a t", t=P))\
                .then_inc(stored[s], 16)

        def attend(i, s, kind, following):
            later, before = (i + s, 1 - s), (i + (s - 1), 1 - s)
            for h in range(N_HEADS):
                if h + 1 < N_HEADS:
                    exponentials(i, s, kind, h + 1)
                elif following:
                    exponentials(*later, following, 0)
                copy_turned(i, s, kind, h)
                if kind != "first":
                    if h == 1:
                        sink_part(*before)
                    if h == 5:
                        copy_out(*before)

        act.sem_inc(exp_done, 2)
        act.sem_inc(probs_t_ready, 2)
        for s in range(2):
            act.sem_inc(stored[s], 16)
        exponentials(0, 0, "first", 0)
        over_blocks(act, attend)
        sink_part(TILES // 2 - 1, 1)
        copy_out(TILES // 2 - 1, 1)
        for s in range(2):
            act.wait_ge(stored[s], (TILES // 2 + 1) * 16)

    used = sum(math.prod(view.shape[1:]) for view in views.values())
    return -(-used // (2 * SSM_J)) * 2


class ChunkScan:
    PER_STEP = 5

    def __init__(self, m, d, states, leaps, on_pool):
        self.d, self.on_pool, self.leaps = d, on_pool, leaps
        self.grid = states[:, :, :, 1 - d:1 - d + SSM_J].rearrange("p r q (j i) -> p r q j i", i=SCAN_I)
        self.end = SCAN_I - 1 if d == 0 else 0
        self.by_re = m.sb(f"by_re{d}", [P, 2, QS, SCAN_J])
        self.by_im = m.sb(f"by_im{d}", [P, 2, QS, SCAN_J])

    def add_semaphores(self, m):
        self.done = m.sem(f"scan_done{self.d}")
        self.start = m.sem(f"scan_start{self.d}")

    def within(self, i):
        now, last = (i + 1, i) if self.d == 0 else (SCAN_I - 2 - i, SCAN_I - 1 - i)
        target, source = (self.grid[:, :, :, :, bass.ds(n, 1)].rearrange("p r q j i -> p r q (j i)")
                          for n in (now, last))
        return target, source, slice(0, 1), SCAN_J, i * self.PER_STEP + 1

    def of_last(self, i):
        now, last = (i + 1, i) if self.d == 0 else (SCAN_J - 2 - i, SCAN_J - 1 - i)
        target, source = (self.grid[:, :, :, bass.ds(n, 1), self.end] for n in (now, last))
        return target, source, slice(SCAN_I - 1, SCAN_I), 1, i * self.PER_STEP + (self.PER_STEP * (SCAN_I - 1) + 1)

    def into_next(self, i):
        targets, sources = slice(1, SCAN_J), slice(0, SCAN_J - 1)
        now = i
        if self.d == 1:
            targets, sources = sources, targets
            now = SCAN_I - 1 - i
        target = self.grid[:, :, :, targets, bass.ds(now, 1)].rearrange("p r q j i -> p r q (j i)")
        return (target, self.grid[:, :, :, sources, self.end], bass.ds(i, 1), SCAN_J - 1,
                i * self.PER_STEP + (self.PER_STEP * (SCAN_I + SCAN_J - 2) + 1))

    def part(self, engine, step, n):
        target, source, power, blocks, before = step
        by_re, by_im = self.by_re[:, :, :, 0:blocks], self.by_im[:, :, :, 0:blocks]
        done = self.done
        engine.wait_ge(done, before + n)
        if self.on_pool:
            engine.sem_inc(self.start, 1)
        if n < 2:
            factor = self.leaps[:, n, power, :].rearrange("p k (q b) -> p k q b", b=1)\
                .broadcast_to([P, 2, QS, blocks])
            engine.tensor_tensor((by_re, by_im)[n], source, factor, ALU.mult).then_inc(done, 1)
        elif n == 2:
            engine.tensor_tensor(target, target, by_re, ALU.add).then_inc(done, 1)
        else:
            engine.tensor_tensor(target[:, 0:1], target[:, 0:1], by_im[:, 1:2], ALU.subtract).then_inc(done, 1)
            engine.tensor_tensor(target[:, 1:2], target[:, 1:2], by_im[:, 0:1], ALU.add).then_inc(done, 1)

    def over_blocks(self, engine):
        with engine.Fori(0, SCAN_J - 1) as i:
            for n in range(4):
                self.part(engine, self.of_last(i), n)

    def run(self, engine):
        engine.sem_inc(self.done, 1)
        with engine.Fori(0, SCAN_I - 1) as i:
            for n in range(4):
                self.part(engine, self.within(i), n)
        self.over_blocks(engine)
        with engine.Fori(0, SCAN_I - 1) as i:
            for n in range(4):
                self.part(engine, self.into_next(i), n)


def load_chunks(engine, u, u_scratch, u_in, side, parts):
    u_chunks = u_scratch.rearrange("(g c) (l j) -> l c g j", c=SSM_CH, l=SSM_L)
    for part, groups in enumerate(parts):
        for l in range(side, SSM_L, 2):
            engine.dma_start(u[l * SSM_CH:(l + 1) * SSM_CH, groups], u_chunks[l, :, groups]).then_inc(u_in[part], 16)


def chunks_into_states(nc, m, u, into, states):
    banks = m.psum("banks", [P, 8, BANK])
    edge_zero = m.sem("edge_zero")
    into_done = m.sem("into_done")
    into_copied = [m.sem("into_copied0"), m.sem("into_copied1")]
    block = m.ctx.enter_context(nc.Block())

    @block.tensor
    def _(pe):
        for g in range(GROUPS):
            for d in range(2):
                if g >= 4:
                    pe.wait_ge(into_copied[d], 2 * (g - 3))
                done = pe.matmul(banks[:, g % 4 * 2 + d, 0:SSM_J],
                                 into[:, d, g // 2, g % 2].rearrange("p r n -> p (r n)"), u[:, g, :],
                                 start=True, stop=True)
            done.then_inc(into_done, 1)

    def lay_out(copy, g, d):
        q, e = g // 2, g % 2
        for r in range(2):
            copy(states[d][e * SSM_N:(e + 1) * SSM_N, r, q, 1 - d:1 - d + SSM_J],
                 banks[r * SSM_N:(r + 1) * SSM_N, g % 4 * 2 + d, 0:SSM_J]).then_inc(into_copied[d], 1)

    @block.scalar
    def _(act):
        for g in range(GROUPS):
            act.wait_ge(into_done, g + 1)
            lay_out(lambda out, part: act.activation(out, part, ACT.Copy), g, 0)

    @block.vector
    def _(dve):
        dve.memset(states[0][:, :, :, 0:1], 0.0).then_inc(edge_zero, 1)
        dve.memset(states[1][:, :, :, SSM_J:SSM_J + 1], 0.0).then_inc(edge_zero, 1)
        for g in range(GROUPS):
            dve.wait_ge(into_done, g + 1)
            lay_out(dve.tensor_copy, g, 1)


def states_to_outputs(nc, m, region, u, lost, u_scratch, y_scratch, outof, local, states):
    y = carve(region, {"y": (P, (2, 4, SSM_J))})["y"]
    banks = m.psum("banks", [P, 8, BANK])
    u_in = [m.sem("u_in0"), m.sem("u_in1")]
    y_done = m.sem("y_done")
    y_ready = m.sem("y_ready")
    store_started = m.sem("store_started")
    stored = [m.sem("stored0"), m.sem("stored1")]
    y_chunks = y_scratch.rearrange("(g c) (l j) -> l c g j", c=SSM_CH, l=SSM_L)
    middle = lost // 4 * 2
    lost_groups = [slice(middle, lost), slice(0, middle)]
    pairs = list(reversed(range(QS)))
    block = m.ctx.enter_context(nc.Block())

    @block.sync
    def _(sync):
        load_chunks(sync, u, u_scratch, u_in, 0, lost_groups)
        with sync.Fori(0, QS // 4) as i:
            for s in range(2):
                sync.wait_ge(y_ready, i * 4 + s * 2 + 2)
                sync.sem_inc(store_started, 1)
                for l in range(SSM_L):
                    sync.dma_start(y_chunks[l, :, bass.ds((QS // 2 - 1 - s - i * 2) * 4, 4), :],
                                   y[l * SSM_CH:(l + 1) * SSM_CH, s]).then_inc(stored[s], 16)
        for s in range(2):
            sync.wait_ge(stored[s], QS // 4 * SSM_L * 16)

    @block.tensor
    def _(pe):
        def own_tokens(n):
            q = pairs[n]
            for e in range(2):
                if 2 * q + e < lost:
                    pe.wait_ge(u_in[0 if 2 * q + e >= middle else 1], 16 * SSM_L)
                pe.matmul(banks[:, n % 4 * 2 + e, 0:SSM_J], local[:, 2 * q + e, :], u[:, 2 * q + e, :],
                          start=True, stop=False)

        for n in range(4):
            own_tokens(n)
        for n, q in enumerate(pairs):
            for e in range(2):
                half = slice(e * SSM_N, (e + 1) * SSM_N)
                bank = banks[:, n % 4 * 2 + e, 0:SSM_J]
                for d in range(2):
                    for r in range(2):
                        done = pe.matmul(bank, outof[d][r][half, q, 1 - d:1 - d + SSM_L].rearrange("p k c -> p (k c)"),
                                         states[d][half, r, q, d:d + SSM_J],
                                         start=False, stop=d == 1 and r == 1)
            done.then_inc(y_done, 1)
            if 1 <= n < QS - 3:
                pe.wait_ge(y_ready, n)
                own_tokens(n + 3)

    @block.scalar
    def _(act):
        load_chunks(act, u, u_scratch, u_in, 1, lost_groups)
        for n, q in enumerate(pairs):
            act.wait_ge(y_done, n + 1)
            if n >= 4 and n % 2 == 0:
                act.wait_ge(stored[n // 2 % 2], n // 4 * SSM_L * 16)
            act.activation(y[:, n // 2 % 2, q % 2 * 2:q % 2 * 2 + 2], banks[:, n % 4 * 2:n % 4 * 2 + 2, 0:SSM_J],
                           ACT.Gelu_apprx_tanh).then_inc(y_ready, 1)


LAM_NAMES = ("lam_re", "lam_im", "log_dt", "b_re", "b_im", "c_re", "c_im")


def hybrid_layer(nc, t):
    def scratch(name, shape):
        return nc.dram_tensor(name, shape, F32, kind="Internal").ap()

    qkv = scratch("qkv", (ATTN + 2 * KV, TOK))
    u = scratch("u", (SSM, TOK))
    gates = scratch("gates", (2 * D, TOK))
    attn = scratch("attn", (ATTN, TOK))
    y = scratch("y_ssm", (SSM, TOK))
    merged = scratch("merged", (D, TOK))
    x_mid = scratch("x_mid", (TOK, D))
    f = scratch("f", (FF, TOK))
    params = [[t[f"{name}_{direction}"] for name in LAM_NAMES] for direction in "fb"]

    with nc.sbuf_tensor("bases", [P, RING * D], F32) as memory:
        bases = SsmBases(params, memory)
        stage_project_in(nc, t["x"], t["norm_mix_pre"], t["w_in"], qkv, u, gates, bases)
        stage_mixers(nc, qkv, t["attn_sink"], attn, u, bases, t["ssm_d"], y)
    stage_branches(nc, attn, y, gates, t["w_glu"], t["b_glu"], t["w_branch_attn"], t["w_branch_ssm"], merged)
    stage_out(nc, merged, t["w_out"], t["norm_mix_post"], t["x"], x_mid)
    stage_gate_up(nc, x_mid, t["norm_ffn_pre"], t["w_ffn_gate"], t["w_ffn_up"], t["conv_w"], t["conv_b"], f)
    stage_down(nc, f, t["w_ffn_down"], t["norm_ffn_post"], x_mid, t["out"])


def kernel(**inputs):
    import numpy as np
    from concourse import bacc
    from concourse.bass_utils import run_bass_kernel_spmd

    nc = bacc.Bacc("TRN2", target_bir_lowering=False, num_devices=1)
    arrays, tensors = {}, {}
    for name, value in inputs.items():
        array = np.ascontiguousarray(value)
        arrays[f"in_{name}"] = array
        handle = nc.dram_tensor(f"in_{name}", array.shape, mybir.dt.from_np(array.dtype), kind="ExternalInput").ap()
        tensors[name] = handle[0]
    out = nc.dram_tensor("out", (1, TOK, D), F32, kind="ExternalOutput").ap()
    tensors["out"] = out[0]
    hybrid_layer(nc, tensors)
    result = run_bass_kernel_spmd(nc, [arrays], core_ids=[0])
    return result.results[0]["out"]
```
